# Optimizing a Trainium2 kernel written in Bass

```python
import math
import jax, jax.numpy as jnp
from jax import lax
import numpy as np

D_MODEL = 1024
BATCH = 1
SEQ = 256
DEPTH = 1

N_META = 16
ATTN_HEADS = 4
ATTN_HEAD_DIM = 64
ATTN_VALUE_DIM = 2 * ATTN_HEAD_DIM
ATTN_WIDTH = ATTN_HEADS * ATTN_VALUE_DIM
CONV_WIDTH = D_MODEL - ATTN_WIDTH
CONV_K = 3
MIX_WIDTH = ATTN_WIDTH + CONV_WIDTH
IN_PROJ_WIDTH = 3 * ATTN_WIDTH + 3 * CONV_WIDTH
N_EXPERTS = 16
EC_CAPACITY_FACTOR = 2
D_FF_EXPERT = 2 * D_MODEL
ROPE_THETA = 10000.0
Q_BLOCK = 128
NORM_EPS = 1e-6


def rms_norm(x, g):
    xf = x.astype(jnp.float32)
    y = xf * lax.rsqrt(jnp.mean(xf * xf, axis=-1, keepdims=True) + NORM_EPS)
    return (y * g.astype(jnp.float32)).astype(x.dtype)

def rope_tables(n):
    d = ATTN_HEAD_DIM
    inv_freq = ROPE_THETA ** (-jnp.arange(0, d, 2, dtype=jnp.float32) / d)
    ang = jnp.arange(n, dtype=jnp.float32)[:, None] * inv_freq[None, :]
    ang = jnp.concatenate([ang, ang], axis=-1)
    return jnp.cos(ang), jnp.sin(ang)

def apply_rope(x, cos, sin):
    half = x.shape[-1] // 2
    x1, x2 = x[..., :half], x[..., half:]
    rot = jnp.concatenate([-x2, x1], axis=-1)
    return (x * cos + rot * sin).astype(x.dtype)

def diff_attention_group(q, k, v, lq1, lk1, lq2, lk2, subln_g, lam_init, cos, sin):
    B, L, _ = q.shape
    Lp = cos.shape[0]
    H, d = ATTN_HEADS, ATTN_HEAD_DIM
    pad = Lp - L
    q = jnp.pad(q.reshape(B, L, H, 2, d), ((0, 0), (0, pad), (0, 0), (0, 0), (0, 0)))
    k = jnp.pad(k.reshape(B, L, H, 2, d), ((0, 0), (0, pad), (0, 0), (0, 0), (0, 0)))
    v = jnp.pad(v.reshape(B, L, H, 2 * d), ((0, 0), (0, pad), (0, 0), (0, 0)))
    q = apply_rope(q.transpose(0, 2, 3, 1, 4), cos, sin)
    k = apply_rope(k.transpose(0, 2, 3, 1, 4), cos, sin)
    v32 = v.transpose(0, 2, 1, 3).astype(jnp.float32)

    lam = (jnp.exp(jnp.sum(lq1.astype(jnp.float32) * lk1.astype(jnp.float32)))
           - jnp.exp(jnp.sum(lq2.astype(jnp.float32) * lk2.astype(jnp.float32)))
           + lam_init)
    key_valid = jnp.arange(Lp) < L
    scale = d ** -0.5
    n_blk = Lp // Q_BLOCK
    qb = jnp.moveaxis(q.reshape(B, H, 2, n_blk, Q_BLOCK, d), 3, 0)

    def one_block(qi):
        s = jnp.einsum('bhiqd,bhikd->bhiqk', qi, k,
                       preferred_element_type=jnp.float32) * scale
        s = jnp.where(key_valid, s, jnp.finfo(jnp.float32).min)
        p = jax.nn.softmax(s, axis=-1)
        a = p[:, :, 0] - lam * p[:, :, 1]
        return jnp.einsum('bhqk,bhkv->bhqv', a, v32)

    o = lax.map(one_block, qb)
    o = o.transpose(1, 0, 3, 2, 4).reshape(B, Lp, H, 2 * d)[:, :L]
    o = rms_norm(o, subln_g) * (1.0 - lam_init)
    return o.reshape(B, L, ATTN_WIDTH).astype(q.dtype)

def centred_depthwise_conv(u, w):
    L = u.shape[1]
    half = CONV_K // 2
    up = jnp.pad(u, ((0, 0), (half, half), (0, 0)))
    return sum(w[j] * up[:, j:j + L] for j in range(CONV_K))

def expert_choice_ffn(h, w_router, w_gate, w_up, w_down):
    B, L, D = h.shape
    cap = EC_CAPACITY_FACTOR * L // N_EXPERTS

    def one_group(hs):
        logits = jnp.einsum('ld,de->le', hs, w_router, preferred_element_type=jnp.float32)
        aff = jax.nn.softmax(logits, axis=-1)
        g, idx = lax.top_k(aff.T, cap)
        xg = hs[idx]
        a = jnp.einsum('ecd,edf->ecf', xg, w_gate)
        u = jnp.einsum('ecd,edf->ecf', xg, w_up)
        y = jnp.einsum('ecf,efd->ecd', jax.nn.silu(a) * u, w_down)
        y = y * g[..., None].astype(y.dtype)
        out = jnp.zeros((L, D), y.dtype).at[idx.reshape(-1)].add(y.reshape(-1, D))
        return out.astype(hs.dtype)

    return lax.map(one_group, h)

def first_inputs(seed: int = 0) -> dict:
    key = jax.random.key(seed)
    ks = jax.random.split(key, 20)
    f32 = jnp.float32
    nrm = lambda k, shape, s: jax.random.normal(k, shape, f32) * s
    gain = lambda k, shape: 1.0 + 0.02 * jax.random.normal(k, shape, f32)
    return {
        "x": nrm(ks[0], (BATCH, SEQ, D_MODEL), 1.0),
        "meta_tokens": nrm(ks[1], (N_META, D_MODEL), 1.0),
        "mix_norm_g": gain(ks[2], (DEPTH, D_MODEL)),
        "w_in": nrm(ks[3], (DEPTH, D_MODEL, IN_PROJ_WIDTH), D_MODEL ** -0.5),
        "conv_w": nrm(ks[4], (DEPTH, CONV_K, CONV_WIDTH), CONV_K ** -0.5),
        "lambda_q1": nrm(ks[5], (DEPTH, ATTN_HEAD_DIM), 0.1),
        "lambda_k1": nrm(ks[6], (DEPTH, ATTN_HEAD_DIM), 0.1),
        "lambda_q2": nrm(ks[7], (DEPTH, ATTN_HEAD_DIM), 0.1),
        "lambda_k2": nrm(ks[8], (DEPTH, ATTN_HEAD_DIM), 0.1),
        "attn_subln_g": gain(ks[9], (DEPTH, ATTN_VALUE_DIM)),
        "w_out": nrm(ks[10], (DEPTH, MIX_WIDTH, D_MODEL), MIX_WIDTH ** -0.5),
        "ffn_norm_g": gain(ks[11], (DEPTH, D_MODEL)),
        "w_router": nrm(ks[12], (DEPTH, D_MODEL, N_EXPERTS), D_MODEL ** -0.5),
        "w_gate": nrm(ks[13], (DEPTH, N_EXPERTS, D_MODEL, D_FF_EXPERT), D_MODEL ** -0.5),
        "w_up": nrm(ks[14], (DEPTH, N_EXPERTS, D_MODEL, D_FF_EXPERT), D_MODEL ** -0.5),
        "w_down": nrm(ks[15], (DEPTH, N_EXPERTS, D_FF_EXPERT, D_MODEL), D_FF_EXPERT ** -0.5),
        "final_norm_g": gain(ks[16], (D_MODEL,)),
    }

def first_block(x, meta_tokens, mix_norm_g, w_in, conv_w, lambda_q1, lambda_k1, lambda_q2,
              lambda_k2, attn_subln_g, w_out, ffn_norm_g, w_router, w_gate, w_up, w_down,
              final_norm_g):
    B = x.shape[0]
    meta = jnp.broadcast_to(meta_tokens.astype(x.dtype)[None], (B, N_META, D_MODEL))
    h = jnp.concatenate([meta, x], axis=1)
    L = h.shape[1]
    Lp = -(-L // Q_BLOCK) * Q_BLOCK
    cos, sin = rope_tables(Lp)
    splits = [ATTN_WIDTH, 2 * ATTN_WIDTH, 3 * ATTN_WIDTH,
              3 * ATTN_WIDTH + CONV_WIDTH, 3 * ATTN_WIDTH + 2 * CONV_WIDTH]

    for l in range(DEPTH):
        lam_init = 0.8 - 0.6 * math.exp(-0.3 * l)
        hn = rms_norm(h, mix_norm_g[l])
        proj = jnp.einsum('bld,dp->blp', hn, w_in[l])
        q, k, v, cx, cb, cc = jnp.split(proj, splits, axis=-1)
        attn = diff_attention_group(q, k, v, lambda_q1[l], lambda_k1[l], lambda_q2[l],
                                    lambda_k2[l], attn_subln_g[l], lam_init, cos, sin)
        conv = cb * centred_depthwise_conv(cc * cx, conv_w[l])
        mixed = jnp.concatenate([attn, conv.astype(attn.dtype)], axis=-1)
        h = h + jnp.einsum('blm,md->bld', mixed, w_out[l])
        h = h + expert_choice_ffn(rms_norm(h, ffn_norm_g[l]), w_router[l], w_gate[l],
                                  w_up[l], w_down[l])

    y = rms_norm(h, final_norm_g)
    return y[:, N_META:, :]


N_BRANCHES = 4
BRANCH_WIDTH = 512
D_FF = 4 * D_MODEL

DN_HEADS = 4
DN_HEAD_DIM = 128
DN_CONV = 4
DN_CHUNK = 64

MLA_HEADS = 4
MLA_Q_RANK = 256
MLA_KV_RANK = 128
MLA_NOPE = 128
MLA_ROPE = 64
MLA_V = 128
MLA_QK_DIM = MLA_NOPE + MLA_ROPE

SG_GROUPS = 4
SG_GROUP_DIM = 128
SG_CHUNK = 128

FOX_HEADS = 4
FOX_HEAD_DIM = 128

IN_SPLITS = (
    3 * DN_HEADS * DN_HEAD_DIM,
    DN_HEADS * DN_HEAD_DIM,
    DN_HEADS,
    DN_HEADS,
    MLA_Q_RANK,
    MLA_KV_RANK,
    MLA_ROPE,
    SG_GROUPS * SG_GROUP_DIM,
    SG_GROUPS * SG_GROUP_DIM,
    3 * FOX_HEADS * FOX_HEAD_DIM,
    FOX_HEADS,
    N_BRANCHES * D_MODEL,
)
D_IN = sum(IN_SPLITS)


def rms_norm_2(x, g, eps=NORM_EPS):
    xf = x.astype(jnp.float32)
    y = xf * lax.rsqrt(jnp.mean(xf * xf, axis=-1, keepdims=True) + eps)
    return (y * g.astype(jnp.float32)).astype(x.dtype)

def l2_norm(x, eps=NORM_EPS):
    return x * lax.rsqrt(jnp.sum(x * x, axis=-1, keepdims=True) + eps)

def causal_depthwise_conv(x, w):
    K = w.shape[0]
    S = x.shape[1]
    xp = jnp.pad(x, ((0, 0), (K - 1, 0), (0, 0)))
    out = xp[:, 0:S, :] * w[0]
    for k in range(1, K):
        out = out + xp[:, k:k + S, :] * w[k]
    return out

def rope_tables_2(positions):
    inv_freq = ROPE_THETA ** (-jnp.arange(0, MLA_ROPE, 2, dtype=jnp.float32) / MLA_ROPE)
    ang = positions.astype(jnp.float32)[..., None] * inv_freq
    return jnp.cos(ang)[:, :, None, :], jnp.sin(ang)[:, :, None, :]

def apply_rope_2(x, cos, sin):
    xf = x.astype(jnp.float32)
    x1, x2 = jnp.split(xf, 2, axis=-1)
    return jnp.concatenate([x1 * cos - x2 * sin, x2 * cos + x1 * sin], axis=-1).astype(x.dtype)

def block_causal_attention(q, k, v, log_decay=None):
    B, H, S, dk = q.shape
    nb = S // Q_BLOCK
    scale = dk ** -0.5
    k_pos = jnp.arange(S)

    def to_blocks(a):
        return jnp.moveaxis(a.reshape(B, H, nb, Q_BLOCK, *a.shape[3:]), 2, 0)

    xs = {"idx": jnp.arange(nb), "q": to_blocks(q)}
    if log_decay is not None:
        xs["d"] = to_blocks(log_decay)

    def attend(blk):
        q_pos = blk["idx"] * Q_BLOCK + jnp.arange(Q_BLOCK)
        s = jnp.einsum("bhqd,bhkd->bhqk", blk["q"], k).astype(jnp.float32) * scale
        if log_decay is not None:
            s = s + (blk["d"][..., :, None] - log_decay[..., None, :])
        s = jnp.where(k_pos[None, :] <= q_pos[:, None], s, -jnp.inf)
        p = jax.nn.softmax(s, axis=-1).astype(v.dtype)
        return jnp.einsum("bhqk,bhkd->bhqd", p, v)

    out = lax.map(attend, xs)
    return jnp.moveaxis(out, 0, 2).reshape(B, H, S, v.shape[-1])

def gated_deltanet(qkv, z, a_logit, b_logit, conv_w, a_log, dt_bias, out_g):
    B, S, _ = qkv.shape
    H, dk, C = DN_HEADS, DN_HEAD_DIM, DN_CHUNK
    N = S // C
    qkv = jax.nn.silu(causal_depthwise_conv(qkv, conv_w)).astype(jnp.float32)
    q, k, v = jnp.split(qkv, 3, axis=-1)

    def heads(t):
        return t.reshape(B, S, H, dk).transpose(0, 2, 1, 3)

    q = l2_norm(heads(q)) * dk ** -0.5
    k = l2_norm(heads(k))
    v = heads(v)
    beta = jax.nn.sigmoid(b_logit.astype(jnp.float32)).transpose(0, 2, 1)
    g = (-jnp.exp(a_log.astype(jnp.float32))
         * jax.nn.softplus(a_logit.astype(jnp.float32) + dt_bias.astype(jnp.float32))).transpose(0, 2, 1)

    def chunk(t):
        return t.reshape(B, H, N, C, *t.shape[3:])

    q, k, v, beta, g = chunk(q), chunk(k), chunk(v), chunk(beta), chunk(g)
    gc = jnp.cumsum(g, axis=-1)
    tril = jnp.tril(jnp.ones((C, C), dtype=bool))
    strict = jnp.tril(jnp.ones((C, C), dtype=bool), -1)
    diff = gc[..., :, None] - gc[..., None, :]
    decay = jnp.where(tril, jnp.exp(jnp.where(tril, diff, 0.0)), 0.0)

    kb = k * beta[..., None]
    lower = jnp.where(strict, jnp.einsum("bhnid,bhnjd->bhnij", kb, k) * decay, 0.0)
    rhs = jnp.concatenate([v * beta[..., None], kb * jnp.exp(gc)[..., None]], axis=-1)
    sol = lax.linalg.triangular_solve(lower + jnp.eye(C, dtype=jnp.float32), rhs,
                                      left_side=True, lower=True, unit_diagonal=True)
    u, w = jnp.split(sol, 2, axis=-1)

    a_qk = jnp.einsum("bhnid,bhnjd->bhnij", q, k) * decay
    q_dec = q * jnp.exp(gc)[..., None]
    k_dec = k * jnp.exp(gc[..., -1:] - gc)[..., None]
    g_last = jnp.exp(gc[..., -1])

    def step(state, xs):
        q_i, k_i, u_i, w_i, a_i, gl_i = xs
        v_new = u_i - jnp.einsum("bhcd,bhde->bhce", w_i, state)
        o_i = jnp.einsum("bhcd,bhde->bhce", q_i, state) + jnp.einsum("bhij,bhje->bhie", a_i, v_new)
        state = state * gl_i[..., None, None] + jnp.einsum("bhcd,bhce->bhde", k_i, v_new)
        return state, o_i

    xs = tuple(jnp.moveaxis(t, 2, 0) for t in (q_dec, k_dec, u, w, a_qk, g_last))
    _, o = lax.scan(step, jnp.zeros((B, H, dk, dk), jnp.float32), xs)
    o = jnp.moveaxis(o, 0, 2).reshape(B, H, S, dk)
    o = rms_norm_2(o, out_g).transpose(0, 2, 1, 3).reshape(B, S, H * dk)
    return (o * jax.nn.silu(z.astype(jnp.float32))).astype(z.dtype)

def latent_attention(c_q, c_kv, k_rope, positions, q_norm_g, kv_norm_g, w_uq, w_ukv, qk_q_g, qk_k_g):
    B, S, _ = c_q.shape
    H = MLA_HEADS
    q = (rms_norm_2(c_q, q_norm_g) @ w_uq).reshape(B, S, H, MLA_QK_DIM)
    kv = (rms_norm_2(c_kv, kv_norm_g) @ w_ukv).reshape(B, S, H, MLA_NOPE + MLA_V)
    k_nope, v = jnp.split(kv, [MLA_NOPE], axis=-1)
    k = jnp.concatenate([k_nope, jnp.broadcast_to(k_rope[:, :, None, :], (B, S, H, MLA_ROPE))], axis=-1)
    q = rms_norm_2(q, qk_q_g)
    k = rms_norm_2(k, qk_k_g)
    cos, sin = rope_tables_2(positions)
    q = jnp.concatenate([q[..., :MLA_NOPE], apply_rope_2(q[..., MLA_NOPE:], cos, sin)], axis=-1)
    k = jnp.concatenate([k[..., :MLA_NOPE], apply_rope_2(k[..., MLA_NOPE:], cos, sin)], axis=-1)
    o = block_causal_attention(q.transpose(0, 2, 1, 3), k.transpose(0, 2, 1, 3), v.transpose(0, 2, 1, 3))
    return o.transpose(0, 2, 1, 3).reshape(B, S, H * MLA_V)

def spatial_gating(u, v, norm_g, w_s, b_s):
    B, S, _ = u.shape
    G, Cg, T = SG_GROUPS, SG_GROUP_DIM, SG_CHUNK
    N = S // T
    u = jax.nn.gelu(u)
    v = rms_norm_2(jax.nn.gelu(v).reshape(B, S, G, Cg), norm_g).reshape(B, N, T, G, Cg)
    w_causal = jnp.where(jnp.tril(jnp.ones((T, T), dtype=bool)), w_s, 0.0)
    mixed = jnp.einsum("gts,bnsgc->bntgc", w_causal, v) + b_s.T[None, None, :, :, None]
    return u * mixed.reshape(B, S, G * Cg)

def forgetting_attention(qkv, f_logit, f_bias, q_g, k_g):
    B, S, _ = qkv.shape
    H, dh = FOX_HEADS, FOX_HEAD_DIM
    q, k, v = jnp.split(qkv, 3, axis=-1)

    def heads(t):
        return t.reshape(B, S, H, dh).transpose(0, 2, 1, 3)

    q = rms_norm_2(heads(q), q_g)
    k = rms_norm_2(heads(k), k_g)
    log_f = jax.nn.log_sigmoid(f_logit.astype(jnp.float32) + f_bias.astype(jnp.float32))
    cum = jnp.cumsum(log_f, axis=1).transpose(0, 2, 1)
    o = block_causal_attention(q, k, heads(v), cum)
    return o.transpose(0, 2, 1, 3).reshape(B, S, H * dh)

def second_inputs(seed: int = 0) -> dict:
    key = jax.random.key(seed)
    ks = jax.random.split(key, 26)
    L = DEPTH
    f32 = jnp.float32

    def nrm(k, shape, fan_in):
        return jax.random.normal(k, shape, f32) * fan_in ** -0.5

    def gain(k, shape):
        return 1.0 + 0.1 * jax.random.normal(k, shape, f32)

    dt = jnp.exp(jax.random.uniform(ks[4], (L, DN_HEADS), f32, math.log(1e-3), math.log(1e-1)))
    return {
        "x": jax.random.normal(ks[0], (BATCH, SEQ, D_MODEL), f32),
        "positions": jnp.broadcast_to(jnp.arange(SEQ, dtype=jnp.int32)[None, :], (BATCH, SEQ)),
        "norm1_g": gain(ks[1], (L, D_MODEL)),
        "w_in": nrm(ks[2], (L, D_MODEL, D_IN), D_MODEL),
        "dn_conv_w": nrm(ks[3], (L, DN_CONV, 3 * DN_HEADS * DN_HEAD_DIM), DN_CONV),
        "dn_a_log": jnp.log(jax.random.uniform(ks[5], (L, DN_HEADS), f32, 1.0, 16.0)),
        "dn_dt_bias": dt + jnp.log(-jnp.expm1(-dt)),
        "dn_out_norm_g": gain(ks[6], (L, DN_HEAD_DIM)),
        "mla_q_norm_g": gain(ks[7], (L, MLA_Q_RANK)),
        "mla_kv_norm_g": gain(ks[8], (L, MLA_KV_RANK)),
        "mla_w_uq": nrm(ks[9], (L, MLA_Q_RANK, MLA_HEADS * MLA_QK_DIM), MLA_Q_RANK),
        "mla_w_ukv": nrm(ks[10], (L, MLA_KV_RANK, MLA_HEADS * (MLA_NOPE + MLA_V)), MLA_KV_RANK),
        "mla_qk_q_g": gain(ks[11], (L, MLA_QK_DIM)),
        "mla_qk_k_g": gain(ks[12], (L, MLA_QK_DIM)),
        "sg_v_norm_g": gain(ks[13], (L, SG_GROUPS, SG_GROUP_DIM)),
        "sg_w_s": nrm(ks[14], (L, SG_GROUPS, SG_CHUNK, SG_CHUNK), SG_CHUNK),
        "sg_b_s": gain(ks[15], (L, SG_GROUPS, SG_CHUNK)),
        "fox_q_norm_g": gain(ks[16], (L, FOX_HEAD_DIM)),
        "fox_k_norm_g": gain(ks[17], (L, FOX_HEAD_DIM)),
        "fox_f_bias": 4.0 + jax.random.normal(ks[18], (L, FOX_HEADS), f32),
        "w_branch": nrm(ks[19], (L, N_BRANCHES, BRANCH_WIDTH, D_MODEL), BRANCH_WIDTH),
        "w_out": nrm(ks[20], (L, D_MODEL, D_MODEL), D_MODEL),
        "norm2_g": gain(ks[21], (L, D_MODEL)),
        "w_ff1": nrm(ks[22], (L, D_MODEL, D_FF), D_MODEL),
        "w_ff2": nrm(ks[23], (L, D_FF, D_MODEL), D_FF),
    }

def second_block(x, positions, norm1_g, w_in, dn_conv_w, dn_a_log, dn_dt_bias, dn_out_norm_g,
              mla_q_norm_g, mla_kv_norm_g, mla_w_uq, mla_w_ukv, mla_qk_q_g, mla_qk_k_g,
              sg_v_norm_g, sg_w_s, sg_b_s, fox_q_norm_g, fox_k_norm_g, fox_f_bias,
              w_branch, w_out, norm2_g, w_ff1, w_ff2):
    B, S, _ = x.shape
    split_points = np.cumsum(IN_SPLITS)[:-1]
    for l in range(DEPTH):
        h = rms_norm_2(x, norm1_g[l])
        proj = h @ w_in[l]
        (dn_qkv, dn_z, dn_a, dn_b, mla_cq, mla_ckv, mla_kr,
         sg_u, sg_v, fox_qkv, fox_f, gate_logits) = jnp.split(proj, split_points, axis=-1)

        o_a = gated_deltanet(dn_qkv, dn_z, dn_a, dn_b, dn_conv_w[l], dn_a_log[l],
                             dn_dt_bias[l], dn_out_norm_g[l])
        o_b = latent_attention(mla_cq, mla_ckv, mla_kr, positions, mla_q_norm_g[l], mla_kv_norm_g[l],
                               mla_w_uq[l], mla_w_ukv[l], mla_qk_q_g[l], mla_qk_k_g[l])
        o_c = spatial_gating(sg_u, sg_v, sg_v_norm_g[l], sg_w_s[l], sg_b_s[l])
        o_d = forgetting_attention(fox_qkv, fox_f, fox_f_bias[l], fox_q_norm_g[l], fox_k_norm_g[l])

        branches = jnp.stack([o_a.astype(x.dtype), o_b.astype(x.dtype),
                              o_c.astype(x.dtype), o_d.astype(x.dtype)], axis=2)
        projected = jnp.einsum("bsiw,iwd->bsid", branches, w_branch[l])
        gates = jax.nn.sigmoid(gate_logits.reshape(B, S, N_BRANCHES, D_MODEL))
        merged = jnp.sum(gates * projected, axis=2)
        x = x + merged @ w_out[l]

        h2 = rms_norm_2(x, norm2_g[l])
        x = x + jnp.square(jax.nn.relu(h2 @ w_ff1[l])) @ w_ff2[l]
    return x


def setup_inputs(seed=0):
    out = dict(first_inputs(seed))
    for name, value in second_inputs(seed + 1).items():
        if name != "x":
            out[name + "_2"] = value
    return out


def reference(
    x, meta_tokens, mix_norm_g, w_in, conv_w, lambda_q1, lambda_k1, lambda_q2, lambda_k2,
    attn_subln_g, w_out, ffn_norm_g, w_router, w_gate, w_up, w_down, final_norm_g, positions_2,
    norm1_g_2, w_in_2, dn_conv_w_2, dn_a_log_2, dn_dt_bias_2, dn_out_norm_g_2, mla_q_norm_g_2,
    mla_kv_norm_g_2, mla_w_uq_2, mla_w_ukv_2, mla_qk_q_g_2, mla_qk_k_g_2, sg_v_norm_g_2,
    sg_w_s_2, sg_b_s_2, fox_q_norm_g_2, fox_k_norm_g_2, fox_f_bias_2, w_branch_2, w_out_2,
    norm2_g_2, w_ff1_2, w_ff2_2,
):
    x = first_block(
        x, meta_tokens, mix_norm_g, w_in, conv_w, lambda_q1, lambda_k1, lambda_q2, lambda_k2,
        attn_subln_g, w_out, ffn_norm_g, w_router, w_gate, w_up, w_down, final_norm_g,
    )
    return second_block(
        x, positions_2, norm1_g_2, w_in_2, dn_conv_w_2, dn_a_log_2, dn_dt_bias_2,
        dn_out_norm_g_2, mla_q_norm_g_2, mla_kv_norm_g_2, mla_w_uq_2, mla_w_ukv_2, mla_qk_q_g_2,
        mla_qk_k_g_2, sg_v_norm_g_2, sg_w_s_2, sg_b_s_2, fox_q_norm_g_2, fox_k_norm_g_2,
        fox_f_bias_2, w_branch_2, w_out_2, norm2_g_2, w_ff1_2, w_ff2_2,
    )


_drawn_inputs = setup_inputs


def setup_inputs(seed=0):
    import zlib

    import numpy as np

    out = dict(_drawn_inputs(seed))
    spreads = {}
    factors = {'lambda_q1': 8.0,
     'attn_subln_g': 3.729,
     'ffn_norm_g': 3.964,
     'mla_q_norm_g_2': 6.351,
     'mla_kv_norm_g_2': 3.432,
     'mla_qk_q_g_2': 6.075,
     'mla_qk_k_g_2': 6.016,
     'fox_q_norm_g_2': 4.181,
     'fox_k_norm_g_2': 4.613,
     'dn_out_norm_g_2': 3.466,
     'sg_v_norm_g_2': 4.938,
     'sg_b_s_2': 3.411}
    for name, (base, spread) in spreads.items():
        noise = np.random.default_rng([zlib.crc32(name.encode()), seed]).standard_normal(out[name].shape)
        drawn = base * np.exp(spread * noise) if base else spread * noise
        out[name] = __import__('jax').numpy.asarray(drawn.astype(out[name].dtype))
    for name, factor in factors.items():
        out[name] = (out[name] * factor).astype(out[name].dtype)
    return out
```

```python
from contextlib import ExitStack

import numpy as np
import concourse.bass as bass
from concourse import mybir

F32 = mybir.dt.float32
I32 = mybir.dt.int32
ALU = mybir.AluOpType
ACT = mybir.ActivationFunctionType
AX = mybir.AxisListType.X

P = 128
D = 1024
L = 272
NM = 16
NE = 16
CAP = 34
EPS = 1e-6
RING = 12
AR = 22000
TT = [(16, 128), (144, 128), (0, 16)]

C_ID, C_ONE, C_ROT, C_COS, C_SIN, C_IOTA = 0, 128, 256, 384, 656, 928
NCST = 992
K_TRIC, K_TRI, K_ONE, K_BLK, K_SEL, K_LEV, K_MB, K_INV = 0, 128, 256, 384, 512, 768, 1536, 1792
NK2 = 1824
W_N1, W_CONV, W_DT, W_ALOG, W_OUTG, W_QN, W_KVN, W_QG, W_KG = 0, 8, 56, 60, 64, 65, 67, 68, 260
W_SGB, W_FQ, W_FK, W_FB, W_N2, W_SGG = 452, 456, 457, 458, 462, 470
NW2 = 982
RING2 = 4
TWO_PI = 6.283185307179586
C1 = 6.28125
C2 = float(np.float32(0.0019350051879882812))
C3 = TWO_PI - C1 - C2
V_MIXG, V_CONV, V_SUB, V_LAM, V_WR = 0, 8, 20, 21, 277
NVEC = 277 + 128


def constants():
    c = np.zeros((P, NCST), np.float32)
    c[:, C_ID:C_ID + 128] = np.eye(P)
    c[:, C_ONE:C_ONE + 128] = 1.0
    for m in range(P):
        if m % 64 < 32:
            c[m + 32, C_ROT + m] = -1.0
        else:
            c[m - 32, C_ROT + m] = 1.0
    inv = (np.float32(10000.0) ** (-np.arange(0, 64, 2, dtype=np.float32) / np.float32(64))).astype(np.float32)
    ang = np.arange(L, dtype=np.float32)[:, None] * inv[None, :]
    c[:, C_COS:C_COS + L] = np.tile(np.cos(ang).T, (4, 1))
    c[:, C_SIN:C_SIN + L] = np.tile(np.sin(ang).T, (4, 1))
    c[:, C_IOTA:C_IOTA + 64] = np.arange(64)[None, :]
    return c


def constants_2():
    k = np.zeros((P, NK2), np.float32)
    j, i = np.arange(P)[:, None], np.arange(P)[None, :]
    k[:, K_TRIC:K_TRIC + 128] = (j <= i) & (j // 64 == i // 64)
    k[:, K_TRI:K_TRI + 128] = j <= i
    k[:, K_ONE:K_ONE + 128] = 1.0
    k[:, K_BLK:K_BLK + 128] = j // 64 == i // 64
    k[:64, K_SEL:K_SEL + 128] = 1.0
    k[64:, K_SEL + 128:K_SEL + 256] = 1.0
    for n in range(6):
        s = 1 << n
        k[:, K_LEV + 128 * n:K_LEV + 128 * n + 128] = (i // s % 2 == 1) & (j // s == i // s - 1)
    k[:, K_MB + 128:K_MB + 256] = np.where(i <= j, 0.0, -1e30)
    k[:, K_INV:K_INV + 32] = (np.float32(10000.0) ** (-np.arange(0, 64, 2, dtype=np.float32) / np.float32(64)))[None, :]
    return k


class Queue:

    def __init__(self, sem, chained=False):
        self.sem, self.n, self.items, self.chained = sem, 0, [], chained

    def op(self, fn, *after):
        if self.chained and self.n:
            after += ((self.sem, self.n),)
        self.n += 1
        self.items.append((after, fn, self.sem, 1))
        return (self.sem, self.n)

    def quiet(self, fn, *after):
        self.items.append((after, fn, None, 0))

    def dma(self, fn, counter, *after):
        counter[1] += 16
        self.items.append((after, fn, counter[0], 16))
        return (counter[0], counter[1])

    def emit(self, eng):
        reached = {}
        for after, fn, sem, by in self.items:
            for s, v in after:
                if reached.get(s.name, 0) < v:
                    eng.wait_ge(s, v)
                    reached[s.name] = v
            ins = fn(eng) if fn is not None else None
            if sem is not None:
                ins.then_inc(sem, by)


class Banks:

    def __init__(self, ids):
        self.ids, self.at = list(ids), 0
        self.read = {b: [] for b in self.ids}

    def take(self):
        b = self.ids[self.at % len(self.ids)]
        self.at += 1
        return b


def bc(ap, axis, n):
    a = ap.unsqueeze(axis)
    shape = list(a.shape)
    shape[axis] = n
    return a.broadcast_to(shape)


def program(nc, t):
    ctx = ExitStack()
    with ctx:
        def sb(name, cols, dt=F32):
            return ctx.enter_context(nc.sbuf_tensor(f"sb_{name}", [P, cols], dt))

        def sem(name):
            return ctx.enter_context(nc.semaphore(name))

        pe, dve, act, sp = (Queue(sem(f"s_{n}")) for n in ("pe", "dve", "act", "sp"))
        pool = Queue(sem("s_pool"), chained=True)
        PS = ctx.enter_context(nc.psum_tensor("PS", [P, 8, 512], F32))

        ring = sb("ring", RING * 2048)
        cst = sb("cst", NCST)
        vec = sb("vec", NVEC)
        gbc = sb("gbc", 1024)
        Hx = sb("Hx", 3 * 1024)
        sm = sb("sm", 768)
        ar = sb("ar", AR)

        H = Hx[:, :].rearrange("p (t d) -> p t d", t=3)
        ident = cst[:, C_ID:C_ID + 128]
        ones = cst[:, C_ONE:C_ONE + 128]
        nsm = [0]

        def small(n):
            nsm[0] += n
            assert nsm[0] <= 768
            return sm[:, nsm[0] - n:nsm[0]]

        at = [0]

        def take(n, *dims):
            at[0] += n
            assert at[0] <= AR, at[0]
            v = ar[:, at[0] - n:at[0]]
            if len(dims) == 1:
                v = v.rearrange("p (a b) -> p a b", a=dims[0])
            elif len(dims) == 2:
                v = v.rearrange("p (a b c) -> p a b c", a=dims[0], b=dims[1])
            return v

        slot_sem = [[sem(f"w{i}"), 0] for i in range(RING)]
        stream = []
        used = []

        narrow = [None]
        place = []
        holder = [None] * RING
        turns = [0] * RING
        before = []

        def assign():
            i = len(place)
            s = i % RING if narrow[0] is None else (i - narrow[0]) % RING2
            place.append(s)
            before.append(holder[s])
            holder[s] = i
            turns[s] += 1
            return s, turns[s]

        def weights(fn):
            stream.append(fn)
            used.append(None)
            return len(stream) - 1

        class Slot:

            def __init__(self, src, shape=None):
                self.i = weights(src)
                s, turn_ = assign()
                self.v = ring[:, s * 2048:s * 2048 + 2048]
                self.tok = (slot_sem[s][0], 16 * turn_)

            def done(self, tok):
                used[self.i] = tok

        def packed(src, n):
            return [Slot(src[i]) for i in range(n)]

        c_x = [sem("c_x"), 0]
        c_cst = [sem("c_cst"), 0]
        c_vec = [sem("c_vec"), 0]
        c_g = [sem("c_g"), 0]
        Lx = act.dma(lambda e: e.dma_start(H[:, 0:2, :], t["x"]), c_x)
        Lm = act.dma(lambda e: e.dma_start(H[0:NM, 2, :], t["meta"]), c_x)
        Lc = act.dma(lambda e: e.dma_start(cst[:, :], t["cst"]), c_cst)
        Lv = act.dma(lambda e: e.dma_start(vec[:, :], t["vec"]), c_vec)
        Lg = act.dma(lambda e: e.dma_start(gbc[:, :], t["gbc"][0]), c_g)

        c_k2 = [sem("c_k2"), 0]
        posi = ctx.enter_context(nc.sbuf_tensor("sb_posi", [P, 2], I32))
        tab = sb("tab", 128)
        invf = sb("invf", 32)
        cosN = tab[:, 0:64].rearrange("p (t c) -> p t c", t=2)
        sinN = tab[:, 64:128].rearrange("p (t c) -> p t c", t=2)
        Lp = sp.dma(lambda e: e.dma_start(posi[:, :], t["pos"]), c_k2)
        Lp = sp.dma(lambda e: e.dma_start(invf[:, :], t["kw2"][:, K_INV:K_INV + 32]), c_k2)
        posf = small(2)
        tr_ = small(64 * 3)
        ang, kk, rr = (tr_[:, 64 * q:64 * q + 64] for q in range(3))
        a = dve.op(lambda e: e.tensor_copy(posf, posi[:, :]), Lp)
        a = dve.op(lambda e: e.tensor_tensor(ang.rearrange("p (t c) -> p t c", t=2), bc(posf, 2, 32), bc(invf[:, :], 1, 2), ALU.mult), a)
        a = dve.op(lambda e: e.tensor_scalar(kk, ang, 1.0 / TWO_PI, 12582912.0, ALU.mult, ALU.add), a)
        a = dve.op(lambda e: e.tensor_scalar(kk, kk, -12582912.0, None, ALU.add), a)
        a = dve.op(lambda e: e.scalar_tensor_tensor(rr, kk, -C1, ang, ALU.mult, ALU.add), a)
        a = dve.op(lambda e: e.scalar_tensor_tensor(rr, kk, -C2, rr, ALU.mult, ALU.add), a)
        a = dve.op(lambda e: e.scalar_tensor_tensor(rr, kk, -C3, rr, ALU.mult, ALU.add), a)
        a = dve.op(lambda e: e.tensor_scalar(rr, rr, 3.1415925, -3.1415925, ALU.min, ALU.max), a)
        x = act.op(lambda e: e.activation(sinN.rearrange("p t c -> p (t c)"), rr, ACT.Sin), a)
        a = dve.op(lambda e: e.tensor_scalar(kk, rr, TWO_PI / 4, TWO_PI / 2, ALU.add, ALU.is_gt), a)
        a = dve.op(lambda e: e.scalar_tensor_tensor(kk, kk, -TWO_PI, rr, ALU.mult, ALU.add), a)
        a = dve.op(lambda e: e.tensor_scalar(kk, kk, TWO_PI / 4, 3.1415925, ALU.add, ALU.min), a)
        a = dve.op(lambda e: e.tensor_scalar(kk, kk, -3.1415925, None, ALU.max), a)
        k_tab = act.op(lambda e: e.activation(cosN.rearrange("p t c -> p (t c)"), kk, ACT.Sin), a)

        XN = take(3072, 3)
        hnT = take(8 * L, 8)
        junk = take(1024)
        ss = small(4)
        rs = small(4)
        mhalf = small(16)
        k_mh = dve.op(lambda e: e.memset(mhalf, -0.5))
        bk = Banks(range(8))

        def rms(src, n, sscol, rscol, inv_n, width_junk, *after):
            a = act.op(lambda e: e.activation(width_junk, src, ACT.Square, accum_out=sscol), *after)
            b = dve.op(lambda e: e.tensor_scalar(rscol, sscol, inv_n, EPS, ALU.mult, ALU.add), a)
            c = pool.op(lambda e: e.tensor_tensor(rscol, rscol, mhalf[0:n, 0:1], ALU.pow), b, k_mh)
            return a, c

        def turn(src, n, dst_fn, evac_fn, *after):
            pass

        def turn_tile(XN, ti, n, col0, dstT, after, gcol=None, eng=None):
            out = []
            for half in range(2):
                b = bk.take()
                rd = bk.read[b]
                for k in range(4):
                    c = half * 4 + k
                    f = lambda e, b=b, k=k, c=c: e.transpose(
                        PS[:, b, k * 128:k * 128 + n], XN[0:n, ti, c * 128:c * 128 + 128], ident[0:n, 0:n])
                    if k < 3:
                        pe.quiet(f, *(rd + after + [Lc] if k == 0 else []))
                    else:
                        tk = pe.op(f)
                src = PS[:, b, :].rearrange("p (k c) -> p k c", k=4)[:, :, 0:n]
                dst = dstT[:, half * 4:half * 4 + 4, col0:col0 + n]
                if gcol is not None:
                    r = dve.op(lambda e, s=src, d=dst, h=half: e.tensor_tensor(
                        d, s, bc(gcol[:, h * 4:h * 4 + 4], 2, n), ALU.mult), tk, Lv)
                elif half == 0:
                    r = act.op(lambda e, s=src, d=dst: e.copy(d, s), tk)
                else:
                    r = dve.op(lambda e, s=src, d=dst: e.tensor_copy(d, s), tk)
                bk.read[b] = [r]
                out.append(r)
            return out

        hn_ok = []
        xn_free = []
        jprev = ()
        for ti, (c0, n) in enumerate(TT):
            a, r = rms(H[0:n, ti, :], n, ss[0:n, ti:ti + 1], rs[0:n, ti:ti + 1], 1.0 / D, junk[0:n, :], Lx, Lm, *jprev)
            jprev = (a,)
            x = dve.op(lambda e, ti=ti, n=n: e.tensor_scalar(
                XN[0:n, ti, :], H[0:n, ti, :], rs[0:n, ti:ti + 1], None, ALU.mult), r)
            hn_ok += turn_tile(XN, ti, n, c0, hnT, [x], vec[:, V_MIXG:V_MIXG + 8])
        last_turn = (pe.sem, pe.n)

        def proj_T(sl, half, N, actT, *after):
            b = bk.take()
            for k in range(8):
                f = lambda e, k=k: e.matmul(PS[:, b, 0:N], sl.v.rearrange("p (k c) -> p k c", k=8)[
                    :, k, half * 128:half * 128 + 128], actT[:, k, 0:N], start=(k == 0), stop=(k == 7))
                w = (sl.tok, *bk.read[b], *after) if k == 0 else ()
                if k < 7:
                    pe.quiet(f, *w)
                else:
                    tk = pe.op(f, *w)
            if half == 1:
                sl.done(tk)
            return b, tk

        qraw = take(2 * L, 2)
        t1 = take(2 * L, 2)
        t2 = take(2 * L, 2)
        kT = take(4 * L, 4)
        qz = take(8 * L, 4, 2)
        z0 = pool.op(lambda e: e.memset(qz[64:128, :, 0, :], 0.0))
        z1 = pool.op(lambda e: e.memset(qz[0:64, :, 1, :], 0.0))
        cosT = cst[:, C_COS:C_COS + L]
        sinT = cst[:, C_SIN:C_SIN + L]
        rotm = cst[:, C_ROT:C_ROT + 128]
        kq_ok = []
        pend = []
        free_raw = [[], []]
        free_t = [[], []]

        def rope(j, which, h, raw_tok):
            b = bk.take()
            tk = pe.op(lambda e: e.matmul(PS[:, b, 0:L], rotm, qraw[:, j, :], start=True, stop=True),
                       raw_tok, *bk.read[b])
            a = pool.op(lambda e: e.tensor_tensor(t1[:, j, :], qraw[:, j, :], cosT, ALU.mult), raw_tok, Lc, *free_t[j])
            c = dve.op(lambda e: e.tensor_tensor(t2[:, j, :], PS[:, b, 0:L], sinT, ALU.mult), tk, *free_t[j])
            bk.read[b] = [c]
            free_raw[j] = [tk, a]
            if which == 0:
                r = [dve.op(lambda e: e.tensor_tensor(kT[:, h, :], t1[:, j, :], t2[:, j, :], ALU.add), a, c)]
            else:
                r = [dve.op(lambda e, i=i: e.tensor_tensor(
                    qz[64 * i:64 * i + 64, h, i, :], t1[64 * i:64 * i + 64, j, :],
                    t2[64 * i:64 * i + 64, j, :], ALU.add), a, c) for i in range(2)]
            free_t[j] = r
            kq_ok.extend(r)

        n = 0
        for which in range(2):
            for s2 in range(2):
                sl = Slot(t["w_in"][which * 2 + s2])
                for half in range(2):
                    j = n % 2
                    b, tk = proj_T(sl, half, L, hnT, *hn_ok)
                    r = act.op(lambda e, b=b, j=j: e.copy(qraw[:, j, :], PS[:, b, 0:L]), tk, *free_raw[j])
                    bk.read[b] = [r]
                    if pend:
                        rope(*pend.pop())
                    pend.append((j, which, s2 * 2 + half, r))
                    n += 1
        V = take(3 * 512, 3)
        sv = [Slot(t["w_in"][4]), Slot(t["w_in"][5])]
        v_ok = []
        for ti, (c0, n) in enumerate(TT):
            b = bk.take()
            for k in range(8):
                f = lambda e, k=k, b=b, c0=c0, n=n: e.matmul(
                    PS[0:n, b, :], hnT[:, k, c0:c0 + n], sv[k // 4].v[:, (k % 4) * 512:(k % 4) * 512 + 512],
                    start=(k == 0), stop=(k == 7))
                w = (sv[0].tok, *bk.read[b]) if k == 0 else (sv[1].tok,) if k == 4 else ()
                if k == 7:
                    tk = pe.op(f, *w)
                else:
                    pe.quiet(f, *w)
            r = act.op(lambda e, b=b, ti=ti, n=n: e.copy(V[0:n, ti, :], PS[0:n, b, :]), tk)
            bk.read[b] = [r]
            v_ok.append(r)
            if pend:
                rope(*pend.pop())
        sv[0].done(tk)
        sv[1].done(tk)

        lt = small(128)
        l2 = small(2)
        l3 = small(2)
        lam = small(2)
        vl = vec[:, V_LAM:V_LAM + 256].rearrange("p (i a d) -> p i a d", i=2, a=2)
        a = dve.op(lambda e: e.tensor_tensor(lt.rearrange("p (i d) -> p i d", i=2), vl[:, :, 0, :], vl[:, :, 1, :], ALU.mult), Lv)
        a = dve.op(lambda e: e.tensor_reduce(l2, lt.rearrange("p (i d) -> p i d", i=2), AX, ALU.add), a)
        a = act.op(lambda e: e.activation(l3, l2, ACT.Exp), a)
        a = dve.op(lambda e: e.tensor_tensor(lam[:, 0:1], l3[:, 1:2], l3[:, 0:1], ALU.subtract), a)
        k_lam = dve.op(lambda e: e.tensor_scalar(lam[:, 1:2], lam[:, 0:1], -(0.8 - 0.6 * 1.0), None, ALU.add), a)

        Pm = take(2 * 2 * L, 2, 2)
        Am = take(2 * L, 2)
        AT = take(2 * 3 * 128, 2, 3)
        O = take(3 * 512, 3)
        O2 = take(512)
        mixT = take(8 * L, 8)
        cxs = take(L)
        up = take(2 * (L + 2), 2)
        cv = take(2 * L, 2)
        st = small(16)
        z2 = pool.op(lambda e: e.memset(up[:, :, 0:1], 0.0))
        z3 = pool.op(lambda e: e.memset(up[:, :, L + 1:L + 2], 0.0))
        p_free = [[], []]
        a_free = [[], []]
        at_free = [[], []]

        def scores(u):
            ti, h = divmod(u, 4)
            c0, n = TT[ti]
            j = u % 2
            bs = [bk.take(), bk.take()]
            rowm = st[0:n, 8 * j:8 * j + 2]
            rowb = st[0:n, 8 * j + 2:8 * j + 4]
            rows = st[0:n, 8 * j + 4:8 * j + 6]
            rowr = st[0:n, 8 * j + 6:8 * j + 8]
            ex = []
            for i in range(2):
                b = bs[i]
                tk = pe.op(lambda e, b=b, i=i: e.matmul(
                    PS[0:n, b, 0:L], qz[:, h, i, c0:c0 + n], kT[:, h, :], start=True, stop=True),
                    *kq_ok, z0, z1, *bk.read[b])
                m = dve.op(lambda e, b=b, i=i: e.tensor_reduce(rowm[:, i:i + 1], PS[0:n, b, 0:L], AX, ALU.max), tk, *a_free[j])
                m = dve.op(lambda e, i=i: e.tensor_scalar(rowb[:, i:i + 1], rowm[:, i:i + 1], -0.125, None, ALU.mult), m)
                x = act.op(lambda e, b=b, i=i: e.activation(
                    Pm[0:n, j, i, :], PS[0:n, b, 0:L], ACT.Exp, bias=rowb[:, i:i + 1], scale=0.125,
                    accum_out=rows[:, i:i + 1]), m, *p_free[j])
                bk.read[b] = [x]
                ex.append(x)
            r = dve.op(lambda e: e.reciprocal(rowr, rows), *ex)
            c = dve.op(lambda e: e.tensor_scalar(rowm[:, 1:2], rowr[:, 1:2], lam[0:n, 1:2], None, ALU.mult), r, k_lam)
            c = dve.op(lambda e: e.tensor_scalar(Am[0:n, j, :], Pm[0:n, j, 1, :], rowm[:, 1:2], None, ALU.mult), c, *a_free[j])
            c = dve.op(lambda e: e.scalar_tensor_tensor(
                Am[0:n, j, :], Pm[0:n, j, 0, :], rowr[:, 0:1], Am[0:n, j, :], ALU.mult, ALU.add), c)
            p_free[j] = [c]
            return c

        ob = {}

        def pv(u, tok):
            ti, h = divmod(u, 4)
            c0, n = TT[ti]
            j = u % 2
            b = bk.take()
            for kt, (k0, kn) in enumerate(TT):
                f = lambda e, kt=kt, k0=k0, kn=kn: e.transpose(
                    PS[0:kn, b, kt * 128:kt * 128 + n], Am[0:n, j, k0:k0 + kn], ident[0:n, 0:n])
                if kt < 2:
                    pe.quiet(f, *((tok, *bk.read[b]) if kt == 0 else ()))
                else:
                    tk = pe.op(f)
            a_free[j] = [tk]
            src = PS[:, b, 0:256].rearrange("p (k c) -> p k c", k=2)[:, :, 0:n]
            r1 = act.op(lambda e: e.copy(AT[:, j, 0:2, 0:n], src), tk, *at_free[j])
            r2 = act.op(lambda e: e.copy(AT[0:NM, j, 2, 0:n], PS[0:NM, b, 256:256 + n]), tk)
            bk.read[b] = [r2]
            if h == 0:
                ob[ti] = obk.take()
            o = ob[ti]
            for kt, (k0, kn) in enumerate(TT):
                f = lambda e, kt=kt, kn=kn: e.matmul(
                    PS[0:n, o, h * 128:h * 128 + 128], AT[0:kn, j, kt, 0:n], V[0:kn, kt, h * 128:h * 128 + 128],
                    start=(kt == 0), stop=(kt == 2))
                if kt < 2:
                    pe.quiet(f, *((r2, *v_ok, *(obk.read[o] if h == 0 else [])) if kt == 0 else ()))
                else:
                    tk = pe.op(f)
            at_free[j] = [tk]
            if h == 3:
                r = act.op(lambda e: e.copy(O[0:n, ti, :], PS[0:n, o, :]), tk)
                obk.read[o] = [r]
                return r

        oss = small(12)
        osr = small(12)
        o2_free = []

        def o_norm(ti, tok):
            n = TT[ti][1]
            c0 = TT[ti][0]
            o3 = O[0:n, ti, :].rearrange("p (h d) -> p h d", h=4)
            a = pool.op(lambda e: e.tensor_tensor(O2[0:n, :], O[0:n, ti, :], O[0:n, ti, :], ALU.mult), tok, *o2_free)
            a = dve.op(lambda e: e.tensor_reduce(oss[0:n, 4 * ti:4 * ti + 4], O2[0:n, :].rearrange("p (h d) -> p h d", h=4), AX, ALU.add), a)
            o2_free[:] = [a]
            a = dve.op(lambda e: e.tensor_scalar(osr[0:n, 4 * ti:4 * ti + 4], oss[0:n, 4 * ti:4 * ti + 4], 1.0 / 128, EPS, ALU.mult, ALU.add), a)
            a = pool.op(lambda e: e.tensor_tensor(osr[0:n, 4 * ti:4 * ti + 4], osr[0:n, 4 * ti:4 * ti + 4], mhalf[0:n, 0:4], ALU.pow), a)
            a = dve.op(lambda e: e.tensor_tensor(o3, o3, bc(osr[0:n, 4 * ti:4 * ti + 4], 2, 128), ALU.mult), a)
            b = bk.take()
            for h in range(4):
                f = lambda e, h=h: e.transpose(PS[:, b, h * 128:h * 128 + n], O[0:n, ti, h * 128:h * 128 + 128], ident[0:n, 0:n])
                if h < 3:
                    pe.quiet(f, *((a, *bk.read[b]) if h == 0 else ()))
                else:
                    tk = pe.op(f)
            r = dve.op(lambda e: e.tensor_scalar(
                mixT[:, 0:4, c0:c0 + n], PS[:, b, :].rearrange("p (h c) -> p h c", h=4)[:, :, 0:n],
                vec[:, V_SUB:V_SUB + 1], 0.8, ALU.mult, ALU.mult), tk)
            bk.read[b] = [r]
            return r

        cx_state = {}
        cxs_free = [[]]
        up_free = [[z2, z3], [z2, z3]]
        mix_ok = []

        def conv(i):
            m, part = divmod(i, 3)
            if i % 2 == 0:
                cx_state["sl"] = Slot(t["w_in"][6 + i // 2])
            b, tk = proj_T(cx_state["sl"], i % 2, L, hnT)
            j = m % 2
            cw = lambda k: vec[:, V_CONV + 3 * m + k:V_CONV + 3 * m + k + 1]
            if part == 0:
                r = act.op(lambda e: e.copy(cxs, PS[:, b, 0:L]), tk, *cxs_free[0])
                cx_state["cx"] = r
            elif part == 1:
                r = dve.op(lambda e: e.tensor_tensor(up[:, j, 1:L + 1], PS[:, b, 0:L], cxs, ALU.mult), tk, cx_state["cx"], *up_free[j])
                cxs_free[0] = [r]
                a = dve.op(lambda e: e.tensor_scalar(cv[:, j, :], up[:, j, 0:L], cw(0), None, ALU.mult), r, *up_free[j])
                a = dve.op(lambda e: e.scalar_tensor_tensor(cv[:, j, :], up[:, j, 1:L + 1], cw(1), cv[:, j, :], ALU.mult, ALU.add), a)
                a = dve.op(lambda e: e.scalar_tensor_tensor(cv[:, j, :], up[:, j, 2:L + 2], cw(2), cv[:, j, :], ALU.mult, ALU.add), a)
                cx_state["cv"] = a
            else:
                r = dve.op(lambda e: e.tensor_tensor(mixT[:, 4 + m, :], PS[:, b, 0:L], cv[:, j, :], ALU.mult), tk, cx_state["cv"])
                up_free[j] = [r]
                mix_ok.append(r)
            bk.read[b] = [r]

        obk = Banks([6, 7])
        att = Banks(range(6))
        for b in range(8):
            (obk if b > 5 else att).read[b] = bk.read[b]
        bk = att
        prev = None
        for u in range(12):
            tok = scores(u)
            conv(u)
            if prev is not None:
                r = pv(u - 1, prev)
                if r is not None:
                    mix_ok.append(o_norm((u - 1) // 4, r))
            prev = tok
        r = pv(11, prev)
        mix_ok.append(o_norm(2, r))

        whole = Banks(range(8))
        for b in range(8):
            whole.read[b] = (obk if b > 5 else att).read[b]
        bk = whole
        so1 = [Slot(t["w_out"][i]) for i in range(4)]
        H_ok = {}
        for ti, (c0, n) in enumerate(TT):
            for db in range(2):
                b = bk.take()
                for c in range(8):
                    f = lambda e, c=c, b=b, c0=c0, n=n, db=db: e.matmul(
                        PS[0:n, b, :], mixT[:, c, c0:c0 + n],
                        so1[c // 2].v[:, (c % 2) * 1024 + db * 512:(c % 2) * 1024 + db * 512 + 512],
                        start=(c == 0), stop=(c == 7))
                    w = ((*mix_ok, *bk.read[b]) if c == 0 else ()) + (so1[c // 2].tok,)
                    if c < 7:
                        pe.quiet(f, *w)
                    else:
                        tk = pe.op(f, *w)
                hv = H[0:n, ti, db * 512:db * 512 + 512]
                r = dve.op(lambda e, hv=hv, b=b, n=n: e.tensor_tensor(hv, hv, PS[0:n, b, :], ALU.add), tk)
                bk.read[b] = [r]
                H_ok[ti] = [r] if db == 0 else H_ok[ti] + [r]
        for s in so1:
            s.done(tk)

        lg = take(3 * 16, 3)
        af = take(3 * 16, 3)
        rt = small(12)
        wr = vec[:, V_WR:V_WR + 128].rearrange("p (k c) -> p k c", k=8)
        xn_ok = []
        af_ok = []
        aT = take(L + 6)
        wk = take(2 * (L + 6), 2)
        bt = bk.take()
        bt_read = bk.read[bt]
        bk_ids = [b for b in range(8) if b != bt]
        rest = Banks(bk_ids)
        for b in bk_ids:
            rest.read[b] = bk.read[b]
        bk = rest
        for ti, (c0, n) in enumerate(TT):
            a, r = rms(H[0:n, ti, :], n, ss[0:n, ti:ti + 1], rs[0:n, ti:ti + 1], 1.0 / D, junk[0:n, :], *H_ok[ti], *jprev)
            jprev = (a,)
            x = dve.op(lambda e, ti=ti, n=n: e.scalar_tensor_tensor(
                XN[0:n, ti, :], H[0:n, ti, :], rs[0:n, ti:ti + 1], gbc[0:n, :], ALU.mult, ALU.mult), r, Lg, last_turn)
            xn_ok.append(x)
            tr = turn_tile(XN, ti, n, c0, hnT, [x, tk])
            b = bk.take()
            for k in range(8):
                f = lambda e, k=k, b=b, c0=c0, n=n: e.matmul(
                    PS[0:n, b, 0:16], hnT[:, k, c0:c0 + n], wr[:, k, :], start=(k == 0), stop=(k == 7))
                if k < 7:
                    pe.quiet(f, *((*tr, Lv, *bk.read[b]) if k == 0 else ()))
                else:
                    t3 = pe.op(f)
            m = rt[0:n, 4 * ti:4 * ti + 1]
            s_ = rt[0:n, 4 * ti + 1:4 * ti + 2]
            r_ = rt[0:n, 4 * ti + 2:4 * ti + 3]
            a = dve.op(lambda e, m=m, b=b, n=n: e.tensor_reduce(m, PS[0:n, b, 0:16], AX, ALU.max, negate=True), t3)
            a = act.op(lambda e, ti=ti, n=n, b=b, m=m, s_=s_: e.activation(
                lg[0:n, ti, :], PS[0:n, b, 0:16], ACT.Exp, bias=m, scale=1.0, accum_out=s_), a)
            bk.read[b] = [a]
            a = dve.op(lambda e, s_=s_, r_=r_: e.reciprocal(r_, s_), a)
            a = dve.op(lambda e, ti=ti, n=n, r_=r_: e.tensor_scalar(af[0:n, ti, :], lg[0:n, ti, :], r_, None, ALU.mult), a)
            af_ok.append(a)
            t4 = pe.op(lambda e, ti=ti, n=n, c0=c0: e.transpose(PS[0:16, bt, c0:c0 + n], af[0:n, ti, :], ident[0:n, 0:n]), a, *bt_read)
        a0 = dve.op(lambda e: e.tensor_copy(aT[0:16, 0:L], PS[0:16, bt, 0:L]), t4)
        a1 = dve.op(lambda e: e.memset(aT[0:16, L:L + 6], 2.0))
        bk_bt = [a0]
        m8 = small(8)
        cur = aT
        a = a1
        for r in range(5):
            a = dve.op(lambda e, cur=cur: e.max(m8[0:16, :], cur[0:16, :]), a, a0)
            nxt = wk[:, r % 2, :]
            a = dve.op(lambda e, cur=cur, nxt=nxt: e.match_replace(nxt[0:16, :], m8[0:16, :], cur[0:16, :], -1.0), a)
            cur = nxt
        mk = wk[0:16, 1, 0:L]
        cs = aT[0:16, 0:L]
        fin = wk[0:16, 0, 0:L]
        a = dve.op(lambda e: e.tensor_scalar(mk, fin, -1.0, None, ALU.is_equal), a)
        a = dve.op(lambda e: e.tensor_tensor_scan(cs, ones[0:16, 0:1].broadcast_to([16, L]), mk, 0.0, ALU.mult, ALU.add), a)
        a = dve.op(lambda e: e.tensor_tensor(cs, cs, mk, ALU.mult), a)
        a = dve.op(lambda e: e.tensor_scalar(cs, cs, -1.0, None, ALU.add), a)
        ps_ = take(3 * 16, 3)
        for ti, (c0, n) in enumerate(TT):
            t4 = pe.op(lambda e, ti=ti, n=n, c0=c0: e.transpose(PS[0:n, bt, ti * 16:ti * 16 + 16], cs[:, c0:c0 + n], ident[0:16, 0:16]), a)
        a = dve.op(lambda e: e.tensor_copy(ps_[:, 0:2, :], PS[:, bt, 0:32].rearrange("p (t c) -> p t c", t=2)), t4)
        b_ = dve.op(lambda e: e.tensor_copy(ps_[0:NM, 2, :], PS[0:NM, bt, 32:48]), t4)
        bt_free = b_
        base = at[0]
        at[0] = 3072
        S = take(3 * 1024, 3, 16)
        XG = take(2 * 1024, 2, 8)
        SL = take(1024, 2)
        Hh = take(1024, 2)
        HT = take(2 * 1024, 2, 8)
        Y = take(2 * 1024, 2)
        GA = take(256, 2)
        GT = take(256, 2)
        assert at[0] <= AR - 3 * 16 * 3 - 3 * (L + 6)
        at[0] = base
        iota = cst[:, C_IOTA:C_IOTA + 64]
        s_ok = []
        for ti, (c0, n) in enumerate(TT):
            s_ok.append(dve.op(lambda e, ti=ti, n=n: e.tensor_tensor(
                S[0:n, ti, :, :], bc(iota[0:n, :], 1, 16), bc(ps_[0:n, ti, :], 2, 64), ALU.is_equal), a, b_))

        KW = ar[:, 14848:14848 + NK2 + NW2]
        Lk2 = act.dma(lambda e: e.dma_start(KW, t["kw2"]), c_k2, *s_ok, (act.sem, act.n), (pe.sem, pe.n), (pool.sem, pool.n))
        Lg2 = act.dma(lambda e: e.dma_start(gbc[:, :], t["gbc"][1]), c_g, *xn_ok)

        misc = Banks([5, 6, 7])
        for b in misc.ids:
            misc.read[b] = [bt_free, (act.sem, act.n), (dve.sem, dve.n), (pe.sem, pe.n)]
        start_all = [(act.sem, act.n), (dve.sem, dve.n)]
        gu_free = [list(start_all), list(start_all)]
        y_free = list(start_all)
        xg_free = [[], []]
        xg_ok = [None, None]
        ht_free = [[], []]
        yb_free = [[], []]
        gt_ok = {}
        y_tok = {}

        def gather(p):
            j = p % 2
            ok = []
            for half in range(2):
                b = misc.take()
                for c4 in range(4):
                    c = half * 4 + c4
                    for ti, (c0, n) in enumerate(TT):
                        f = lambda e, b=b, c4=c4, c=c, ti=ti, n=n: e.matmul(
                            PS[:, b, c4 * 128:c4 * 128 + 128], XN[0:n, ti, c * 128:c * 128 + 128],
                            S[0:n, ti, 2 * p:2 * p + 2, :], start=(ti == 0), stop=(ti == 2))
                        w = (*s_ok, *xn_ok, *misc.read[b]) if c4 == 0 and ti == 0 else ()
                        if c4 == 3 and ti == 2:
                            tk = pe.op(f, *w)
                        else:
                            pe.quiet(f, *w)
                dst = XG[:, j, half * 4:half * 4 + 4, :]
                src = PS[:, b, :].rearrange("p (k c) -> p k c", k=4)
                if half == 0:
                    r = act.op(lambda e, dst=dst, src=src: e.copy(dst, src), tk, *xg_free[j])
                else:
                    r = dve.op(lambda e, dst=dst, src=src: e.tensor_copy(dst, src), tk, *xg_free[j])
                misc.read[b] = [r]
                ok.append(r)
            xg_ok[j] = ok

        ga_free = [[]]
        gt_free = [[]]

        def gates(p):
            a = [dve.op(lambda e, ti=ti: e.tensor_tensor(
                GA[:, ti, :].rearrange("p (e s) -> p e s", e=2), S[:, ti, 2 * p:2 * p + 2, :],
                bc(af[:, ti, 2 * p:2 * p + 2], 2, 64), ALU.mult), *ga_free[0]) for ti in range(2)]
            b = misc.take()
            pe.quiet(lambda e: e.transpose(PS[:, b, 0:128], GA[:, 0, :], ident), *a, *misc.read[b])
            tk = pe.op(lambda e: e.transpose(PS[:, b, 128:256], GA[:, 1, :], ident))
            ga_free[0] = [tk]
            r = dve.op(lambda e: e.tensor_copy(GT[:, :, :], PS[:, b, 0:256].rearrange("p (t c) -> p t c", t=2)), tk, *gt_free[0])
            misc.read[b] = [r]
            gt_ok[p] = r

        def scatter(p):
            j = p % 2
            out = []
            for ti in range(2):
                for db in range(2):
                    b = misc.take()
                    tk = pe.op(lambda e, ti=ti, db=db, b=b: e.matmul(
                        PS[:, b, :], GT[:, ti, :], Y[:, j, db * 512:db * 512 + 512], start=True, stop=True),
                        gt_ok[p], *y_tok[p], *misc.read[b])
                    hv = H[:, ti, db * 512:db * 512 + 512]
                    r = dve.op(lambda e, hv=hv, b=b: e.tensor_tensor(hv, hv, PS[:, b, :], ALU.add), tk)
                    misc.read[b] = [r]
                    out.append(r)
            gt_free[0] = [tk]
            yb_free[j] = [tk]
            return out

        def gate_up(ex):
            p, par = divmod(ex, 2)
            j = p % 2
            for k in range(8):
                for mat, name in enumerate(("w_gate", "w_up")):
                    sl = Slot(t[name][ex, k * 128:k * 128 + 128, :])
                    for q in range(2):
                        for g in range(2):
                            f = lambda e, k=k, mat=mat, q=q, g=g, sl=sl: e.matmul(
                                PS[64 * g:64 * g + 64, 2 * mat + q, :], XG[:, j, k, 64 * par:64 * par + 64],
                                sl.v[:, (2 * g + q) * 512:(2 * g + q) * 512 + 512], start=(k == 0), stop=(k == 7))
                            w = [sl.tok, *xg_ok[j]]
                            if k == 0:
                                w += gu_free[q]
                            if q == 1 and g == 1:
                                tk = pe.op(f, *w)
                            else:
                                pe.quiet(f, *w)
                    sl.done(tk)
            if par == 1:
                xg_free[j] = [tk]
            return tk

        hh_free = [[], []]

        def hidden(ex, tk):
            ok = []
            for q in range(2):
                a = act.op(lambda e, q=q: e.activation(SL[:, q, :], PS[:, q, :], ACT.Silu), tk, *hh_free[q])
                r = dve.op(lambda e, q=q: e.tensor_tensor(Hh[:, q, :], SL[:, q, :], PS[:, 2 + q, :], ALU.mult), a, *hh_free[q])
                gu_free[q] = [r]
                ok.append(r)
            return ok

        def down(ex, hok):
            p, par = divmod(ex, 2)
            j = ex % 2
            ht_ok = []
            for q in range(2):
                b = misc.take()
                for i in range(4):
                    f = lambda e, q=q, i=i, b=b: e.transpose(PS[:, b, i * 128:i * 128 + 128], Hh[:, q, i * 128:i * 128 + 128], ident)
                    if i < 3:
                        pe.quiet(f, *((hok[q], *misc.read[b]) if i == 0 else ()))
                    else:
                        tk = pe.op(f)
                hh_free[q] = [tk]
                dst = HT[:, j, 4 * q:4 * q + 4, :]
                src = PS[:, b, :].rearrange("p (k c) -> p k c", k=4)
                if q == 0:
                    r = act.op(lambda e, dst=dst, src=src: e.copy(dst, src), tk, *ht_free[j])
                else:
                    r = dve.op(lambda e, dst=dst, src=src: e.tensor_copy(dst, src), tk, *ht_free[j])
                misc.read[b] = [r]
                ht_ok.append(r)
            for s in range(8):
                sl = Slot(t["w_down"][ex, 256 * s:256 * s + 256, :].rearrange("(a p) d -> p a d", p=128))
                for a in range(2):
                    c = 2 * s + a
                    for g in range(2):
                        f = lambda e, a=a, g=g, c=c, sl=sl: e.matmul(
                            PS[64 * g:64 * g + 64, 4, :], HT[:, j, c % 8, (c // 8) * 64:(c // 8) * 64 + 64],
                            sl.v[:, a * 1024 + g * 512:a * 1024 + g * 512 + 512], start=(c == 0), stop=(c == 15))
                        w = [sl.tok, ht_ok[0], ht_ok[1]] + (list(y_free) if c == 0 else [])
                        if a == 1 and g == 1:
                            tk = pe.op(f, *w)
                        else:
                            pe.quiet(f, *w)
                sl.done(tk)
            ht_free[j] = [tk]
            rs_ = [act.op(lambda e, g=g: e.copy(
                Y[64 * par:64 * par + 64, p % 2, 512 * g:512 * g + 512], PS[64 * g:64 * g + 64, 4, :]),
                tk, *yb_free[p % 2]) for g in range(2)]
            y_free[:] = rs_
            y_tok.setdefault(p, []).extend(rs_)

        NX = t.get("n_experts", NE)
        if NX:
            gather(0)
        for ex in range(NX):
            tk = gate_up(ex)
            hok = hidden(ex, tk)
            if ex % 2 == 0:
                if ex >= 2:
                    scatter(ex // 2 - 1)
                gates(ex // 2)
            elif ex + 1 < NX:
                gather(ex // 2 + 1)
            down(ex, hok)
        moe_ok = scatter(NX // 2 - 1) if NX else H_ok[0] + H_ok[1]

        narrow[0] = len(place)
        KT = KW[:, 0:NK2]
        VW = KW[:, NK2:NK2 + NW2]
        moe_end = [(act.sem, act.n), (dve.sem, dve.n), (pe.sem, pe.n)]
        segs = [[ar, 0, 14848], [ar, 14848 + NK2 + NW2, AR], [ring, RING2 * 2048, RING * 2048],
                [Hx, 2048, 3072]]

        def room(n, *dims):
            for s_ in segs:
                if s_[2] - s_[1] >= n:
                    v = s_[0][:, s_[1]:s_[1] + n]
                    s_[1] += n
                    if len(dims) == 1:
                        v = v.rearrange("p (a b) -> p a b", a=dims[0])
                    elif len(dims) == 2:
                        v = v.rearrange("p (a b c) -> p a b c", a=dims[0], b=dims[1])
                    return v
            raise ValueError(f"no room for {n}: {[x[2] - x[1] for x in segs]}")

        XB = room(2048, 2)
        hT = room(2048, 8)
        bk = Banks(range(8))
        for b in bk.ids:
            bk.read[b] = list(moe_end)
        fr = small(8)

        def rms2(XB, ti, c, *after):
            x = fr[:, c:c + 1]
            a = act.op(lambda e: e.activation(XB[:, ti, :], H[:, ti, :], ACT.Square, accum_out=x), *after)
            b = dve.op(lambda e: e.tensor_scalar(x, x, 1.0 / D, EPS, ALU.mult, ALU.add), a)
            return pool.op(lambda e: e.tensor_tensor(x, x, mhalf[:, 0:1], ALU.pow), b, k_mh), x

        hT_ok = []
        for ti in range(2):
            r, x = rms2(XB, ti, ti, *moe_end)
            a = dve.op(lambda e, ti=ti, x=x: e.scalar_tensor_tensor(H[:, ti, :], H[:, ti, :], x, gbc[:, :], ALU.mult, ALU.mult), r, Lg2)
            r, x = rms2(XB, ti, 2 + ti, a)
            a = dve.op(lambda e, ti=ti, x=x: e.tensor_scalar(XB[:, ti, :], H[:, ti, :], x, None, ALU.mult), r)
            hT_ok += turn_tile(XB, ti, 128, 128 * ti, hT, [a], VW[:, W_N1:W_N1 + 8])
        gbc_free = a

        def tile_T(sl, off, K, lhs, rhs, N, *after):
            b = bk.take()
            for k in range(K):
                f = lambda e, k=k: e.matmul(PS[:, b, 0:N], lhs(k), rhs(k), start=(k == 0), stop=(k == K - 1))
                w = (*after, *bk.read[b]) if k == 0 else ()
                if k < K - 1:
                    pe.quiet(f, *w)
                else:
                    tk = pe.op(f, *w)
            return b, tk

        bulk = []
        outs = []

        def fill(n=1):
            for _ in range(n):
                if bulk:
                    bulk.pop(0)()

        R1 = room(4096)
        R4 = room(5120)
        QT = R1[:, 0:3072].rearrange("p (m c) -> p m c", m=12)
        cb_ = R4[:, 0:4 * 259].rearrange("p (a c) -> p a c", a=4)
        cc_ = R4[:, 1100:1100 + 4 * 256].rearrange("p (a c) -> p a c", a=4)
        zz = pool.op(lambda e: e.memset(cb_[:, :, 0:3], 0.0), *moe_end)
        qt_ok = []
        cf = [[zz] for _ in range(4)]
        for m in range(12):
            if m % 2 == 0:
                sl = Slot(t["w2_dn"][m // 2])
            v = sl.v.rearrange("p (k c) -> p k c", k=8)
            o_ = (m % 2) * 128
            b, tk = tile_T(sl, 0, 8, lambda k, v=v, o_=o_: v[:, k, o_:o_ + 128], lambda k: hT[:, k, :], 256, sl.tok, *hT_ok)
            if m % 2 == 1:
                sl.done(tk)
            j = m % 4
            a = act.op(lambda e, b=b, j=j: e.copy(cb_[:, j, 3:259], PS[:, b, 0:256]), tk, *cf[j])
            bk.read[b] = [a]
            cw = lambda k, m=m: VW[:, W_CONV + 4 * m + k:W_CONV + 4 * m + k + 1]
            a = dve.op(lambda e, j=j, cw=cw: e.tensor_scalar(cc_[:, j, :], cb_[:, j, 0:256], cw(0), None, ALU.mult), a, Lk2, *cf[j])
            for k in range(1, 4):
                a = dve.op(lambda e, j=j, k=k, cw=cw: e.scalar_tensor_tensor(
                    cc_[:, j, :], cb_[:, j, k:k + 256], cw(k), cc_[:, j, :], ALU.mult, ALU.add), a)
            a = act.op(lambda e, j=j, m=m: e.activation(QT[:, m, :], cc_[:, j, :], ACT.Silu), a)
            cf[j] = [a]
            qt_ok.append(a)

        def natural(name, i, ti, evac):
            if ti == 0:
                nat[(name, i)] = (Slot(t[name][2 * i]), Slot(t[name][2 * i + 1]))
            s0, s1 = nat[(name, i)]
            b = bk.take()
            for k in range(8):
                s = (s0, s1)[k // 4]
                f = lambda e, k=k, s=s: e.matmul(
                    PS[:, b, :], hT[:, k, ti * 128:ti * 128 + 128], s.v[:, (k % 4) * 512:(k % 4) * 512 + 512],
                    start=(k == 0), stop=(k == 7))
                w = (s.tok, *hT_ok, *bk.read[b]) if k == 0 else (s.tok,)
                if k < 7:
                    pe.quiet(f, *w)
                else:
                    tk = pe.op(f, *w)
                if k == 3 and ti == 1:
                    pass
            if ti == 1:
                s0.done(tk)
                s1.done(tk)
            bk.read[b] = [evac(b, tk)]

        nat = {}
        MS = room(1024, 2)
        Z = room(1024, 2)
        ms_ok, z_ok = [None, None], [None, None]
        for ti in range(2):
            def ev(b, tk, ti=ti):
                ms_ok[ti] = act.op(lambda e: e.copy(MS[:, ti, :], PS[:, b, :]), tk, *moe_end)
                return ms_ok[ti]
            natural("w2_nat", 0, ti, ev)
        for ti in range(2):
            def ev(b, tk, ti=ti):
                z_ok[ti] = act.op(lambda e: e.activation(Z[:, ti, :], PS[:, b, :], ACT.Silu), tk, *moe_end)
                return z_ok[ti]
            natural("w2_nat", 1, ti, ev)

        SU = room(1024, 2)
        SV = room(1024, 2)
        F = room(3072, 2, 3)
        su_ok, sv_ok, f_ok = [None, None], [None, None], {}

        def plan(name, i, dst, keep, fn):
            for ti in range(2):
                def unit(ti=ti):
                    def ev(b, tk):
                        keep(ti, fn(dst(ti), b, tk))
                        return last_ev[0]
                    natural(name, i, ti, ev)
                bulk.append(unit)

        last_ev = [None]

        def by_act(func):
            def g(dst, b, tk):
                last_ev[0] = act.op(lambda e: e.activation(dst, PS[:, b, :], func), tk, *moe_end)
                return last_ev[0]
            return g

        def by_copy(dst, b, tk):
            last_ev[0] = act.op(lambda e: e.copy(dst, PS[:, b, :]), tk, *moe_end)
            return last_ev[0]

        plan("w2_nat", 2, lambda ti: SU[:, ti, :], lambda ti, r: su_ok.__setitem__(ti, r), by_act(ACT.Gelu_apprx_tanh))
        plan("w2_nat", 3, lambda ti: SV[:, ti, :], lambda ti, r: sv_ok.__setitem__(ti, r), by_act(ACT.Gelu_apprx_tanh))
        for q in range(3):
            plan("w2_nat", 4 + q, lambda ti, q=q: F[:, ti, q, :], lambda ti, r, q=q: f_ok.__setitem__((ti, q), r), by_copy)
        fill(4)

        spx = small(16).rearrange("p (t c) -> p t c", t=2)
        spa = small(16).rearrange("p (t c) -> p t c", t=2)
        g8 = small(8).rearrange("p (t c) -> p t c", t=2)
        lf = small(8).rearrange("p (t c) -> p t c", t=2)
        beta = small(8).rearrange("p (t c) -> p t c", t=2)
        ea = small(4)
        GC = small(40)
        eg = small(8)
        ed = small(8)
        egl = small(16)
        bg = small(8)
        a1 = dve.op(lambda e: e.tensor_tensor(spx[:, :, 0:4], MS[:, :, 448:452], bc(VW[:, W_DT:W_DT + 4], 1, 2), ALU.add), *ms_ok, Lk2)
        a = dve.op(lambda e: e.tensor_tensor(spx[:, :, 4:8], MS[:, :, 456:460], bc(VW[:, W_FB:W_FB + 4], 1, 2), ALU.add), *ms_ok)
        a2 = dve.op(lambda e: e.tensor_scalar(spx[:, :, 4:8], spx[:, :, 4:8], -1.0, None, ALU.mult), a)
        a = dve.op(lambda e: e.scalar_tensor_tensor(spa, spx, -1.0, spx, ALU.mult, ALU.max), a1, a2)
        a = act.op(lambda e: e.activation(spa, spa, ACT.Exp, scale=-1.0), a)
        b1 = act.op(lambda e: e.activation(beta, MS[:, :, 452:456], ACT.Exp, scale=-1.0), *ms_ok)
        b2 = act.op(lambda e: e.activation(ea, VW[:, W_ALOG:W_ALOG + 4], ACT.Exp), Lk2)
        a = dve.op(lambda e: e.tensor_scalar(spa, spa, 1.0, None, ALU.add), a)
        a = act.op(lambda e: e.activation(spa, spa, ACT.Ln), a)
        a = dve.op(lambda e: e.scalar_tensor_tensor(spa, spx, 0.0, spa, ALU.max, ALU.add), a)
        g_ok = dve.op(lambda e: e.scalar_tensor_tensor(g8, spa[:, :, 0:4], -1.0, bc(ea, 1, 2), ALU.mult, ALU.mult), a, b2)
        l_ok = dve.op(lambda e: e.tensor_scalar(lf, spa[:, :, 4:8], -1.0, None, ALU.mult), a)
        b1 = dve.op(lambda e: e.tensor_scalar(beta, beta, 1.0, None, ALU.add), b1)
        b_ok = dve.op(lambda e: e.reciprocal(beta, beta), b1)
        g8f, lff = g8.rearrange("p t c -> p (t c)"), lf.rearrange("p t c -> p (t c)")
        tri = KT[:, K_TRI:K_TRI + 128]
        tric = KT[:, K_TRIC:K_TRIC + 128]
        one = KT[:, K_ONE:K_ONE + 128]
        b = bk.take()
        for n_, (c0, lhs, rhs, first, last) in enumerate([
                (0, tric, g8f, True, True), (8, KT[:, K_BLK:K_BLK + 128], g8f, True, True),
                (16, KT[:, K_SEL:K_SEL + 128], g8f, True, True), (24, KT[:, K_SEL + 128:K_SEL + 256], g8f, True, True),
                (32, tri, lf[:, 0, :], True, True), (36, one, lf[:, 0, :], True, False), (36, tri, lf[:, 1, :], False, True)]):
            w = rhs.free_size()
            f = lambda e, b=b, c0=c0, lhs=lhs, rhs=rhs, first=first, last=last, w=w: e.matmul(
                PS[:, b, c0:c0 + w], lhs, rhs, start=first, stop=last)
            if n_ < 6:
                pe.quiet(f, *((g_ok, l_ok, *bk.read[b]) if n_ == 0 else ()))
            else:
                tk = pe.op(f)
        gc_ok = dve.op(lambda e, b=b: e.tensor_copy(GC, PS[:, b, 0:40]), tk)
        bk.read[b] = [gc_ok]
        e1 = act.op(lambda e: e.activation(eg, GC[:, 0:8], ACT.Exp), gc_ok)
        a = dve.op(lambda e: e.tensor_tensor(ed, GC[:, 8:16], GC[:, 0:8], ALU.subtract), gc_ok)
        e2 = act.op(lambda e: e.activation(ed, ed, ACT.Exp), a)
        e3 = act.op(lambda e: e.activation(egl, GC[:, 16:32], ACT.Exp), gc_ok)
        bg_ok = dve.op(lambda e: e.tensor_tensor(bg, beta.rearrange("p t c -> p (t c)"), eg, ALU.mult), e1, b_ok)
        DT = room(1024, 8)
        RB = R4[:, 2200:3224].rearrange("p (r i) -> p r i", r=8)
        a = dve.op(lambda e: e.tensor_tensor(RB, bc(tric, 1, 8), bc(g8f, 2, 128), ALU.mult), g_ok, *moe_end)
        d_ok = []
        for q in range(2):
            b = bk.take()
            tk = pe.op(lambda e, b=b, q=q: e.matmul(PS[:, b, :], one, R4[:, 2200 + 512 * q:2712 + 512 * q], start=True, stop=True), a, *bk.read[b])
            for r in range(4):
                x = dve.op(lambda e, b=b, q=q, r=r: e.tensor_scalar(
                    DT[:, 4 * q + r, :], PS[:, b, r * 128:r * 128 + 128], GC[:, 4 * q + r:4 * q + r + 1], 0.0, ALU.subtract, ALU.min), tk, gc_ok)
            bk.read[b] = [x]
            d_ok.append(act.op(lambda e, q=q: e.activation(DT[:, 4 * q:4 * q + 4, :], DT[:, 4 * q:4 * q + 4, :], ACT.Exp), x))
        dt_ok = dve.op(lambda e: e.tensor_tensor(DT, DT, bc(tric, 1, 8), ALU.mult), *d_ok)
        fill(1)

        SQ = room(1024)
        sq_free = [[]]

        def sums(src, G, W, *after):
            c = small(G)
            s3 = SQ[:, 0:G * W].rearrange("p (g w) -> p g w", g=G)
            a = pool.op(lambda e: e.tensor_tensor(s3, src, src, ALU.mult), *after, *sq_free[0])
            b = dve.op(lambda e: e.tensor_reduce(c, s3, AX, ALU.add), a)
            sq_free[0] = [b]
            return c, b

        def power(c, G, mean, *after):
            a = dve.op(lambda e: e.tensor_scalar(c, c, mean, EPS, ALU.mult, ALU.add), *after)
            return pool.op(lambda e: e.tensor_tensor(c, c, mhalf[:, 0:G], ALU.pow), a)

        def scale(dst, src, c, W, *after):
            return dve.op(lambda e: e.tensor_tensor(dst, src, bc(c, 2, W), ALU.mult), *after)

        def turn4(srcs, dsts, after, gcol=None, rows=128, eng=None):
            b = bk.take()
            G = len(srcs)
            for i, s_ in enumerate(srcs):
                f = lambda e, i=i, s_=s_: e.transpose(PS[0:rows, b, i * 128:i * 128 + 128], s_, ident)
                if i < G - 1:
                    pe.quiet(f, *((*after, *bk.read[b]) if i == 0 else ()))
                else:
                    tk = pe.op(f, *((*after, *bk.read[b]) if i == 0 else ()))
            src = PS[0:rows, b, 0:G * 128].rearrange("p (g c) -> p g c", g=G)
            if gcol is not None:
                r = dve.op(lambda e: e.tensor_scalar(dsts, src, gcol, None, ALU.mult), tk)
            elif eng is dve:
                r = dve.op(lambda e: e.tensor_copy(dsts, src), tk)
            else:
                r = act.op(lambda e: e.copy(dsts, src), tk)
            bk.read[b] = [r]
            return r

        N = room(3072, 2, 12)
        n_ok = {}
        for ti in range(2):
            for q in range(3):
                n_ok[(ti, q)] = turn4([QT[:, 4 * q + h, ti * 128:ti * 128 + 128] for h in range(4)],
                                      N[:, ti, 4 * q:4 * q + 4, :], qt_ok + list(moe_end), eng=dve if q == 1 else None)
        KG = room(1024, 2, 4)
        KD = room(1024, 2, 4)
        QD = R4[:, 0:1024].rearrange("p (t h d) -> p t h d", t=2, h=4)
        KB = R4[:, 1024:2048].rearrange("p (t h d) -> p t h d", t=2, h=4)
        T4 = R1.rearrange("p (w h c) -> p w h c", w=4, h=4)
        t4_ok = []
        kd_ok, kg_ok, vb_ok = [], [], []
        conv_end = [qt_ok[-1], qt_ok[-2], qt_ok[-3], qt_ok[-4]]
        for ti in range(2):
            c, a = sums(N[:, ti, 0:8, :], 8, 128, n_ok[(ti, 0)], n_ok[(ti, 1)])
            r = power(c, 8, 1.0, a)
            qr = dve.op(lambda e, c=c: e.tensor_scalar(c[:, 0:4], c[:, 0:4], 128.0 ** -0.5, None, ALU.mult), r)
            s_ = slice(4 * ti, 4 * ti + 4)
            qn = scale(N[:, ti, 0:4, :], N[:, ti, 0:4, :], c[:, 0:4], 128, qr)
            kn = scale(N[:, ti, 4:8, :], N[:, ti, 4:8, :], c[:, 4:8], 128, r)
            kb = scale(KB[:, ti], N[:, ti, 4:8, :], beta[:, ti, :], 128, kn, b_ok, *conv_end, dt_ok)
            qd = scale(QD[:, ti], N[:, ti, 0:4, :], eg[:, s_], 128, qn, e1)
            vb_ok.append(scale(N[:, ti, 8:12, :], N[:, ti, 8:12, :], beta[:, ti, :], 128, n_ok[(ti, 2)], b_ok))
            kg_ok.append(scale(KG[:, ti], N[:, ti, 4:8, :], bg[:, s_], 128, kn, bg_ok))
            kd_ok.append(scale(KD[:, ti], N[:, ti, 4:8, :], ed[:, s_], 128, kn, e2))
            fill(1)
            turned = list(n_ok.values())
            for w, (src, a) in enumerate(((N[:, ti, 0:4], qn), (N[:, ti, 4:8], kn), (KB[:, ti], kb), (QD[:, ti], qd))):
                t4_ok.append(turn4([src[:, h, :] for h in range(4)], T4[:, w, :, ti * 128:ti * 128 + 128], [a] + turned,
                                   eng=dve if w % 2 else None))
        LT = room(1024, 8)
        QK = room(1024, 8)
        lt_ok, qk_ok = [], []
        for w, dst, ok in ((2, LT, lt_ok), (0, QK, qk_ok)):
            for ti in range(2):
                b = bk.take()
                for h in range(4):
                    f = lambda e, b=b, h=h, ti=ti, w=w: e.matmul(
                        PS[:, b, h * 128:h * 128 + 128], T4[:, 1, h, ti * 128:ti * 128 + 128],
                        T4[:, w, h, ti * 128:ti * 128 + 128], start=True, stop=True)
                    if h < 3:
                        pe.quiet(f, *((*t4_ok, *bk.read[b]) if h == 0 else ()))
                    else:
                        tk = pe.op(f)
                r = dve.op(lambda e, b=b, dst=dst, ti=ti: e.tensor_tensor(
                    dst[:, 4 * ti:4 * ti + 4, :], PS[:, b, :].rearrange("p (h c) -> p h c", h=4),
                    DT[:, 4 * ti:4 * ti + 4, :], ALU.mult), tk, dt_ok)
                bk.read[b] = [r]
                ok.append(r)

        X, XT, T1, M0, M1 = (R4[:, 1024 * q:1024 * q + 1024].rearrange("p (r c) -> p r c", r=8) for q in range(5))
        r4_free = [t4_ok[-1], t4_ok[-2], t4_ok[-3], t4_ok[-4], t4_ok[2], t4_ok[3]]
        id8 = bc(ident, 1, 8)

        def level_mask(n, dst, *after):
            return pool.op(lambda e: e.tensor_tensor(dst, LT, bc(KT[:, K_LEV + 128 * n:K_LEV + 128 * n + 128], 1, 8), ALU.mult), *after)

        m_ok = level_mask(0, M0, *lt_ok, *r4_free)
        m_next = level_mask(1, M1)
        xt_ok = [dve.op(lambda e: e.tensor_tensor(XT, id8, M0, ALU.subtract), m_ok, *r4_free)]
        x_ok = []
        for q in range(2):
            b = bk.take()
            for r in range(4):
                f = lambda e, b=b, r=r, q=q: e.transpose(PS[:, b, r * 128:r * 128 + 128], M0[:, 4 * q + r, :], ident)
                if r < 3:
                    pe.quiet(f, *((m_ok, *bk.read[b]) if r == 0 else ()))
                else:
                    tk = pe.op(f)
            x = dve.op(lambda e, b=b, q=q: e.tensor_tensor(
                X[:, 4 * q:4 * q + 4, :], bc(ident, 1, 4), PS[:, b, :].rearrange("p (r c) -> p r c", r=4), ALU.subtract), tk, *r4_free)
            bk.read[b] = [x]
            x_ok.append(x)

        def eight(lhs, rhs, *after):
            out = []
            for q in range(2):
                b = bk.take()
                for r in range(4):
                    f = lambda e, b=b, r=r, q=q: e.matmul(PS[:, b, r * 128:r * 128 + 128], lhs(4 * q + r), rhs(4 * q + r), start=True, stop=True)
                    if r < 3:
                        pe.quiet(f, *((*after, *bk.read[b]) if r == 0 else ()))
                    else:
                        tk = pe.op(f)
                out.append((b, tk))
            return out

        mt = [tk]
        for n in range(1, 6):
            M = (M0, M1)[n % 2]
            fill(1)
            out = eight(lambda r, M=M: M[:, r, :], lambda r: X[:, r, :], m_next, *x_ok)
            t1_ok = []
            for q, (b, tk) in enumerate(out):
                dst = T1[:, 4 * q:4 * q + 4, :]
                src = PS[:, b, :].rearrange("p (r c) -> p r c", r=4)
                if q == 0:
                    r = act.op(lambda e, dst=dst, src=src: e.copy(dst, src), tk, *mt, *r4_free)
                else:
                    r = dve.op(lambda e, dst=dst, src=src: e.tensor_copy(dst, src), tk, *mt)
                bk.read[b] = [r]
                t1_ok.append(r)
            if n < 5:
                m_next = level_mask(n + 1, (M1, M0)[n % 2], tk, *mt)
            fill(1)
            outT = eight(lambda r: T1[:, r, :], lambda r: XT[:, r, :], *t1_ok, *xt_ok)
            new_x = []
            if n < 5:
                outX = eight(lambda r: XT[:, r, :], lambda r: T1[:, r, :])
                for q, (b, tk) in enumerate(outX):
                    v = X[:, 4 * q:4 * q + 4, :]
                    r = dve.op(lambda e, v=v, b=b: e.tensor_tensor(v, v, PS[:, b, :].rearrange("p (r c) -> p r c", r=4), ALU.subtract), tk)
                    bk.read[b] = [r]
                    new_x.append(r)
                mt = [tk]
            last = outX[1][1] if n < 5 else outT[1][1]
            new_t = []
            for q, (b, tk) in enumerate(outT):
                v = XT[:, 4 * q:4 * q + 4, :]
                r = dve.op(lambda e, v=v, b=b: e.tensor_tensor(v, v, PS[:, b, :].rearrange("p (r c) -> p r c", r=4), ALU.subtract), tk, last)
                bk.read[b] = [r]
                new_t.append(r)
            x_ok, xt_ok = new_x, new_t

        U = M0
        WT = M1
        inv_end = [new_t[0], new_t[1], last]
        out = eight(lambda r: XT[:, r, :], lambda r: N[:, r // 4, 8 + r % 4, :], *xt_ok, *vb_ok)
        u_ok, w_ok = [], []
        for q, (b, tk) in enumerate(out):
            r = act.op(lambda e, b=b, q=q: e.copy(U[:, 4 * q:4 * q + 4, :], PS[:, b, :].rearrange("p (r c) -> p r c", r=4)), tk, *inv_end)
            bk.read[b] = [r]
            u_ok.append(r)
        out = eight(lambda r: KG[:, r // 4, r % 4, :], lambda r: XT[:, r, :], *kg_ok)
        for q, (b, tk) in enumerate(out):
            r = dve.op(lambda e, b=b, q=q: e.tensor_copy(WT[:, 4 * q:4 * q + 4, :], PS[:, b, :].rearrange("p (r c) -> p r c", r=4)), tk, *inv_end)
            bk.read[b] = [r]
            w_ok.append(r)
        uw_end = tk

        ST = R4[:, 0:512].rearrange("p (h d) -> p h d", h=4)
        SD = R4[:, 512:1024].rearrange("p (h d) -> p h d", h=4)
        VN = R4[:, 2048:2560].rearrange("p (h d) -> p h d", h=4)
        ON = KG
        s_t = dve.op(lambda e: e.memset(ST, 0.0), *inv_end)
        on_ok = [[], []]
        vn_free = []
        oq_free = [uw_end]
        for c in range(4):
            ti, r0 = c // 2, 64 * (c % 2)
            rows = slice(r0, r0 + 64)
            b = bk.take()
            for h in range(4):
                f = lambda e, b=b, h=h, ti=ti, rows=rows, r0=r0: e.matmul(
                    PS[rows, b, h * 128:h * 128 + 128], WT[:, 4 * ti + h, r0:r0 + 64], ST[:, h, :], start=True, stop=True)
                if h < 3:
                    pe.quiet(f, *((s_t, *w_ok, *bk.read[b]) if h == 0 else ()))
                else:
                    tk = pe.op(f)
            vn = dve.op(lambda e, b=b, ti=ti, rows=rows: e.tensor_tensor(
                VN[rows], U[rows, 4 * ti:4 * ti + 4, :], PS[rows, b, :].rearrange("p (h d) -> p h d", h=4), ALU.subtract),
                tk, *u_ok, *vn_free, *inv_end)
            bk.read[b] = [vn]
            ob_ = bk.take()
            sb_ = bk.take()
            if c < 3:
                sd = dve.op(lambda e, c=c, ti=ti: e.tensor_tensor(
                    SD, ST, bc(egl[:, 8 * (c % 2) + 4 * ti:8 * (c % 2) + 4 * ti + 4], 2, 128), ALU.mult), s_t, e3, *inv_end)
                for h in range(4):
                    f = lambda e, h=h, ti=ti, rows=rows, sb_=sb_: e.matmul(
                        PS[:, sb_, h * 128:h * 128 + 128], KD[rows, ti, h, :], VN[rows, h, :], start=True, stop=True)
                    if h < 3:
                        pe.quiet(f, *((vn, *kd_ok, *bk.read[sb_]) if h == 0 else ()))
                    else:
                        tk = pe.op(f)
            for h in range(4):
                pe.quiet(lambda e, h=h, ti=ti, r0=r0, rows=rows, ob_=ob_: e.matmul(
                    PS[rows, ob_, h * 128:h * 128 + 128], T4[:, 3, h, ti * 128 + r0:ti * 128 + r0 + 64], ST[:, h, :],
                    start=True, stop=False), *((vn, s_t, *bk.read[ob_]) if h == 0 else ()))
                f = lambda e, h=h, ti=ti, r0=r0, rows=rows, ob_=ob_: e.matmul(
                    PS[rows, ob_, h * 128:h * 128 + 128], QK[rows, 4 * ti + h, r0:r0 + 64], VN[rows, h, :],
                    start=False, stop=True)
                if h < 3:
                    pe.quiet(f, *qk_ok)
                else:
                    tko = pe.op(f)
            vn_free = [tko]
            if c < 3:
                s_t = dve.op(lambda e, sb_=sb_: e.tensor_tensor(
                    ST, SD, PS[:, sb_, :].rearrange("p (h d) -> p h d", h=4), ALU.add), tk, sd, tko)
                bk.read[sb_] = [s_t]
            r = act.op(lambda e, ti=ti, rows=rows, ob_=ob_: e.copy(
                ON[rows, ti, :, :], PS[rows, ob_, :].rearrange("p (h d) -> p h d", h=4)), tko, *oq_free)
            bk.read[ob_] = [r]
            on_ok[ti].append(r)
            fill(1)
        BT = room(4096, 4, 4)
        bt_ok = {}
        dn_end = []
        for ti in range(2):
            c, a = sums(ON[:, ti], 4, 128, *on_ok[ti])
            r = power(c, 4, 1.0 / 128, a)
            a = scale(ON[:, ti], ON[:, ti], c, 128, r)
            a = dve.op(lambda e, ti=ti: e.tensor_tensor(ON[:, ti], ON[:, ti], Z[:, ti, :].rearrange("p (h d) -> p h d", h=4), ALU.mult), a, z_ok[ti])
            fill(1)
            bt_ok[(0, ti)] = turn4([ON[:, ti, h, :] for h in range(4)], BT[:, 0, :, ti * 128:ti * 128 + 128], [a], VW[:, W_OUTG:W_OUTG + 1])
            dn_end.append(bt_ok[(0, ti)])
        while bulk:
            fill(1)
        dn_end += [(pe.sem, pe.n), (dve.sem, dve.n), (act.sem, act.n), (pool.sem, pool.n)]

        GA_ = R4[:, 0:4096].rearrange("p (i m c) -> p i m c", i=2, m=8)
        GB_ = R1.rearrange("p (i m c) -> p i m c", i=2, m=8)
        gate_ok = {}
        gs = {}

        def gate_unit(n):
            def unit():
                if n % 2 == 0:
                    gs["sl"] = Slot(t["w2_gate"][n // 2])
                sl = gs["sl"]
                v = sl.v.rearrange("p (k c) -> p k c", k=8)
                o_ = (n % 2) * 128
                b, tk = tile_T(sl, 0, 8, lambda k: v[:, k, o_:o_ + 128], lambda k: hT[:, k, :], 256, sl.tok)
                if n % 2 == 1:
                    sl.done(tk)
                i, m = divmod(n, 8)
                g_ = (GA_ if i < 2 else GB_)[:, i % 2, m, :]
                a = act.op(lambda e: e.activation(g_, PS[:, b, 0:256], ACT.Exp, scale=-1.0), tk, *dn_end)
                bk.read[b] = [a]
                a = dve.op(lambda e: e.tensor_scalar(g_, g_, 1.0, None, ALU.add), a)
                gate_ok[n] = dve.op(lambda e: e.reciprocal(g_, g_), a)
            return unit

        for n in range(32):
            bulk.append(gate_unit(n))

        FT = XB.rearrange("p t c -> p (t c)").rearrange("p (q h c) -> p q h c", q=2, h=4)
        ft_ok = []
        for ti in range(2):
            c, a = sums(F[:, ti, 0:2, :].rearrange("p q (h d) -> p (q h) d", h=4), 8, 128, f_ok[(ti, 0)], f_ok[(ti, 1)])
            r = power(c, 8, 1.0 / 128, a)
            a = scale(F[:, ti, 0:2, :].rearrange("p q (h d) -> p (q h) d", h=4),
                      F[:, ti, 0:2, :].rearrange("p q (h d) -> p (q h) d", h=4), c, 128, r)
            fill(1)
            for q in range(2):
                ft_ok.append(turn4([F[:, ti, q, 128 * h:128 * h + 128] for h in range(4)],
                                   FT[:, q, :, ti * 128:ti * 128 + 128], [a], VW[:, W_FQ + q:W_FQ + q + 1]))

        SW = room(512, 4)
        c_sw = [sem("c_sw"), 0]
        Lsw = pool.dma(lambda e: e.dma_start(SW, t["sgw"]), c_sw, *moe_end)
        sw_ok = dve.op(lambda e: e.tensor_tensor(SW, SW, bc(tri, 1, 4), ALU.mult), Lsw)
        for ti in range(2):
            v4 = SV[:, ti, :].rearrange("p (g d) -> p g d", g=4)
            c, a = sums(v4, 4, 128, sv_ok[ti])
            r = power(c, 4, 1.0 / 128, a)
            a = scale(v4, v4, c, 128, r)
            a = dve.op(lambda e, ti=ti: e.tensor_tensor(SV[:, ti, :], SV[:, ti, :], VW[:, W_SGG:W_SGG + 512], ALU.mult), a)
            b = bk.take()
            for g in range(4):
                f = lambda e, b=b, g=g, ti=ti: e.matmul(
                    PS[:, b, g * 128:g * 128 + 128], SW[:, g, :], SV[:, ti, g * 128:g * 128 + 128], start=True, stop=True)
                if g < 3:
                    pe.quiet(f, *((a, sw_ok, *bk.read[b]) if g == 0 else ()))
                else:
                    tk = pe.op(f)
            for g in range(4):
                u = SU[:, ti, g * 128:g * 128 + 128]
                r = dve.op(lambda e, b=b, g=g, u=u: e.scalar_tensor_tensor(
                    u, PS[:, b, g * 128:g * 128 + 128], VW[:, W_SGB + g:W_SGB + g + 1], u, ALU.add, ALU.mult), tk, su_ok[ti])
            bk.read[b] = [r]
            bt_ok[(2, ti)] = turn4([SU[:, ti, g * 128:g * 128 + 128] for g in range(4)], BT[:, 2, :, ti * 128:ti * 128 + 128], [r])

        CT = R4[:, 4096:4864].rearrange("p (c k) -> p c k", c=3)
        Nf = N.rearrange("p t m c -> p (t m c)")
        MQ = Nf[:, 0:1536].rearrange("p (t h d) -> p t h d", t=2, h=4)
        MK = Nf[:, 1536:2560].rearrange("p (t h d) -> p t h d", t=2, h=4)
        MR = Nf[:, 2560:3072].rearrange("p (t h d) -> p t h d", t=2, h=4)
        MV = KG
        Q1, Q2, K1, K2 = KD.rearrange("p t h d -> p (t h d)").rearrange("p (h c) -> p h c", h=4), *(
            x.rearrange("p r c -> p (r c)").rearrange("p (h c) -> p h c", h=4) for x in (DT, LT, QK))
        RT = room(512)
        ct_ok = []
        for ti in range(2):
            cq, ckv = MS[:, ti, 0:256], MS[:, ti, 256:384]
            c1, a1 = sums(MS[:, ti, 0:256].unsqueeze(1), 1, 256, ms_ok[ti])
            c2, a2 = sums(MS[:, ti, 256:384].unsqueeze(1), 1, 128, ms_ok[ti])
            r1 = power(c1, 1, 1.0 / 256, a1)
            r2 = power(c2, 1, 1.0 / 128, a2)
            a1 = dve.op(lambda e, cq=cq, c1=c1: e.tensor_scalar(cq, cq, c1, None, ALU.mult), r1)
            a2 = dve.op(lambda e, ckv=ckv, c2=c2: e.tensor_scalar(ckv, ckv, c2, None, ALU.mult), r2)
            b = bk.take()
            for i in range(3):
                f = lambda e, b=b, i=i, ti=ti: e.transpose(PS[:, b, i * 128:i * 128 + 128], MS[:, ti, i * 128:i * 128 + 128], ident)
                if i < 2:
                    pe.quiet(f, *((a1, a2, *bk.read[b]) if i == 0 else ()))
                else:
                    tk = pe.op(f)
            for i in range(3):
                r = dve.op(lambda e, b=b, i=i, ti=ti: e.tensor_scalar(
                    CT[:, i, ti * 128:ti * 128 + 128], PS[:, b, i * 128:i * 128 + 128], VW[:, W_QN + i:W_QN + i + 1], None, ALU.mult), tk, *dn_end)
            bk.read[b] = [r]
            ct_ok.append(r)
        s_uq, s_kv = Slot(t["w2_uq"]), Slot(t["w2_ukv"])
        vq = s_uq.v[:, 0:1536].rearrange("p (k n) -> p k n", k=2)
        vkv = s_kv.v[:, 0:1024]
        mq_ok, mk_ok, mv_ok = {}, {}, {}
        for ti in range(2):
            for nb in range(2):
                b, tk = tile_T(None, 0, 2, lambda k, ti=ti: CT[:, k, ti * 128:ti * 128 + 128],
                               lambda k, nb=nb: vq[:, k, 384 * nb:384 * nb + 384], 384, s_uq.tok, *ct_ok)
                r = act.op(lambda e, b=b, ti=ti, nb=nb: e.copy(
                    MQ[:, ti, 2 * nb:2 * nb + 2, :], PS[:, b, 0:384].rearrange("p (h d) -> p h d", h=2)), tk, *dn_end)
                bk.read[b] = [r]
                mq_ok[(ti, nb)] = r
        s_uq.done(tk)
        for ti in range(2):
            for nb in range(2):
                b, tk = tile_T(None, 0, 1, lambda k, ti=ti: CT[:, 2, ti * 128:ti * 128 + 128],
                               lambda k, nb=nb: vkv[:, 512 * nb:512 * nb + 512], 512, s_kv.tok)
                src = PS[:, b, :].rearrange("p (h d) -> p h d", h=2)
                r = act.op(lambda e, src=src, ti=ti, nb=nb: e.copy(MK[:, ti, 2 * nb:2 * nb + 2, :], src[:, :, 0:128]), tk, *dn_end)
                r2 = act.op(lambda e, src=src, ti=ti, nb=nb: e.copy(MV[:, ti, 2 * nb:2 * nb + 2, :], src[:, :, 128:256]), tk, *dn_end)
                bk.read[b] = [r2]
                mk_ok[(ti, nb)] = r
                mv_ok[(ti, nb)] = r2
        s_kv.done(tk)
        gq, gk = VW[:, W_QG:W_QG + 192], VW[:, W_KG:W_KG + 192]
        rt_free = [[]]

        def rope_nat(x, ti, *after):
            w = [RT[:, 128 * i:128 * i + 128].rearrange("p (h d) -> p h d", h=4) for i in range(4)]
            cs, sn = bc(cosN[:, ti, :], 1, 4), bc(sinN[:, ti, :], 1, 4)
            x1, x2 = x[:, :, 0:32], x[:, :, 32:64]
            p = []
            for i, (a_, b_) in enumerate(((x1, cs), (x2, sn), (x2, cs), (x1, sn))):
                p.append(dve.op(lambda e, i=i, a_=a_, b_=b_: e.tensor_tensor(w[i], a_, b_, ALU.mult), k_tab, *after, *rt_free[0]))
            a = dve.op(lambda e: e.tensor_tensor(x1, w[0], w[1], ALU.subtract), *p)
            b = dve.op(lambda e: e.tensor_tensor(x2, w[2], w[3], ALU.add), *p)
            rt_free[0] = [b]
            return [a, b]

        qk2_ok = []
        for ti in range(2):
            c, a = sums(MQ[:, ti], 4, 192, mq_ok[(ti, 0)], mq_ok[(ti, 1)])
            r = power(c, 4, 1.0 / 192, a)
            a = scale(MQ[:, ti], MQ[:, ti], c, 192, r)
            a = dve.op(lambda e, ti=ti: e.tensor_tensor(MQ[:, ti], MQ[:, ti], bc(gq, 1, 4), ALU.mult), a)
            rp = rope_nat(MQ[:, ti, :, 128:192], ti, a)
            fill(1)
            tsl = slice(ti * 128, ti * 128 + 128)
            qk2_ok.append(turn4([MQ[:, ti, h, 0:128] for h in range(4)], Q1[:, :, tsl], [a, *dn_end]))
            qk2_ok.append(turn4([MQ[:, ti, h, 128:192] for h in range(4)], Q2[0:64, :, tsl], rp, rows=64))
            kr = MS[:, ti, 384:448]
            c, a = sums(MK[:, ti], 4, 128, mk_ok[(ti, 0)], mk_ok[(ti, 1)])
            c2, a2 = sums(kr.unsqueeze(1), 1, 64, ms_ok[ti])
            a = dve.op(lambda e, c=c, c2=c2: e.tensor_scalar(c, c, c2, None, ALU.add), a, a2)
            r = power(c, 4, 1.0 / 192, a)
            a = scale(MK[:, ti], MK[:, ti], c, 128, r)
            a = dve.op(lambda e, ti=ti: e.tensor_tensor(MK[:, ti], MK[:, ti], bc(gk[:, 0:128], 1, 4), ALU.mult), a)
            b = dve.op(lambda e, ti=ti, c=c, kr=kr: e.tensor_tensor(MR[:, ti], bc(kr, 1, 4), bc(c, 2, 64), ALU.mult), r, *dn_end)
            b = dve.op(lambda e, ti=ti: e.tensor_tensor(MR[:, ti], MR[:, ti], bc(gk[:, 128:192], 1, 4), ALU.mult), b)
            rp = rope_nat(MR[:, ti], ti, b)
            fill(1)
            qk2_ok.append(turn4([MK[:, ti, h, :] for h in range(4)], K1[:, :, tsl], [a]))
            qk2_ok.append(turn4([MR[:, ti, h, :] for h in range(4)], K2[0:64, :, tsl], rp, rows=64))

        DM = Z.rearrange("p t c -> p (t c)").rearrange("p (j t c) -> p j t c", j=2, t=2)
        SC = room(512, 2)
        PT = room(512, 2)
        sr = small(8)
        FR = Nf[:, 0:1536]
        sc_free, pt_free = [[], []], [[], []]
        dm_ok, dm_free = {}, [[], []]
        MB = KT[:, K_MB:K_MB + 256]
        fr_free = [[]]

        def row_decay(h):
            j = h % 2
            R0 = RT[:, 0:256]
            R1_ = RT[:, 256:384]
            a = dve.op(lambda e: e.tensor_scalar(R0, KT[:, K_TRI:K_TRI + 256], lf[:, 0, h:h + 1], None, ALU.mult), l_ok, *fr_free[0], *rt_free[0])
            c = dve.op(lambda e: e.tensor_scalar(R1_, tri, lf[:, 1, h:h + 1], None, ALU.mult), l_ok, *fr_free[0], *rt_free[0])
            b = bk.take()
            pe.quiet(lambda e: e.matmul(PS[:, b, 0:256], one, R0, start=True, stop=False), a, c, *bk.read[b])
            tk = pe.op(lambda e: e.matmul(PS[:, b, 128:256], one, R1_, start=False, stop=True))
            fr_free[0] = [tk]
            r = []
            for ti in range(2):
                nk = 128 * ti + 128
                r.append(dve.op(lambda e, ti=ti, nk=nk: e.scalar_tensor_tensor(
                    DM[:, j, ti, 0:nk], PS[:, b, 0:nk], GC[:, 32 + 4 * ti + h:33 + 4 * ti + h], MB[:, 256 - nk:256],
                    ALU.subtract, ALU.subtract, reverse1=True), tk, gc_ok, *dm_free[j]))
            bk.read[b] = r
            dm_ok[h] = r

        def score(u):
            fox, h, ti = u
            nk = 128 * ti + 128
            j = cnt[0] % 2
            cnt[0] += 1
            q0 = slice(ti * 128, ti * 128 + 128)
            b = bk.take()
            if fox:
                if ti == 0:
                    row_decay(h)
                tk = pe.op(lambda e: e.matmul(PS[:, b, 0:nk], FT[:, 0, h, q0], FT[:, 1, h, 0:nk], start=True, stop=True), *ft_ok, *bk.read[b])
                bias, sc, w = DM[:, h % 2, ti, 0:nk], 128.0 ** -0.5, dm_ok[h]
            else:
                pe.quiet(lambda e: e.matmul(PS[:, b, 0:nk], Q1[:, h, q0], K1[:, h, 0:nk], start=True, stop=False), *qk2_ok, *bk.read[b])
                tk = pe.op(lambda e: e.matmul(PS[:, b, 0:nk], Q2[0:64, h, q0], K2[0:64, h, 0:nk], start=False, stop=True))
                bias, sc, w = MB[:, 256 - nk:256], 192.0 ** -0.5, []
            S_ = SC[:, j, 0:nk]
            m, l, rc = sr[:, 4 * j:4 * j + 1], sr[:, 4 * j + 1:4 * j + 2], sr[:, 4 * j + 2:4 * j + 3]
            a = dve.op(lambda e: e.scalar_tensor_tensor(S_, PS[:, b, 0:nk], sc, bias, ALU.mult, ALU.add), tk, *w, *sc_free[j])
            bk.read[b] = [a]
            if fox:
                dm_free[h % 2] = [a]
            a = dve.op(lambda e: e.tensor_reduce(m, S_, AX, ALU.max, negate=True), a)
            a = act.op(lambda e: e.activation(S_, S_, ACT.Exp, bias=m, scale=1.0, accum_out=l), a)
            a = dve.op(lambda e: e.reciprocal(rc, l), a)
            a = dve.op(lambda e: e.tensor_scalar(S_, S_, rc, None, ALU.mult), a)
            return (u, j, a)

        oacc = {}

        def value(state):
            (fox, h, ti), j, tok = state
            b = bk.take()
            for kt in range(ti + 1):
                f = lambda e, kt=kt: e.transpose(PS[:, b, kt * 128:kt * 128 + 128], SC[:, j, kt * 128:kt * 128 + 128], ident)
                w = (tok, *bk.read[b]) if kt == 0 else ()
                if kt < ti:
                    pe.quiet(f, *w)
                else:
                    tk = pe.op(f, *w)
            sc_free[j] = [tk]
            nk = 128 * ti + 128
            r = act.op(lambda e: e.copy(PT[:, j, 0:nk], PS[:, b, 0:nk]), tk, *pt_free[j])
            bk.read[b] = [r]
            b2 = bk.take()
            for kt in range(ti + 1):
                vv = F[:, kt, 2, 128 * h:128 * h + 128] if fox else MV[:, kt, h, :]
                f = lambda e, kt=kt, vv=vv: e.matmul(PS[:, b2, 0:128], vv, PT[:, j, kt * 128:kt * 128 + 128], start=(kt == 0), stop=(kt == ti))
                w = (r, *([f_ok[(0, 2)], f_ok[(1, 2)]] if fox else mv_ok.values()), *bk.read[b2]) if kt == 0 else ()
                if kt < ti:
                    pe.quiet(f, *w)
                else:
                    tk = pe.op(f, *w)
            pt_free[j] = [tk]
            br = 3 if fox else 1
            r = act.op(lambda e: e.copy(BT[:, br, h, ti * 128:ti * 128 + 128], PS[:, b2, 0:128]), tk)
            bk.read[b2] = [r]
            bt_ok[(br, h, ti)] = r

        cnt = [0]
        prev = None
        for u in [(True, h, ti) for h in range(4) for ti in range(2)] + [(False, h, ti) for h in range(4) for ti in range(2)]:
            st_ = score(u)
            fill(1)
            if prev is not None:
                value(prev)
            prev = st_
        fill(1)
        value(prev)
        while bulk:
            fill(1)

        MT = XB.rearrange("p t c -> p (t c)").rearrange("p (m c) -> p m c", m=8)
        TM = SC
        tm_free = [[sc_free[0][0]], [sc_free[1][0]]]
        mt_ok = []
        n = 0
        for m in range(8):
            sl = Slot(t["w2_br"][m])
            v = sl.v.rearrange("p (i k c) -> p i k c", i=4, k=4)
            a = None
            for i in range(4):
                b, tk = tile_T(sl, 0, 4, lambda k, v=v, i=i: v[:, i, k, :], lambda k, i=i: BT[:, i, k, :], 256, sl.tok, *bt_ok.values())
                g_ = (GA_ if i < 2 else GB_)[:, i % 2, m, :]
                if i == 0:
                    a = dve.op(lambda e, b=b, g_=g_, m=m: e.tensor_tensor(MT[:, m, :], PS[:, b, 0:256], g_, ALU.mult), tk, gate_ok[i * 8 + m])
                    bk.read[b] = [a]
                else:
                    j = n % 2
                    n += 1
                    c = dve.op(lambda e, b=b, g_=g_, j=j: e.tensor_tensor(TM[:, j, :], PS[:, b, 0:256], g_, ALU.mult), tk, gate_ok[i * 8 + m], *tm_free[j])
                    bk.read[b] = [c]
                    a = dve.op(lambda e, m=m, j=j: e.tensor_tensor(MT[:, m, :], MT[:, m, :], TM[:, j, :], ALU.add), a, c)
                    tm_free[j] = [a]
            sl.done(tk)
            mt_ok.append(a)
        merge_end = [(dve.sem, dve.n), (pe.sem, pe.n), (act.sem, act.n), (pool.sem, pool.n)]

        so = [Slot(t["w2_out"][i]) for i in range(4)]
        h_ok = {}
        for ti in range(2):
            for db in range(2):
                b = bk.take()
                for c in range(8):
                    f = lambda e, c=c, b=b, ti=ti, db=db: e.matmul(
                        PS[:, b, :], MT[:, c, ti * 128:ti * 128 + 128],
                        so[c // 2].v[:, (c % 2) * 1024 + db * 512:(c % 2) * 1024 + db * 512 + 512], start=(c == 0), stop=(c == 7))
                    w = ((*bk.read[b],) if c == 0 else ()) + (so[c // 2].tok, mt_ok[c])
                    if c < 7:
                        pe.quiet(f, *w)
                    else:
                        tk = pe.op(f, *w)
                hv = H[:, ti, db * 512:db * 512 + 512]
                h_ok[(ti, db)] = dve.op(lambda e, hv=hv, b=b: e.tensor_tensor(hv, hv, PS[:, b, :], ALU.add), tk)
                bk.read[b] = [h_ok[(ti, db)]]
        for s_ in so:
            s_.done(tk)

        XB2 = Nf[:, 0:2048].rearrange("p (t c) -> p t c", t=2)
        h2_ok = []
        for ti in range(2):
            r, x = rms2(XB2, ti, 4 + ti, h_ok[(ti, 0)], h_ok[(ti, 1)], *merge_end)
            a = dve.op(lambda e, ti=ti, x=x: e.tensor_scalar(XB2[:, ti, :], H[:, ti, :], x, None, ALU.mult), r)
            h2_ok += turn_tile(XB2, ti, 128, 128 * ti, hT, [a, *merge_end], VW[:, W_N2:W_N2 + 8])
        FA = R4[:, 0:4096].rearrange("p (m c) -> p m c", m=16)
        FB_ = R1.rearrange("p (m c) -> p m c", m=16)
        ff_ok = []
        for m in range(32):
            if m % 2 == 0:
                sl = Slot(t["w2_ff1"][m // 2])
            v = sl.v.rearrange("p (k c) -> p k c", k=8)
            o_ = (m % 2) * 128
            b, tk = tile_T(sl, 0, 8, lambda k, v=v, o_=o_: v[:, k, o_:o_ + 128], lambda k: hT[:, k, :], 256, sl.tok, *h2_ok)
            if m % 2 == 1:
                sl.done(tk)
            d_ = (FA if m < 16 else FB_)[:, m % 16, :]
            a = act.op(lambda e, b=b, d_=d_: e.activation(d_, PS[:, b, 0:256], ACT.Relu), tk, *merge_end)
            bk.read[b] = [a]
            ff_ok.append(dve.op(lambda e, d_=d_: e.tensor_tensor(d_, d_, d_, ALU.mult), a))
        acc = [bk.take() for _ in range(4)]
        for m in range(32):
            if m % 2 == 0:
                sl = Slot(t["w2_ff2"][m // 2])
            hm = (FA if m < 16 else FB_)[:, m % 16, :]
            for ti in range(2):
                for db in range(2):
                    f = lambda e, m=m, ti=ti, db=db, hm=hm, sl=sl: e.matmul(
                        PS[:, acc[2 * ti + db], :], hm[:, ti * 128:ti * 128 + 128],
                        sl.v[:, (m % 2) * 1024 + db * 512:(m % 2) * 1024 + db * 512 + 512], start=(m == 0), stop=(m == 31))
                    w = (sl.tok, ff_ok[m], *(bk.read[acc[2 * ti + db]] if m == 0 else []))
                    if m == 31 or (m % 2 == 1 and ti == 1 and db == 1):
                        tk = pe.op(f, *w)
                        if m == 31:
                            hv = H[:, ti, db * 512:db * 512 + 512]
                            r = dve.op(lambda e, hv=hv, ti=ti, db=db: e.tensor_tensor(hv, hv, PS[:, acc[2 * ti + db], :], ALU.add), tk)
                            c_o = [sem(f"c_o{ti}{db}"), 0]
                            o = act.dma(lambda e, hv=hv, ti=ti, db=db: e.dma_start(
                                t["out"][:, ti, db * 512:db * 512 + 512], hv), c_o, r)
                            outs.append(o)
                    else:
                        pe.quiet(f, *w)
            if m % 2 == 1:
                sl.done(tk)
        act.quiet(None, *outs)

        for i, src in enumerate(stream):
            after = (used[before[i]],) if before[i] is not None else ()
            s = place[i]
            dst = ring[:, s * 2048:s * 2048 + 2048][:, 0:src.shape[1] if len(src.shape) == 2 else 2048]
            if len(src.shape) == 3:
                dst = dst.rearrange("p (a d) -> p a d", a=src.shape[1])
            sp.dma(lambda e, dst=dst, src=src: e.dma_start(dst, src), slot_sem[s], *after)

        block = ctx.enter_context(nc.Block())

        @block.sync
        def _(e):
            sp.emit(e)

        @block.scalar
        def _(e):
            act.emit(e)

        @block.vector
        def _(e):
            dve.emit(e)

        @block.gpsimd
        def _(e):
            pool.emit(e)

        @block.tensor
        def _(e):
            pe.emit(e)


def pack_T(w):
    K, N = w.shape
    return np.ascontiguousarray(w.reshape(K // 128, 128, N // 256, 256).transpose(2, 1, 0, 3)).reshape(N // 256, 128, -1)


def pack_N(w):
    K, N = w.shape
    a = w.reshape(K // 512, 4, 128, N // 512, 512).transpose(3, 0, 2, 1, 4)
    return np.ascontiguousarray(a).reshape(-1, 128, 2048)


def pack_R(w):
    K, N = w.shape
    return np.ascontiguousarray(w.reshape(K // 256, 2, 128, N).transpose(0, 2, 1, 3)).reshape(-1, 128, 2 * N)


def col(v):
    return np.ascontiguousarray(v.reshape(-1, 128).T)


def layout(i):
    a = {}
    a["x"] = np.ascontiguousarray(i["x"][0].reshape(2, 128, D).transpose(1, 0, 2))
    a["meta"] = np.ascontiguousarray(i["meta_tokens"])
    a["cst"] = constants()
    w = i["w_in"][0]
    order = [w[:, 512:1024], w[:, 0:512]]
    tri = [w[:, o + 128 * m:o + 128 * m + 128] for m in range(4) for o in (1536, 2560, 2048)]
    a["w_in"] = np.concatenate([pack_T(order[0]), pack_T(order[1]), pack_N(w[:, 1024:1536]), pack_T(np.concatenate(tri, 1))])
    a["w_out"] = pack_R(i["w_out"][0])
    for n in ("w_gate", "w_up", "w_down"):
        a[n] = np.ascontiguousarray(i[n][0])
    v = np.zeros((P, NVEC), np.float32)
    v[:, V_MIXG:V_MIXG + 8] = col(i["mix_norm_g"][0])
    cw = i["conv_w"][0]
    for m in range(4):
        for k in range(3):
            v[:, V_CONV + 3 * m + k] = cw[k, 128 * m:128 * m + 128]
    v[:, V_SUB] = i["attn_subln_g"][0]
    for j, n in enumerate(("lambda_q1", "lambda_k1", "lambda_q2", "lambda_k2")):
        v[:, V_LAM + 64 * j:V_LAM + 64 * j + 64] = i[n][0][None, :]
    v[:, V_WR:V_WR + 128] = i["w_router"][0].reshape(8, 128, 16).transpose(1, 0, 2).reshape(128, 128)
    a["vec"] = v
    g = np.zeros((2, P, D), np.float32)
    g[0] = i["ffn_norm_g"][0][None, :]
    g[1] = i["final_norm_g"][None, :]
    a["gbc"] = g
    a["pos"] = np.ascontiguousarray(i["positions_2"][0].reshape(2, 128).T)
    w = i["w_in_2"][0]
    q_, z_, a_, b_, cq, ckv, kr, su, sv, fq, ff, gt = np.split(
        w, np.cumsum([1536, 512, 4, 4, 256, 128, 64, 512, 512, 1536, 4])[:11], axis=1)
    a["w2_dn"] = pack_T(q_)
    misc = np.concatenate([cq, ckv, kr, a_, b_, ff, np.zeros((D, 52), np.float32)], 1)
    a["w2_nat"] = pack_N(np.concatenate([misc, z_, su, sv, fq], 1))
    a["w2_gate"] = pack_T(gt)
    u = i["mla_w_uq_2"][0]
    a["w2_uq"] = np.ascontiguousarray(u.reshape(2, 128, 768).transpose(1, 0, 2)).reshape(128, 1536)
    a["w2_ukv"] = np.ascontiguousarray(i["mla_w_ukv_2"][0])
    wb = i["w_branch_2"][0]
    a["w2_br"] = np.ascontiguousarray(wb.reshape(4, 4, 128, 8, 128).transpose(3, 2, 0, 1, 4)).reshape(8, 128, 2048)
    a["w2_out"] = pack_R(i["w_out_2"][0])
    a["w2_ff1"] = pack_T(i["w_ff1_2"][0])
    a["w2_ff2"] = pack_R(i["w_ff2_2"][0])
    a["sgw"] = np.ascontiguousarray(i["sg_w_s_2"][0].transpose(2, 0, 1))
    v = np.zeros((P, NW2), np.float32)
    v[:, W_N1:W_N1 + 8] = col(i["norm1_g_2"][0])
    v[:, W_CONV:W_CONV + 48] = i["dn_conv_w_2"][0].reshape(4, 12, 128).transpose(2, 1, 0).reshape(128, 48)
    v[:, W_DT:W_DT + 4] = i["dn_dt_bias_2"][0][None, :]
    v[:, W_ALOG:W_ALOG + 4] = i["dn_a_log_2"][0][None, :]
    v[:, W_OUTG] = i["dn_out_norm_g_2"][0]
    v[:, W_QN:W_QN + 2] = col(i["mla_q_norm_g_2"][0])
    v[:, W_KVN] = i["mla_kv_norm_g_2"][0]
    v[:, W_QG:W_QG + 192] = i["mla_qk_q_g_2"][0][None, :]
    v[:, W_KG:W_KG + 192] = i["mla_qk_k_g_2"][0][None, :]
    v[:, W_SGB:W_SGB + 4] = i["sg_b_s_2"][0].T
    v[:, W_FQ] = i["fox_q_norm_g_2"][0]
    v[:, W_FK] = i["fox_k_norm_g_2"][0]
    v[:, W_FB:W_FB + 4] = i["fox_f_bias_2"][0][None, :]
    v[:, W_N2:W_N2 + 8] = col(i["norm2_g_2"][0])
    v[:, W_SGG:W_SGG + 512] = i["sg_v_norm_g_2"][0].reshape(1, 512)
    a["kw2"] = np.concatenate([constants_2(), v], 1)
    return a


def kernel(**inputs):
    import concourse.bacc as bacc
    from concourse.bass_utils import run_bass_kernel_spmd

    arrays = layout({n: np.asarray(a) for n, a in inputs.items()})
    nc = bacc.Bacc("TRN2", target_bir_lowering=False, num_devices=1)
    t = {n: nc.dram_tensor(f"in_{n}", a.shape, mybir.dt.from_np(a.dtype), kind="ExternalInput").ap()
         for n, a in arrays.items()}
    t["out"] = nc.dram_tensor("out_y", (P, 2, D), F32, kind="ExternalOutput").ap()
    program(nc, t)
    r = run_bass_kernel_spmd(nc, [{f"in_{n}": a for n, a in arrays.items()}], core_ids=[0])
    y = r.results[0]["out_y"]
    return np.ascontiguousarray(y.transpose(1, 0, 2)).reshape(1, 256, D)
```

```python
from contextlib import ExitStack

import numpy as np
import concourse.bass as bass
from concourse import mybir

F32 = mybir.dt.float32
F32R = mybir.dt.float32r
I32 = mybir.dt.int32
ALU = mybir.AluOpType
ACT = mybir.ActivationFunctionType
AX = mybir.AxisListType.X

P = 128
D = 1024
L = 272
NM = 16
NE = 16
CAP = 34
EPS = 1e-6
RING = 12
AR = 22000
TT = [(16, 128), (144, 128), (0, 16)]

C_ID, C_ONE, C_ROT, C_COS, C_SIN, C_IOTA = 0, 128, 256, 384, 656, 928
NCST = 992
K_TRIC, K_TRI, K_ONE, K_BLK, K_SEL, K_LEV, K_MB, K_INV = 0, 128, 256, 384, 512, 768, 1536, 1792
NK2 = 1824
W_N1, W_CONV, W_DT, W_ALOG, W_OUTG, W_QN, W_KVN, W_QG, W_KG = 0, 8, 56, 60, 64, 65, 67, 68, 260
W_SGB, W_FQ, W_FK, W_FB, W_N2, W_SGG = 452, 456, 457, 458, 462, 470
NW2 = 982
RAW = 3
WR = 4
FIRST_ROOM = RING * 2048 + 14848
TWO_PI = 6.283185307179586
C1 = 6.28125
C2 = float(np.float32(0.0019350051879882812))
C3 = TWO_PI - C1 - C2
V_MIXG, V_CONV, V_SUB, V_LAM, V_WR = 0, 8, 20, 21, 277
V_N2 = 405
NVEC = 413
FILLS = (4, 2, 2, 1, 1, 1)


def constants():
    c = np.zeros((P, NCST), np.float32)
    c[:, C_ID:C_ID + 128] = np.eye(P)
    c[:, C_ONE:C_ONE + 128] = 1.0
    for m in range(P):
        if m % 64 < 32:
            c[m + 32, C_ROT + m] = -1.0
        else:
            c[m - 32, C_ROT + m] = 1.0
    inv = (np.float32(10000.0) ** (-np.arange(0, 64, 2, dtype=np.float32) / np.float32(64))).astype(np.float32)
    ang = np.arange(L, dtype=np.float32)[:, None] * inv[None, :]
    c[:, C_COS:C_COS + L] = np.tile(np.cos(ang).T, (4, 1))
    c[:, C_SIN:C_SIN + L] = np.tile(np.sin(ang).T, (4, 1))
    c[:, C_IOTA:C_IOTA + 64] = np.arange(64)[None, :]
    return c


def constants_2():
    k = np.zeros((P, NK2), np.float32)
    j, i = np.arange(P)[:, None], np.arange(P)[None, :]
    k[:, K_TRIC:K_TRIC + 128] = (j <= i) & (j // 64 == i // 64)
    k[:, K_TRI:K_TRI + 128] = j <= i
    k[:, K_ONE:K_ONE + 128] = 1.0
    k[:, K_BLK:K_BLK + 128] = j // 64 == i // 64
    k[:64, K_SEL:K_SEL + 128] = 1.0
    k[64:, K_SEL + 128:K_SEL + 256] = 1.0
    for n in range(6):
        s = 1 << n
        k[:, K_LEV + 128 * n:K_LEV + 128 * n + 128] = (i // s % 2 == 1) & (j // s == i // s - 1)
    k[:, K_MB + 128:K_MB + 256] = np.where(i <= j, 0.0, -1e30)
    k[:, K_INV:K_INV + 32] = (np.float32(10000.0) ** (-np.arange(0, 64, 2, dtype=np.float32) / np.float32(64)))[None, :]
    return k


class Queue:

    def __init__(self, sem, chained=False):
        self.sem, self.n, self.items, self.chained = sem, 0, [], chained

    def op(self, fn, *after):
        if self.chained and self.n:
            after += ((self.sem, self.n),)
        self.n += 1
        self.items.append((after, fn, self.sem, 1))
        return (self.sem, self.n)

    def quiet(self, fn, *after):
        self.items.append((after, fn, None, 0))

    def dma(self, fn, counter, *after):
        counter[1] += 16
        self.items.append((after, fn, counter[0], 16))
        return (counter[0], counter[1])

    def emit(self, eng):
        reached = {}
        for after, fn, sem, by in self.items:
            for s, v in after:
                if reached.get(s.name, 0) < v:
                    eng.wait_ge(s, v)
                    reached[s.name] = v
            ins = fn(eng) if fn is not None else None
            if sem is not None:
                ins.then_inc(sem, by)


class Banks:

    def __init__(self, ids):
        self.ids, self.at = list(ids), 0
        self.read = {b: [] for b in self.ids}

    def take(self):
        b = self.ids[self.at % len(self.ids)]
        self.at += 1
        return b


def bc(ap, axis, n):
    a = ap.unsqueeze(axis)
    shape = list(a.shape)
    shape[axis] = n
    return a.broadcast_to(shape)


def program(nc, t):
    ctx = ExitStack()
    with ctx:
        def sb(name, cols, dt=F32):
            return ctx.enter_context(nc.sbuf_tensor(f"sb_{name}", [P, cols], dt))

        def sem(name):
            return ctx.enter_context(nc.semaphore(name))

        pe, dve, act, sp = (Queue(sem(f"s_{n}")) for n in ("pe", "dve", "act", "sp"))
        pool = Queue(sem("s_pool"), chained=True)
        PS = ctx.enter_context(nc.psum_tensor("PS", [P, 8, 512], F32))

        cst = sb("cst", NCST)
        vec = sb("vec", NVEC)
        gbc = sb("gbc", 1024)
        Hx = sb("Hx", 3 * 1024)
        sm = sb("sm", 768)
        posi = ctx.enter_context(nc.sbuf_tensor("sb_posi", [P, 2], I32))
        tab = sb("tab", 128)
        invf = sb("invf", 32)
        first = ExitStack()

        def sb1(name, cols, dt=F32, of=first):
            return of.enter_context(nc.sbuf_tensor(f"sb_{name}", [P, cols], dt))

        ring = sb1("ring", RING * 2048)
        ar = sb1("ar", AR)

        H = Hx[:, :].rearrange("p (t d) -> p t d", t=3)
        ident = cst[:, C_ID:C_ID + 128]
        ones = cst[:, C_ONE:C_ONE + 128]
        nsm = [0]

        def small(n):
            nsm[0] += n
            assert nsm[0] <= 768
            return sm[:, nsm[0] - n:nsm[0]]

        at = [0]

        def take(n, *dims):
            at[0] += n
            assert at[0] <= AR, at[0]
            v = ar[:, at[0] - n:at[0]]
            if len(dims) == 1:
                v = v.rearrange("p (a b) -> p a b", a=dims[0])
            elif len(dims) == 2:
                v = v.rearrange("p (a b c) -> p a b c", a=dims[0], b=dims[1])
            return v

        slot_sem = [[sem(f"w{i}"), 0] for i in range(RING)]
        stream = []
        used = []

        place = []
        holder = [None] * RING
        turns = [0] * RING
        before = []

        def assign():
            i = len(place)
            s = i % RING
            place.append(s)
            before.append(holder[s])
            holder[s] = i
            turns[s] += 1
            return s, turns[s]

        def weights(fn):
            stream.append(fn)
            used.append(None)
            return len(stream) - 1

        class Slot:

            def __init__(self, src, shape=None):
                self.i = weights(src)
                s, turn_ = assign()
                self.v = ring[:, s * 2048:s * 2048 + 2048]
                self.tok = (slot_sem[s][0], 16 * turn_)

            def done(self, tok):
                used[self.i] = tok

        def packed(src, n):
            return [Slot(src[i]) for i in range(n)]

        c_x = [sem("c_x"), 0]
        c_cst = [sem("c_cst"), 0]
        c_vec = [sem("c_vec"), 0]
        c_g = [sem("c_g"), 0]
        Lx = act.dma(lambda e: e.dma_start(H[:, 0:2, :], t["x"]), c_x)
        Lm = act.dma(lambda e: e.dma_start(H[0:NM, 2, :], t["meta"]), c_x)
        Lc = act.dma(lambda e: e.dma_start(cst[:, :], t["cst"]), c_cst)
        Lv = act.dma(lambda e: e.dma_start(vec[:, :], t["vec"]), c_vec)
        Lg = act.dma(lambda e: e.dma_start(gbc[:, :], t["gbc"][0]), c_g)

        c_k2 = [sem("c_k2"), 0]
        cosN = tab[:, 0:64].rearrange("p (t c) -> p t c", t=2)
        sinN = tab[:, 64:128].rearrange("p (t c) -> p t c", t=2)
        Lp = sp.dma(lambda e: e.dma_start(posi[:, :], t["pos"]), c_k2)
        Lp = sp.dma(lambda e: e.dma_start(invf[:, :], t["kw2"][:, K_INV:K_INV + 32]), c_k2)
        posf = small(2)
        tr_ = small(64 * 3)
        ang, kk, rr = (tr_[:, 64 * q:64 * q + 64] for q in range(3))
        a = dve.op(lambda e: e.tensor_copy(posf, posi[:, :]), Lp)
        a = dve.op(lambda e: e.tensor_tensor(ang.rearrange("p (t c) -> p t c", t=2), bc(posf, 2, 32), bc(invf[:, :], 1, 2), ALU.mult), a)
        a = dve.op(lambda e: e.tensor_scalar(kk, ang, 1.0 / TWO_PI, 12582912.0, ALU.mult, ALU.add), a)
        a = dve.op(lambda e: e.tensor_scalar(kk, kk, -12582912.0, None, ALU.add), a)
        a = dve.op(lambda e: e.scalar_tensor_tensor(rr, kk, -C1, ang, ALU.mult, ALU.add), a)
        a = dve.op(lambda e: e.scalar_tensor_tensor(rr, kk, -C2, rr, ALU.mult, ALU.add), a)
        a = dve.op(lambda e: e.scalar_tensor_tensor(rr, kk, -C3, rr, ALU.mult, ALU.add), a)
        a = dve.op(lambda e: e.tensor_scalar(rr, rr, 3.1415925, -3.1415925, ALU.min, ALU.max), a)
        x = act.op(lambda e: e.activation(sinN.rearrange("p t c -> p (t c)"), rr, ACT.Sin), a)
        a = dve.op(lambda e: e.tensor_scalar(kk, rr, TWO_PI / 4, TWO_PI / 2, ALU.add, ALU.is_gt), a)
        a = dve.op(lambda e: e.scalar_tensor_tensor(kk, kk, -TWO_PI, rr, ALU.mult, ALU.add), a)
        a = dve.op(lambda e: e.tensor_scalar(kk, kk, TWO_PI / 4, 3.1415925, ALU.add, ALU.min), a)
        a = dve.op(lambda e: e.tensor_scalar(kk, kk, -3.1415925, None, ALU.max), a)
        k_tab = act.op(lambda e: e.activation(cosN.rearrange("p t c -> p (t c)"), kk, ACT.Sin), a)

        XN = take(3072, 3)
        hnT = take(8 * L, 8)
        junk = take(1024)
        ss = small(4)
        rs = small(4)
        mhalf = small(16)
        k_mh = dve.op(lambda e: e.memset(mhalf, -0.5))
        bk = Banks(range(8))

        def rms(src, n, sscol, rscol, inv_n, width_junk, *after):
            a = act.op(lambda e: e.activation(width_junk, src, ACT.Square, accum_out=sscol), *after)
            b = dve.op(lambda e: e.tensor_scalar(rscol, sscol, inv_n, EPS, ALU.mult, ALU.add), a)
            c = pool.op(lambda e: e.tensor_tensor(rscol, rscol, mhalf[0:n, 0:1], ALU.pow), b, k_mh)
            return a, c

        def turn(src, n, dst_fn, evac_fn, *after):
            pass

        def turn_tile(XN, ti, n, col0, dstT, after, gcol=None, eng=None):
            out = []
            for half in range(2):
                b = bk.take()
                rd = bk.read[b]
                for k in range(4):
                    c = half * 4 + k
                    f = lambda e, b=b, k=k, c=c: e.transpose(
                        PS[:, b, k * 128:k * 128 + n], XN[0:n, ti, c * 128:c * 128 + 128], ident[0:n, 0:n])
                    if k < 3:
                        pe.quiet(f, *(rd + after + [Lc] if k == 0 else []))
                    else:
                        tk = pe.op(f)
                src = PS[:, b, :].rearrange("p (k c) -> p k c", k=4)[:, :, 0:n]
                dst = dstT[:, half * 4:half * 4 + 4, col0:col0 + n]
                if gcol is not None:
                    r = dve.op(lambda e, s=src, d=dst, h=half: e.tensor_tensor(
                        d, s, bc(gcol[:, h * 4:h * 4 + 4], 2, n), ALU.mult), tk, Lv)
                elif half == 0:
                    r = act.op(lambda e, s=src, d=dst: e.copy(d, s), tk)
                else:
                    r = dve.op(lambda e, s=src, d=dst: e.tensor_copy(d, s), tk)
                bk.read[b] = [r]
                out.append(r)
            return out

        hn_ok = []
        xn_free = []
        jprev = ()
        for ti, (c0, n) in enumerate(TT):
            a, r = rms(H[0:n, ti, :], n, ss[0:n, ti:ti + 1], rs[0:n, ti:ti + 1], 1.0 / D, junk[0:n, :], Lx, Lm, *jprev)
            jprev = (a,)
            x = dve.op(lambda e, ti=ti, n=n: e.tensor_scalar(
                XN[0:n, ti, :], H[0:n, ti, :], rs[0:n, ti:ti + 1], None, ALU.mult), r)
            hn_ok += turn_tile(XN, ti, n, c0, hnT, [x], vec[:, V_MIXG:V_MIXG + 8])
        last_turn = (pe.sem, pe.n)

        def proj_T(sl, half, N, actT, *after):
            b = bk.take()
            for k in range(8):
                f = lambda e, k=k: e.matmul(PS[:, b, 0:N], sl.v.rearrange("p (k c) -> p k c", k=8)[
                    :, k, half * 128:half * 128 + 128], actT[:, k, 0:N], start=(k == 0), stop=(k == 7))
                w = (sl.tok, *bk.read[b], *after) if k == 0 else ()
                if k < 7:
                    pe.quiet(f, *w)
                else:
                    tk = pe.op(f, *w)
            if half == 1:
                sl.done(tk)
            return b, tk

        qraw = take(2 * L, 2)
        t1 = take(2 * L, 2)
        t2 = take(2 * L, 2)
        kT = take(4 * L, 4)
        qz = take(8 * L, 4, 2)
        z0 = pool.op(lambda e: e.memset(qz[64:128, :, 0, :], 0.0))
        z1 = pool.op(lambda e: e.memset(qz[0:64, :, 1, :], 0.0))
        cosT = cst[:, C_COS:C_COS + L]
        sinT = cst[:, C_SIN:C_SIN + L]
        rotm = cst[:, C_ROT:C_ROT + 128]
        kq_ok = []
        pend = []
        free_raw = [[], []]
        free_t = [[], []]

        def rope(j, which, h, raw_tok):
            b = bk.take()
            tk = pe.op(lambda e: e.matmul(PS[:, b, 0:L], rotm, qraw[:, j, :], start=True, stop=True),
                       raw_tok, *bk.read[b])
            a = pool.op(lambda e: e.tensor_tensor(t1[:, j, :], qraw[:, j, :], cosT, ALU.mult), raw_tok, Lc, *free_t[j])
            c = dve.op(lambda e: e.tensor_tensor(t2[:, j, :], PS[:, b, 0:L], sinT, ALU.mult), tk, *free_t[j])
            bk.read[b] = [c]
            free_raw[j] = [tk, a]
            if which == 0:
                r = [dve.op(lambda e: e.tensor_tensor(kT[:, h, :], t1[:, j, :], t2[:, j, :], ALU.add), a, c)]
            else:
                r = [dve.op(lambda e, i=i: e.tensor_tensor(
                    qz[64 * i:64 * i + 64, h, i, :], t1[64 * i:64 * i + 64, j, :],
                    t2[64 * i:64 * i + 64, j, :], ALU.add), a, c) for i in range(2)]
            free_t[j] = r
            kq_ok.extend(r)

        n = 0
        for which in range(2):
            for s2 in range(2):
                sl = Slot(t["w_in"][which * 2 + s2])
                for half in range(2):
                    j = n % 2
                    b, tk = proj_T(sl, half, L, hnT, *hn_ok)
                    r = act.op(lambda e, b=b, j=j: e.copy(qraw[:, j, :], PS[:, b, 0:L]), tk, *free_raw[j])
                    bk.read[b] = [r]
                    if pend:
                        rope(*pend.pop())
                    pend.append((j, which, s2 * 2 + half, r))
                    n += 1
        V = take(3 * 512, 3)
        sv = [Slot(t["w_in"][4]), Slot(t["w_in"][5])]
        v_ok = []
        for ti, (c0, n) in enumerate(TT):
            b = bk.take()
            for k in range(8):
                f = lambda e, k=k, b=b, c0=c0, n=n: e.matmul(
                    PS[0:n, b, :], hnT[:, k, c0:c0 + n], sv[k // 4].v[:, (k % 4) * 512:(k % 4) * 512 + 512],
                    start=(k == 0), stop=(k == 7))
                w = (sv[0].tok, *bk.read[b]) if k == 0 else (sv[1].tok,) if k == 4 else ()
                if k == 7:
                    tk = pe.op(f, *w)
                else:
                    pe.quiet(f, *w)
            r = act.op(lambda e, b=b, ti=ti, n=n: e.copy(V[0:n, ti, :], PS[0:n, b, :]), tk)
            bk.read[b] = [r]
            v_ok.append(r)
            if pend:
                rope(*pend.pop())
        sv[0].done(tk)
        sv[1].done(tk)

        lt = small(128)
        l2 = small(2)
        l3 = small(2)
        lam = small(2)
        vl = vec[:, V_LAM:V_LAM + 256].rearrange("p (i a d) -> p i a d", i=2, a=2)
        a = dve.op(lambda e: e.tensor_tensor(lt.rearrange("p (i d) -> p i d", i=2), vl[:, :, 0, :], vl[:, :, 1, :], ALU.mult), Lv)
        a = dve.op(lambda e: e.tensor_reduce(l2, lt.rearrange("p (i d) -> p i d", i=2), AX, ALU.add), a)
        a = act.op(lambda e: e.activation(l3, l2, ACT.Exp), a)
        a = dve.op(lambda e: e.tensor_tensor(lam[:, 0:1], l3[:, 1:2], l3[:, 0:1], ALU.subtract), a)
        k_lam = dve.op(lambda e: e.tensor_scalar(lam[:, 1:2], lam[:, 0:1], -(0.8 - 0.6 * 1.0), None, ALU.add), a)

        Pm = take(2 * 2 * L, 2, 2)
        Am = take(2 * L, 2)
        AT = take(2 * 3 * 128, 2, 3)
        O = take(3 * 512, 3)
        O2 = take(512)
        mixT = take(8 * L, 8)
        cxs = take(L)
        up = take(2 * (L + 2), 2)
        cv = take(2 * L, 2)
        st = small(16)
        z2 = pool.op(lambda e: e.memset(up[:, :, 0:1], 0.0))
        z3 = pool.op(lambda e: e.memset(up[:, :, L + 1:L + 2], 0.0))
        p_free = [[], []]
        a_free = [[], []]
        at_free = [[], []]

        def scores(u):
            ti, h = divmod(u, 4)
            c0, n = TT[ti]
            j = u % 2
            bs = [bk.take(), bk.take()]
            rowm = st[0:n, 8 * j:8 * j + 2]
            rowb = st[0:n, 8 * j + 2:8 * j + 4]
            rows = st[0:n, 8 * j + 4:8 * j + 6]
            rowr = st[0:n, 8 * j + 6:8 * j + 8]
            ex = []
            for i in range(2):
                b = bs[i]
                tk = pe.op(lambda e, b=b, i=i: e.matmul(
                    PS[0:n, b, 0:L], qz[:, h, i, c0:c0 + n], kT[:, h, :], start=True, stop=True),
                    *kq_ok, z0, z1, *bk.read[b])
                m = dve.op(lambda e, b=b, i=i: e.tensor_reduce(rowm[:, i:i + 1], PS[0:n, b, 0:L], AX, ALU.max), tk, *a_free[j])
                m = dve.op(lambda e, i=i: e.tensor_scalar(rowb[:, i:i + 1], rowm[:, i:i + 1], -0.125, None, ALU.mult), m)
                x = act.op(lambda e, b=b, i=i: e.activation(
                    Pm[0:n, j, i, :], PS[0:n, b, 0:L], ACT.Exp, bias=rowb[:, i:i + 1], scale=0.125,
                    accum_out=rows[:, i:i + 1]), m, *p_free[j])
                bk.read[b] = [x]
                ex.append(x)
            r = dve.op(lambda e: e.reciprocal(rowr, rows), *ex)
            c = dve.op(lambda e: e.tensor_scalar(rowm[:, 1:2], rowr[:, 1:2], lam[0:n, 1:2], None, ALU.mult), r, k_lam)
            c = dve.op(lambda e: e.tensor_scalar(Am[0:n, j, :], Pm[0:n, j, 1, :], rowm[:, 1:2], None, ALU.mult), c, *a_free[j])
            c = dve.op(lambda e: e.scalar_tensor_tensor(
                Am[0:n, j, :], Pm[0:n, j, 0, :], rowr[:, 0:1], Am[0:n, j, :], ALU.mult, ALU.add), c)
            p_free[j] = [c]
            return c

        ob = {}

        def pv(u, tok):
            ti, h = divmod(u, 4)
            c0, n = TT[ti]
            j = u % 2
            b = bk.take()
            for kt, (k0, kn) in enumerate(TT):
                f = lambda e, kt=kt, k0=k0, kn=kn: e.transpose(
                    PS[0:kn, b, kt * 128:kt * 128 + n], Am[0:n, j, k0:k0 + kn], ident[0:n, 0:n])
                if kt < 2:
                    pe.quiet(f, *((tok, *bk.read[b]) if kt == 0 else ()))
                else:
                    tk = pe.op(f)
            a_free[j] = [tk]
            src = PS[:, b, 0:256].rearrange("p (k c) -> p k c", k=2)[:, :, 0:n]
            r1 = act.op(lambda e: e.copy(AT[:, j, 0:2, 0:n], src), tk, *at_free[j])
            r2 = act.op(lambda e: e.copy(AT[0:NM, j, 2, 0:n], PS[0:NM, b, 256:256 + n]), tk)
            bk.read[b] = [r2]
            if h == 0:
                ob[ti] = obk.take()
            o = ob[ti]
            for kt, (k0, kn) in enumerate(TT):
                f = lambda e, kt=kt, kn=kn: e.matmul(
                    PS[0:n, o, h * 128:h * 128 + 128], AT[0:kn, j, kt, 0:n], V[0:kn, kt, h * 128:h * 128 + 128],
                    start=(kt == 0), stop=(kt == 2))
                if kt < 2:
                    pe.quiet(f, *((r2, *v_ok, *(obk.read[o] if h == 0 else [])) if kt == 0 else ()))
                else:
                    tk = pe.op(f)
            at_free[j] = [tk]
            if h == 3:
                r = act.op(lambda e: e.copy(O[0:n, ti, :], PS[0:n, o, :]), tk)
                obk.read[o] = [r]
                return r

        oss = small(12)
        osr = small(12)
        o2_free = []

        def o_norm(ti, tok):
            n = TT[ti][1]
            c0 = TT[ti][0]
            o3 = O[0:n, ti, :].rearrange("p (h d) -> p h d", h=4)
            a = pool.op(lambda e: e.tensor_tensor(O2[0:n, :], O[0:n, ti, :], O[0:n, ti, :], ALU.mult), tok, *o2_free)
            a = dve.op(lambda e: e.tensor_reduce(oss[0:n, 4 * ti:4 * ti + 4], O2[0:n, :].rearrange("p (h d) -> p h d", h=4), AX, ALU.add), a)
            o2_free[:] = [a]
            a = dve.op(lambda e: e.tensor_scalar(osr[0:n, 4 * ti:4 * ti + 4], oss[0:n, 4 * ti:4 * ti + 4], 1.0 / 128, EPS, ALU.mult, ALU.add), a)
            a = pool.op(lambda e: e.tensor_tensor(osr[0:n, 4 * ti:4 * ti + 4], osr[0:n, 4 * ti:4 * ti + 4], mhalf[0:n, 0:4], ALU.pow), a)
            a = dve.op(lambda e: e.tensor_tensor(o3, o3, bc(osr[0:n, 4 * ti:4 * ti + 4], 2, 128), ALU.mult), a)
            b = bk.take()
            for h in range(4):
                f = lambda e, h=h: e.transpose(PS[:, b, h * 128:h * 128 + n], O[0:n, ti, h * 128:h * 128 + 128], ident[0:n, 0:n])
                if h < 3:
                    pe.quiet(f, *((a, *bk.read[b]) if h == 0 else ()))
                else:
                    tk = pe.op(f)
            r = dve.op(lambda e: e.tensor_scalar(
                mixT[:, 0:4, c0:c0 + n], PS[:, b, :].rearrange("p (h c) -> p h c", h=4)[:, :, 0:n],
                vec[:, V_SUB:V_SUB + 1], 0.8, ALU.mult, ALU.mult), tk)
            bk.read[b] = [r]
            return r

        cx_state = {}
        cxs_free = [[]]
        up_free = [[z2, z3], [z2, z3]]
        mix_ok = []

        def conv(i):
            m, part = divmod(i, 3)
            if i % 2 == 0:
                cx_state["sl"] = Slot(t["w_in"][6 + i // 2])
            b, tk = proj_T(cx_state["sl"], i % 2, L, hnT)
            j = m % 2
            cw = lambda k: vec[:, V_CONV + 3 * m + k:V_CONV + 3 * m + k + 1]
            if part == 0:
                r = act.op(lambda e: e.copy(cxs, PS[:, b, 0:L]), tk, *cxs_free[0])
                cx_state["cx"] = r
            elif part == 1:
                r = dve.op(lambda e: e.tensor_tensor(up[:, j, 1:L + 1], PS[:, b, 0:L], cxs, ALU.mult), tk, cx_state["cx"], *up_free[j])
                cxs_free[0] = [r]
                a = dve.op(lambda e: e.tensor_scalar(cv[:, j, :], up[:, j, 0:L], cw(0), None, ALU.mult), r, *up_free[j])
                a = dve.op(lambda e: e.scalar_tensor_tensor(cv[:, j, :], up[:, j, 1:L + 1], cw(1), cv[:, j, :], ALU.mult, ALU.add), a)
                a = dve.op(lambda e: e.scalar_tensor_tensor(cv[:, j, :], up[:, j, 2:L + 2], cw(2), cv[:, j, :], ALU.mult, ALU.add), a)
                cx_state["cv"] = a
            else:
                r = dve.op(lambda e: e.tensor_tensor(mixT[:, 4 + m, :], PS[:, b, 0:L], cv[:, j, :], ALU.mult), tk, cx_state["cv"])
                up_free[j] = [r]
                mix_ok.append(r)
            bk.read[b] = [r]

        obk = Banks([6, 7])
        att = Banks(range(6))
        for b in range(8):
            (obk if b > 5 else att).read[b] = bk.read[b]
        bk = att
        prev = None
        for u in range(12):
            tok = scores(u)
            conv(u)
            if prev is not None:
                r = pv(u - 1, prev)
                if r is not None:
                    mix_ok.append(o_norm((u - 1) // 4, r))
            prev = tok
        r = pv(11, prev)
        mix_ok.append(o_norm(2, r))

        whole = Banks(range(8))
        for b in range(8):
            whole.read[b] = (obk if b > 5 else att).read[b]
        bk = whole
        so1 = [Slot(t["w_out"][i]) for i in range(4)]
        H_ok = {}
        for ti, (c0, n) in enumerate(TT):
            for db in range(2):
                b = bk.take()
                for c in range(8):
                    f = lambda e, c=c, b=b, c0=c0, n=n, db=db: e.matmul(
                        PS[0:n, b, :], mixT[:, c, c0:c0 + n],
                        so1[c // 2].v[:, (c % 2) * 1024 + db * 512:(c % 2) * 1024 + db * 512 + 512],
                        start=(c == 0), stop=(c == 7))
                    w = ((*mix_ok, *bk.read[b]) if c == 0 else ()) + (so1[c // 2].tok,)
                    if c < 7:
                        pe.quiet(f, *w)
                    else:
                        tk = pe.op(f, *w)
                hv = H[0:n, ti, db * 512:db * 512 + 512]
                r = dve.op(lambda e, hv=hv, b=b, n=n: e.tensor_tensor(hv, hv, PS[0:n, b, :], ALU.add), tk)
                bk.read[b] = [r]
                H_ok[ti] = [r] if db == 0 else H_ok[ti] + [r]
        for s in so1:
            s.done(tk)

        lg = take(3 * 16, 3)
        af = take(3 * 16, 3)
        rt = small(12)
        wr = vec[:, V_WR:V_WR + 128].rearrange("p (k c) -> p k c", k=8)
        xn_ok = []
        af_ok = []
        aT = take(L + 6)
        wk = take(2 * (L + 6), 2)
        bt = bk.take()
        bt_read = bk.read[bt]
        bk_ids = [b for b in range(8) if b != bt]
        rest = Banks(bk_ids)
        for b in bk_ids:
            rest.read[b] = bk.read[b]
        bk = rest
        for ti, (c0, n) in enumerate(TT):
            a, r = rms(H[0:n, ti, :], n, ss[0:n, ti:ti + 1], rs[0:n, ti:ti + 1], 1.0 / D, junk[0:n, :], *H_ok[ti], *jprev)
            jprev = (a,)
            x = dve.op(lambda e, ti=ti, n=n: e.scalar_tensor_tensor(
                XN[0:n, ti, :], H[0:n, ti, :], rs[0:n, ti:ti + 1], gbc[0:n, :], ALU.mult, ALU.mult), r, Lg, last_turn)
            xn_ok.append(x)
            tr = turn_tile(XN, ti, n, c0, hnT, [x, tk])
            b = bk.take()
            for k in range(8):
                f = lambda e, k=k, b=b, c0=c0, n=n: e.matmul(
                    PS[0:n, b, 0:16], hnT[:, k, c0:c0 + n], wr[:, k, :], start=(k == 0), stop=(k == 7))
                if k < 7:
                    pe.quiet(f, *((*tr, Lv, *bk.read[b]) if k == 0 else ()))
                else:
                    t3 = pe.op(f)
            m = rt[0:n, 4 * ti:4 * ti + 1]
            s_ = rt[0:n, 4 * ti + 1:4 * ti + 2]
            r_ = rt[0:n, 4 * ti + 2:4 * ti + 3]
            a = dve.op(lambda e, m=m, b=b, n=n: e.tensor_reduce(m, PS[0:n, b, 0:16], AX, ALU.max, negate=True), t3)
            a = act.op(lambda e, ti=ti, n=n, b=b, m=m, s_=s_: e.activation(
                lg[0:n, ti, :], PS[0:n, b, 0:16], ACT.Exp, bias=m, scale=1.0, accum_out=s_), a)
            bk.read[b] = [a]
            a = dve.op(lambda e, s_=s_, r_=r_: e.reciprocal(r_, s_), a)
            a = dve.op(lambda e, ti=ti, n=n, r_=r_: e.tensor_scalar(af[0:n, ti, :], lg[0:n, ti, :], r_, None, ALU.mult), a)
            af_ok.append(a)
            t4 = pe.op(lambda e, ti=ti, n=n, c0=c0: e.transpose(PS[0:16, bt, c0:c0 + n], af[0:n, ti, :], ident[0:n, 0:n]), a, *bt_read)
        a0 = dve.op(lambda e: e.tensor_copy(aT[0:16, 0:L], PS[0:16, bt, 0:L]), t4)
        a1 = dve.op(lambda e: e.memset(aT[0:16, L:L + 6], 2.0))
        bk_bt = [a0]
        m8 = small(8)
        cur = aT
        a = a1
        for r in range(5):
            a = dve.op(lambda e, cur=cur: e.max(m8[0:16, :], cur[0:16, :]), a, a0)
            nxt = wk[:, r % 2, :]
            a = dve.op(lambda e, cur=cur, nxt=nxt: e.match_replace(nxt[0:16, :], m8[0:16, :], cur[0:16, :], -1.0), a)
            cur = nxt
        mk = wk[0:16, 1, 0:L]
        cs = aT[0:16, 0:L]
        fin = wk[0:16, 0, 0:L]
        a = dve.op(lambda e: e.tensor_scalar(mk, fin, -1.0, None, ALU.is_equal), a)
        a = dve.op(lambda e: e.tensor_tensor_scan(cs, ones[0:16, 0:1].broadcast_to([16, L]), mk, 0.0, ALU.mult, ALU.add), a)
        a = dve.op(lambda e: e.tensor_tensor(cs, cs, mk, ALU.mult), a)
        a = dve.op(lambda e: e.tensor_scalar(cs, cs, -1.0, None, ALU.add), a)
        ps_ = take(3 * 16, 3)
        for ti, (c0, n) in enumerate(TT):
            t4 = pe.op(lambda e, ti=ti, n=n, c0=c0: e.transpose(PS[0:n, bt, ti * 16:ti * 16 + 16], cs[:, c0:c0 + n], ident[0:16, 0:16]), a)
        a = dve.op(lambda e: e.tensor_copy(ps_[:, 0:2, :], PS[:, bt, 0:32].rearrange("p (t c) -> p t c", t=2)), t4)
        b_ = dve.op(lambda e: e.tensor_copy(ps_[0:NM, 2, :], PS[0:NM, bt, 32:48]), t4)
        bt_free = b_
        base = at[0]
        at[0] = 3072
        S = take(3 * 1024, 3, 16)
        XG = take(2 * 1024, 2, 8)
        SL = take(1024, 2)
        Hh = take(1024, 2)
        HT = take(2 * 1024, 2, 8)
        Y = take(2 * 1024, 2)
        GA = take(256, 2)
        GT = take(256, 2)
        assert at[0] <= AR - 3 * 16 * 3 - 3 * (L + 6)
        at[0] = base
        iota = cst[:, C_IOTA:C_IOTA + 64]
        s_ok = []
        for ti, (c0, n) in enumerate(TT):
            s_ok.append(dve.op(lambda e, ti=ti, n=n: e.tensor_tensor(
                S[0:n, ti, :, :], bc(iota[0:n, :], 1, 16), bc(ps_[0:n, ti, :], 2, 64), ALU.is_equal), a, b_))

        kw_free = [*s_ok, (act.sem, act.n), (pe.sem, pe.n), (pool.sem, pool.n)]
        Lg2 = act.dma(lambda e: e.dma_start(gbc[:, :], t["gbc"][1]), c_g, *xn_ok)

        misc = Banks([5, 6, 7])
        for b in misc.ids:
            misc.read[b] = [bt_free, (act.sem, act.n), (dve.sem, dve.n), (pe.sem, pe.n)]
        start_all = [(act.sem, act.n), (dve.sem, dve.n)]
        gu_free = [list(start_all), list(start_all)]
        y_free = list(start_all)
        xg_free = [[], []]
        xg_ok = [None, None]
        ht_free = [[], []]
        yb_free = [[], []]
        gt_ok = {}
        y_tok = {}

        def gather(p):
            j = p % 2
            ok = []
            for half in range(2):
                b = misc.take()
                for c4 in range(4):
                    c = half * 4 + c4
                    for ti, (c0, n) in enumerate(TT):
                        f = lambda e, b=b, c4=c4, c=c, ti=ti, n=n: e.matmul(
                            PS[:, b, c4 * 128:c4 * 128 + 128], XN[0:n, ti, c * 128:c * 128 + 128],
                            S[0:n, ti, 2 * p:2 * p + 2, :], start=(ti == 0), stop=(ti == 2))
                        w = (*s_ok, *xn_ok, *misc.read[b]) if c4 == 0 and ti == 0 else ()
                        if c4 == 3 and ti == 2:
                            tk = pe.op(f, *w)
                        else:
                            pe.quiet(f, *w)
                dst = XG[:, j, half * 4:half * 4 + 4, :]
                src = PS[:, b, :].rearrange("p (k c) -> p k c", k=4)
                if half == 0:
                    r = act.op(lambda e, dst=dst, src=src: e.copy(dst, src), tk, *xg_free[j])
                else:
                    r = dve.op(lambda e, dst=dst, src=src: e.tensor_copy(dst, src), tk, *xg_free[j])
                misc.read[b] = [r]
                ok.append(r)
            xg_ok[j] = ok

        ga_free = [[]]
        gt_free = [[]]

        def gates(p):
            a = [dve.op(lambda e, ti=ti: e.tensor_tensor(
                GA[:, ti, :].rearrange("p (e s) -> p e s", e=2), S[:, ti, 2 * p:2 * p + 2, :],
                bc(af[:, ti, 2 * p:2 * p + 2], 2, 64), ALU.mult), *ga_free[0]) for ti in range(2)]
            b = misc.take()
            pe.quiet(lambda e: e.transpose(PS[:, b, 0:128], GA[:, 0, :], ident), *a, *misc.read[b])
            tk = pe.op(lambda e: e.transpose(PS[:, b, 128:256], GA[:, 1, :], ident))
            ga_free[0] = [tk]
            r = dve.op(lambda e: e.tensor_copy(GT[:, :, :], PS[:, b, 0:256].rearrange("p (t c) -> p t c", t=2)), tk, *gt_free[0])
            misc.read[b] = [r]
            gt_ok[p] = r

        def scatter(p):
            j = p % 2
            out = []
            for ti in range(2):
                for db in range(2):
                    b = misc.take()
                    tk = pe.op(lambda e, ti=ti, db=db, b=b: e.matmul(
                        PS[:, b, :], GT[:, ti, :], Y[:, j, db * 512:db * 512 + 512], start=True, stop=True),
                        gt_ok[p], *y_tok[p], *misc.read[b])
                    hv = H[:, ti, db * 512:db * 512 + 512]
                    r = dve.op(lambda e, hv=hv, b=b: e.tensor_tensor(hv, hv, PS[:, b, :], ALU.add), tk)
                    misc.read[b] = [r]
                    out.append(r)
            gt_free[0] = [tk]
            yb_free[j] = [tk]
            return out

        def gate_up(ex):
            p, par = divmod(ex, 2)
            j = p % 2
            for k in range(8):
                for mat, name in enumerate(("w_gate", "w_up")):
                    sl = Slot(t[name][ex, k * 128:k * 128 + 128, :])
                    for q in range(2):
                        for g in range(2):
                            f = lambda e, k=k, mat=mat, q=q, g=g, sl=sl: e.matmul(
                                PS[64 * g:64 * g + 64, 2 * mat + q, :], XG[:, j, k, 64 * par:64 * par + 64],
                                sl.v[:, (2 * g + q) * 512:(2 * g + q) * 512 + 512], start=(k == 0), stop=(k == 7))
                            w = [sl.tok, *xg_ok[j]]
                            if k == 0:
                                w += gu_free[q]
                            if q == 1 and g == 1:
                                tk = pe.op(f, *w)
                            else:
                                pe.quiet(f, *w)
                    sl.done(tk)
            if par == 1:
                xg_free[j] = [tk]
            return tk

        hh_free = [[], []]

        def hidden(ex, tk):
            ok = []
            for q in range(2):
                a = act.op(lambda e, q=q: e.activation(SL[:, q, :], PS[:, q, :], ACT.Silu), tk, *hh_free[q])
                r = dve.op(lambda e, q=q: e.tensor_tensor(Hh[:, q, :], SL[:, q, :], PS[:, 2 + q, :], ALU.mult), a, *hh_free[q])
                gu_free[q] = [r]
                ok.append(r)
            return ok

        def down(ex, hok):
            p, par = divmod(ex, 2)
            j = ex % 2
            ht_ok = []
            for q in range(2):
                b = misc.take()
                for i in range(4):
                    f = lambda e, q=q, i=i, b=b: e.transpose(PS[:, b, i * 128:i * 128 + 128], Hh[:, q, i * 128:i * 128 + 128], ident)
                    if i < 3:
                        pe.quiet(f, *((hok[q], *misc.read[b]) if i == 0 else ()))
                    else:
                        tk = pe.op(f)
                hh_free[q] = [tk]
                dst = HT[:, j, 4 * q:4 * q + 4, :]
                src = PS[:, b, :].rearrange("p (k c) -> p k c", k=4)
                if q == 0:
                    r = act.op(lambda e, dst=dst, src=src: e.copy(dst, src), tk, *ht_free[j])
                else:
                    r = dve.op(lambda e, dst=dst, src=src: e.tensor_copy(dst, src), tk, *ht_free[j])
                misc.read[b] = [r]
                ht_ok.append(r)
            for s in range(8):
                sl = Slot(t["w_down"][ex, 256 * s:256 * s + 256, :].rearrange("(a p) d -> p a d", p=128))
                for a in range(2):
                    c = 2 * s + a
                    for g in range(2):
                        f = lambda e, a=a, g=g, c=c, sl=sl: e.matmul(
                            PS[64 * g:64 * g + 64, 4, :], HT[:, j, c % 8, (c // 8) * 64:(c // 8) * 64 + 64],
                            sl.v[:, a * 1024 + g * 512:a * 1024 + g * 512 + 512], start=(c == 0), stop=(c == 15))
                        w = [sl.tok, ht_ok[0], ht_ok[1]] + (list(y_free) if c == 0 else [])
                        if a == 1 and g == 1:
                            tk = pe.op(f, *w)
                        else:
                            pe.quiet(f, *w)
                sl.done(tk)
            ht_free[j] = [tk]
            rs_ = [act.op(lambda e, g=g: e.copy(
                Y[64 * par:64 * par + 64, p % 2, 512 * g:512 * g + 512], PS[64 * g:64 * g + 64, 4, :]),
                tk, *yb_free[p % 2]) for g in range(2)]
            y_free[:] = rs_
            y_tok.setdefault(p, []).extend(rs_)

        NX = t.get("n_experts", NE)
        if NX:
            gather(0)
        for ex in range(NX):
            tk = gate_up(ex)
            hok = hidden(ex, tk)
            if ex % 2 == 0:
                if ex >= 2:
                    scatter(ex // 2 - 1)
                gates(ex // 2)
            elif ex + 1 < NX:
                gather(ex // 2 + 1)
            down(ex, hok)
        moe_ok = scatter(NX // 2 - 1) if NX else H_ok[0] + H_ok[1]

        for i, src in enumerate(stream):
            after = (used[before[i]],) if before[i] is not None else ()
            s = place[i]
            dst = ring[:, s * 2048:s * 2048 + 2048]
            if len(src.shape) == 3:
                dst = dst.rearrange("p (a d) -> p a d", a=src.shape[1])
            sp.dma(lambda e, dst=dst, src=src: e.dma_start(dst, src), slot_sem[s], *after)

        moe_end = [(act.sem, act.n), (dve.sem, dve.n), (pe.sem, pe.n)]
        first.close()
        second = ExitStack()
        ctx.enter_context(second)
        wp = sb1("wp", WR * 2048, F32R, second)[:, :].rearrange("p (w q c) -> p w q c", w=WR, q=2)
        hr = sb1("hr", 4096, F32R, second)[:, :].rearrange("p (q c) -> p q c", q=2)
        raw = sb1("raw", RAW * 1024, F32, second)
        raw_over = WR + 2
        mid = ExitStack()
        ctx.enter_context(mid)
        big = sb1("big", FIRST_ROOM - WR * 2048 - 4096 - RAW * 1024, F32, mid)
        KW = sb1("kw", NK2 + NW2, F32, mid)
        little = sb1("little", RING * 2048 + AR - FIRST_ROOM - NK2 - NW2, F32, mid)
        c_kw = [sem("c_kw"), 0]
        Lk2 = pool.dma(lambda e: e.dma_start(KW[:, :], t["kw2"]), c_kw, *kw_free)
        KT = KW[:, 0:NK2]
        VW = KW[:, NK2:NK2 + NW2]
        segs = {"big": [big, 0, FIRST_ROOM - WR * 2048 - 4096 - RAW * 1024],
                "little": [little, 0, RING * 2048 + AR - FIRST_ROOM - NK2 - NW2], "Hx": [Hx, 2048, 3072]}

        def shaped(v, dims):
            if len(dims) == 1:
                v = v.rearrange("p (a b) -> p a b", a=dims[0])
            elif len(dims) == 2:
                v = v.rearrange("p (a b c) -> p a b c", a=dims[0], b=dims[1])
            return v

        def room(where, n, *dims):
            s_ = segs[where]
            assert s_[2] - s_[1] >= n, (where, n, s_[2] - s_[1])
            s_[1] += n
            return shaped(s_[0][:, s_[1] - n:s_[1]], dims)

        R1 = room("big", 4096)
        R4 = room("big", 4096)
        NN = room("big", 3072)
        BTf = room("big", 4096)
        Ff = room("big", 3072)
        KDT = room("big", 2048)
        KG = room("big", 1024, 2, 4)
        SUV = room("big", 2048)
        RT = room("big", 512)
        MS = room("little", 1024, 2)
        Z = room("little", 1024, 2)
        SQ = room("little", 1024)
        SW = room("little", 512, 4)
        SC = room("little", 512, 2)
        PT = room("Hx", 512, 2)
        XB = NN[:, 0:2048].rearrange("p (t c) -> p t c", t=2)
        hTh = hr[:, 0, :].rearrange("p (k c) -> p k c", k=8)
        hTl = hr[:, 1, :].rearrange("p (k c) -> p k c", k=8)

        raw_sem = [[sem(f"r{n}"), 0] for n in range(RAW)]
        stream2, raw_used = [], []
        last_of_slot = {place[n]: used[n] for n in range(len(place))}

        def raw_piece(src):
            n = len(stream2)
            stream2.append((src, lambda: [raw_used[n - RAW]] if n >= RAW else [last_of_slot[raw_over + n // 2]]))
            raw_used.append(None)
            return n, raw[:, (n % RAW) * 1024:(n % RAW) * 1024 + src.shape[1]], (raw_sem[n % RAW][0], 16 * (n // RAW + 1))

        parts, parts_used, took = [], [], [0]

        def prepare(n):
            if n >= t["w2"].shape[0]:
                return
            r, v, tok = raw_piece(t["w2"][n])
            hi, lo = wp[:, n % WR, 0, :], wp[:, n % WR, 1, :]
            a = act.op(lambda e: e.copy(hi, v), tok, *moe_end, *([parts_used[n - WR]] if n >= WR else []))
            b = dve.op(lambda e: e.tensor_tensor(lo, v, hi.bitcast(F32), ALU.subtract), a)
            raw_used[r] = b
            parts.append((hi, lo, (a, b)))

        def piece():
            n = took[0]
            took[0] += 1
            assert len(parts_used) == n
            prepare(n + WR - 1)
            return parts[n]

        def release(tok):
            parts_used.append(tok)

        for n in range(WR - 1):
            prepare(n)

        bk = Banks(range(6))
        open_read = {b: list(moe_end) for b in range(8)}
        for b in bk.ids:
            bk.read[b] = list(moe_end)
        fr = small(8)

        def rms2(XB, ti, c, *after):
            x = fr[:, c:c + 1]
            a = act.op(lambda e: e.activation(XB[:, ti, :], H[:, ti, :], ACT.Square, accum_out=x), *after)
            b = dve.op(lambda e: e.tensor_scalar(x, x, 1.0 / D, EPS, ALU.mult, ALU.add), a)
            return pool.op(lambda e: e.tensor_tensor(x, x, mhalf[:, 0:1], ALU.pow), b, k_mh), x

        def turn_two(XB, ti, gcol, tmp, after):
            out = []
            for half in range(2):
                b = bk.take()
                for k in range(4):
                    c = half * 4 + k
                    f = lambda e, b=b, k=k, c=c: e.transpose(PS[:, b, k * 128:k * 128 + 128], XB[:, ti, c * 128:c * 128 + 128], ident)
                    if k < 3:
                        pe.quiet(f, *((*after, *bk.read[b]) if k == 0 else ()))
                    else:
                        tk = pe.op(f)
                tm = tmp[:, half * 512:half * 512 + 512].rearrange("p (k c) -> p k c", k=4)
                hi = hTh[:, half * 4:half * 4 + 4, ti * 128:ti * 128 + 128]
                lo = hTl[:, half * 4:half * 4 + 4, ti * 128:ti * 128 + 128]
                r = dve.op(lambda e, tm=tm, b=b, half=half: e.tensor_tensor(
                    tm, PS[:, b, :].rearrange("p (k c) -> p k c", k=4), bc(gcol[:, half * 4:half * 4 + 4], 2, 128), ALU.mult), tk, Lk2, Lv, *after)
                bk.read[b] = [r]
                a = act.op(lambda e, tm=tm, hi=hi: e.copy(hi, tm), r)
                out += [a, dve.op(lambda e, tm=tm, hi=hi, lo=lo: e.tensor_tensor(lo, tm, hi.bitcast(F32), ALU.subtract), a)]
            return out

        hT_ok = []
        for ti in range(2):
            r, x = rms2(XB, ti, ti, *moe_end)
            a = dve.op(lambda e, ti=ti, x=x: e.scalar_tensor_tensor(H[:, ti, :], H[:, ti, :], x, gbc[:, :], ALU.mult, ALU.mult), r, Lg2)
            r, x = rms2(XB, ti, 2 + ti, a)
            a = dve.op(lambda e, ti=ti, x=x: e.tensor_scalar(XB[:, ti, :], H[:, ti, :], x, None, ALU.mult), r)
            hT_ok += turn_two(XB, ti, VW[:, W_N1:W_N1 + 8], SQ, [a, *hT_ok])

        def tile_T(sl, off, K, lhs, rhs, N, *after):
            b = bk.take()
            for k in range(K):
                f = lambda e, k=k: e.matmul(PS[:, b, 0:N], lhs(k), rhs(k), start=(k == 0), stop=(k == K - 1))
                w = (*after, *bk.read[b]) if k == 0 else ()
                if k < K - 1:
                    pe.quiet(f, *w)
                else:
                    tk = pe.op(f, *w)
            return b, tk

        PASSES = ((0, 0), (0, 1), (1, 0))

        def tile3(K, lhs, rhs, N, *after):
            b = bk.take()
            for k in range(K):
                for q, (p1, p2) in enumerate(PASSES):
                    f = lambda e, k=k, p1=p1, p2=p2, q=q: e.matmul(
                        PS[:, b, 0:N], lhs(p1, k), rhs(p2, k), start=(k == 0 and q == 0), stop=(k == K - 1 and q == 2))
                    w = (*after, *bk.read[b]) if k == 0 and q == 0 else ()
                    if k < K - 1 or q < 2:
                        pe.quiet(f, *w)
                    else:
                        tk = pe.op(f, *w)
            return b, tk

        def rows3(banks, first, last, acts, wts, cols, after, toks):
            n = 0
            for (ti, c), b in banks.items():
                for q, (p1, p2) in enumerate(PASSES):
                    f = lambda e, ti=ti, c=c, b=b, p1=p1, p2=p2, q=q: e.matmul(
                        PS[:, b, :], acts(p1, ti), wts(p2)[:, cols[c]], start=(first and q == 0), stop=(last and q == 2))
                    w = tuple(after if n == 0 else ()) + tuple(open_read[b] if first and q == 0 else ())
                    n += 1
                    if q == 2 and (last or n == 3 * len(banks)):
                        tk = pe.op(f, *w)
                        toks[(ti, c)] = tk
                    else:
                        pe.quiet(f, *w)
            return tk

        bulk = []
        outs = []

        def fill(n=1):
            for _ in range(n):
                if bulk:
                    bulk.pop(0)()

        QT = R1[:, 0:3072].rearrange("p (m c) -> p m c", m=12)
        cb_ = R4[:, 0:4 * 259].rearrange("p (a c) -> p a c", a=4)
        cc_ = R4[:, 1100:1100 + 4 * 256].rearrange("p (a c) -> p a c", a=4)
        zz = pool.op(lambda e: e.memset(cb_[:, :, 0:3], 0.0), *moe_end)
        qt_ok = []
        cf = [[zz] for _ in range(4)]

        def tile_hT(*after):
            hi, lo, ok = piece()
            v = [x.rearrange("p (k c) -> p k c", k=8) for x in (hi, lo)]
            b, tk = tile3(8, lambda p, k: v[p][:, k, :], lambda p, k: (hTh, hTl)[p][:, k, :], 256, *ok, *after)
            release(tk)
            return b, tk

        for m in range(12):
            b, tk = tile_hT(*hT_ok)
            j = m % 4
            a = act.op(lambda e, b=b, j=j: e.copy(cb_[:, j, 3:259], PS[:, b, 0:256]), tk, *cf[j])
            bk.read[b] = [a]
            cw = lambda k, m=m: VW[:, W_CONV + 4 * m + k:W_CONV + 4 * m + k + 1]
            a = dve.op(lambda e, j=j, cw=cw: e.tensor_scalar(cc_[:, j, :], cb_[:, j, 0:256], cw(0), None, ALU.mult), a, Lk2, *cf[j])
            for k in range(1, 4):
                a = dve.op(lambda e, j=j, k=k, cw=cw: e.scalar_tensor_tensor(
                    cc_[:, j, :], cb_[:, j, k:k + 256], cw(k), cc_[:, j, :], ALU.mult, ALU.add), a)
            a = act.op(lambda e, j=j, m=m: e.activation(QT[:, m, :], cc_[:, j, :], ACT.Silu), a)
            cf[j] = [a]
            qt_ok.append(a)

        def nat_steps(evac):
            toks = {}

            def step(s_):
                hi, lo, ok = piece()
                for k2 in range(2):
                    k = 2 * s_ + k2
                    tk = rows3({(0, 0): 6, (1, 0): 7}, k == 0, k == 7,
                               lambda p, ti, k=k: (hTh, hTl)[p][:, k, ti * 128:ti * 128 + 128],
                               lambda p, k2=k2: (hi, lo)[p][:, k2 * 512:k2 * 512 + 512], [slice(0, 512)],
                               (*ok, *hT_ok), toks)
                release(tk)
                if s_ == 3:
                    for ti in range(2):
                        open_read[6 + ti] = [evac(ti, 6 + ti, toks[(ti, 0)])]
            return [lambda s_=s_: step(s_) for s_ in range(4)]

        ms_ok, z_ok = [None, None], [None, None]
        SU = SUV[:, 0:1024].rearrange("p (t c) -> p t c", t=2)
        SV = SUV[:, 1024:2048].rearrange("p (t c) -> p t c", t=2)
        F = Ff.rearrange("p (q t c) -> p q t c", q=3, t=2)
        su_ok, sv_ok, f_ok = [None, None], [None, None], {}

        def to(dst, ok, key, func=None):
            def evac(ti, b, tk):
                r = act.op((lambda e: e.copy(dst[:, ti, :], PS[:, b, :])) if func is None else
                           (lambda e: e.activation(dst[:, ti, :], PS[:, b, :], func)), tk, *moe_end)
                ok[key(ti)] = r
                return r
            return evac

        for f in nat_steps(to(MS, ms_ok, lambda ti: ti)) + nat_steps(to(Z, z_ok, lambda ti: ti, ACT.Silu)):
            f()
        bulk += nat_steps(to(SU, su_ok, lambda ti: ti, ACT.Gelu_apprx_tanh))
        bulk += nat_steps(to(SV, sv_ok, lambda ti: ti, ACT.Gelu_apprx_tanh))
        for q in range(3):
            bulk += nat_steps(to(F[:, q], f_ok, lambda ti, q=q: (ti, q)))
        fill(FILLS[0])

        spx = small(16).rearrange("p (t c) -> p t c", t=2)
        spa = small(16).rearrange("p (t c) -> p t c", t=2)
        g8 = small(8).rearrange("p (t c) -> p t c", t=2)
        lf = small(8).rearrange("p (t c) -> p t c", t=2)
        beta = small(8).rearrange("p (t c) -> p t c", t=2)
        ea = small(4)
        GC = small(40)
        eg = small(8)
        ed = small(8)
        egl = small(16)
        bg = small(8)
        a1 = dve.op(lambda e: e.tensor_tensor(spx[:, :, 0:4], MS[:, :, 448:452], bc(VW[:, W_DT:W_DT + 4], 1, 2), ALU.add), *ms_ok, Lk2)
        a = dve.op(lambda e: e.tensor_tensor(spx[:, :, 4:8], MS[:, :, 456:460], bc(VW[:, W_FB:W_FB + 4], 1, 2), ALU.add), *ms_ok)
        a2 = dve.op(lambda e: e.tensor_scalar(spx[:, :, 4:8], spx[:, :, 4:8], -1.0, None, ALU.mult), a)
        a = dve.op(lambda e: e.scalar_tensor_tensor(spa, spx, -1.0, spx, ALU.mult, ALU.max), a1, a2)
        a = act.op(lambda e: e.activation(spa, spa, ACT.Exp, scale=-1.0), a)
        b1 = act.op(lambda e: e.activation(beta, MS[:, :, 452:456], ACT.Exp, scale=-1.0), *ms_ok)
        b2 = act.op(lambda e: e.activation(ea, VW[:, W_ALOG:W_ALOG + 4], ACT.Exp), Lk2)
        a = dve.op(lambda e: e.tensor_scalar(spa, spa, 1.0, None, ALU.add), a)
        a = act.op(lambda e: e.activation(spa, spa, ACT.Ln), a)
        a = dve.op(lambda e: e.scalar_tensor_tensor(spa, spx, 0.0, spa, ALU.max, ALU.add), a)
        g_ok = dve.op(lambda e: e.scalar_tensor_tensor(g8, spa[:, :, 0:4], -1.0, bc(ea, 1, 2), ALU.mult, ALU.mult), a, b2)
        l_ok = dve.op(lambda e: e.tensor_scalar(lf, spa[:, :, 4:8], -1.0, None, ALU.mult), a)
        b1 = dve.op(lambda e: e.tensor_scalar(beta, beta, 1.0, None, ALU.add), b1)
        b_ok = dve.op(lambda e: e.reciprocal(beta, beta), b1)
        g8f, lff = g8.rearrange("p t c -> p (t c)"), lf.rearrange("p t c -> p (t c)")
        tri = KT[:, K_TRI:K_TRI + 128]
        tric = KT[:, K_TRIC:K_TRIC + 128]
        one = KT[:, K_ONE:K_ONE + 128]
        b = bk.take()
        for n_, (c0, lhs, rhs, first, last) in enumerate([
                (0, tric, g8f, True, True), (8, KT[:, K_BLK:K_BLK + 128], g8f, True, True),
                (16, KT[:, K_SEL:K_SEL + 128], g8f, True, True), (24, KT[:, K_SEL + 128:K_SEL + 256], g8f, True, True),
                (32, tri, lf[:, 0, :], True, True), (36, one, lf[:, 0, :], True, False), (36, tri, lf[:, 1, :], False, True)]):
            w = rhs.free_size()
            f = lambda e, b=b, c0=c0, lhs=lhs, rhs=rhs, first=first, last=last, w=w: e.matmul(
                PS[:, b, c0:c0 + w], lhs, rhs, start=first, stop=last)
            if n_ < 6:
                pe.quiet(f, *((g_ok, l_ok, *bk.read[b]) if n_ == 0 else ()))
            else:
                tk = pe.op(f)
        gc_ok = dve.op(lambda e, b=b: e.tensor_copy(GC, PS[:, b, 0:40]), tk)
        bk.read[b] = [gc_ok]
        e1 = act.op(lambda e: e.activation(eg, GC[:, 0:8], ACT.Exp), gc_ok)
        a = dve.op(lambda e: e.tensor_tensor(ed, GC[:, 8:16], GC[:, 0:8], ALU.subtract), gc_ok)
        e2 = act.op(lambda e: e.activation(ed, ed, ACT.Exp), a)
        e3 = act.op(lambda e: e.activation(egl, GC[:, 16:32], ACT.Exp), gc_ok)
        bg_ok = dve.op(lambda e: e.tensor_tensor(bg, beta.rearrange("p t c -> p (t c)"), eg, ALU.mult), e1, b_ok)
        KD = KDT[:, 0:1024].rearrange("p (t h d) -> p t h d", t=2, h=4)
        DT = KDT[:, 1024:2048].rearrange("p (r i) -> p r i", r=8)
        RB = R4[:, 2200:3224].rearrange("p (r i) -> p r i", r=8)
        a = dve.op(lambda e: e.tensor_tensor(RB, bc(tric, 1, 8), bc(g8f, 2, 128), ALU.mult), g_ok, *moe_end)
        d_ok = []
        for q in range(2):
            b = bk.take()
            tk = pe.op(lambda e, b=b, q=q: e.matmul(PS[:, b, :], one, R4[:, 2200 + 512 * q:2712 + 512 * q], start=True, stop=True), a, *bk.read[b])
            for r in range(4):
                x = dve.op(lambda e, b=b, q=q, r=r: e.tensor_scalar(
                    DT[:, 4 * q + r, :], PS[:, b, r * 128:r * 128 + 128], GC[:, 4 * q + r:4 * q + r + 1], 0.0, ALU.subtract, ALU.min), tk, gc_ok)
            bk.read[b] = [x]
            d_ok.append(act.op(lambda e, q=q: e.activation(DT[:, 4 * q:4 * q + 4, :], DT[:, 4 * q:4 * q + 4, :], ACT.Exp), x))
        dt_ok = dve.op(lambda e: e.tensor_tensor(DT, DT, bc(tric, 1, 8), ALU.mult), *d_ok)
        fill(FILLS[1])

        sq_free = [[]]

        def sums(src, G, W, *after):
            c = small(G)
            s3 = SQ[:, 0:G * W].rearrange("p (g w) -> p g w", g=G)
            a = pool.op(lambda e: e.tensor_tensor(s3, src, src, ALU.mult), *after, *sq_free[0])
            b = dve.op(lambda e: e.tensor_reduce(c, s3, AX, ALU.add), a)
            sq_free[0] = [b]
            return c, b

        def power(c, G, mean, *after):
            a = dve.op(lambda e: e.tensor_scalar(c, c, mean, EPS, ALU.mult, ALU.add), *after)
            return pool.op(lambda e: e.tensor_tensor(c, c, mhalf[:, 0:G], ALU.pow), a)

        def scale(dst, src, c, W, *after):
            return dve.op(lambda e: e.tensor_tensor(dst, src, bc(c, 2, W), ALU.mult), *after)

        def turn4(srcs, dsts, after, gcol=None, rows=128, eng=None):
            b = bk.take()
            G = len(srcs)
            for i, s_ in enumerate(srcs):
                f = lambda e, i=i, s_=s_: e.transpose(PS[0:rows, b, i * 128:i * 128 + 128], s_, ident)
                if i < G - 1:
                    pe.quiet(f, *((*after, *bk.read[b]) if i == 0 else ()))
                else:
                    tk = pe.op(f, *((*after, *bk.read[b]) if i == 0 else ()))
            src = PS[0:rows, b, 0:G * 128].rearrange("p (g c) -> p g c", g=G)
            if gcol is not None:
                r = dve.op(lambda e: e.tensor_scalar(dsts, src, gcol, None, ALU.mult), tk)
            elif eng is dve:
                r = dve.op(lambda e: e.tensor_copy(dsts, src), tk)
            else:
                r = act.op(lambda e: e.copy(dsts, src), tk)
            bk.read[b] = [r]
            return r

        N = NN.rearrange("p (t m c) -> p t m c", t=2, m=12)
        n_ok = {}
        for ti in range(2):
            for q in range(3):
                n_ok[(ti, q)] = turn4([QT[:, 4 * q + h, ti * 128:ti * 128 + 128] for h in range(4)],
                                      N[:, ti, 4 * q:4 * q + 4, :], qt_ok + list(moe_end), eng=dve if q == 1 else None)
        QD = R4[:, 0:1024].rearrange("p (t h d) -> p t h d", t=2, h=4)
        KB = R4[:, 1024:2048].rearrange("p (t h d) -> p t h d", t=2, h=4)
        T4 = R1.rearrange("p (w h c) -> p w h c", w=4, h=4)
        t4_ok = []
        kd_ok, kg_ok, vb_ok = [], [], []
        conv_end = [qt_ok[-1], qt_ok[-2], qt_ok[-3], qt_ok[-4]]
        for ti in range(2):
            c, a = sums(N[:, ti, 0:8, :], 8, 128, n_ok[(ti, 0)], n_ok[(ti, 1)])
            r = power(c, 8, 1.0, a)
            qr = dve.op(lambda e, c=c: e.tensor_scalar(c[:, 0:4], c[:, 0:4], 128.0 ** -0.5, None, ALU.mult), r)
            s_ = slice(4 * ti, 4 * ti + 4)
            qn = scale(N[:, ti, 0:4, :], N[:, ti, 0:4, :], c[:, 0:4], 128, qr)
            kn = scale(N[:, ti, 4:8, :], N[:, ti, 4:8, :], c[:, 4:8], 128, r)
            kb = scale(KB[:, ti], N[:, ti, 4:8, :], beta[:, ti, :], 128, kn, b_ok, *conv_end, dt_ok)
            qd = scale(QD[:, ti], N[:, ti, 0:4, :], eg[:, s_], 128, qn, e1)
            vb_ok.append(scale(N[:, ti, 8:12, :], N[:, ti, 8:12, :], beta[:, ti, :], 128, n_ok[(ti, 2)], b_ok))
            kg_ok.append(scale(KG[:, ti], N[:, ti, 4:8, :], bg[:, s_], 128, kn, bg_ok))
            kd_ok.append(scale(KD[:, ti], N[:, ti, 4:8, :], ed[:, s_], 128, kn, e2))
            fill(FILLS[2])
            turned = list(n_ok.values())
            for w, (src, a) in enumerate(((N[:, ti, 0:4], qn), (N[:, ti, 4:8], kn), (KB[:, ti], kb), (QD[:, ti], qd))):
                t4_ok.append(turn4([src[:, h, :] for h in range(4)], T4[:, w, :, ti * 128:ti * 128 + 128], [a] + turned,
                                   eng=dve if w % 2 else None))
        LT = BTf[:, 0:1024].rearrange("p (r c) -> p r c", r=8)
        QK = BTf[:, 1024:2048].rearrange("p (r c) -> p r c", r=8)
        lt_ok, qk_ok = [], []
        for w, dst, ok in ((2, LT, lt_ok), (0, QK, qk_ok)):
            for ti in range(2):
                b = bk.take()
                for h in range(4):
                    f = lambda e, b=b, h=h, ti=ti, w=w: e.matmul(
                        PS[:, b, h * 128:h * 128 + 128], T4[:, 1, h, ti * 128:ti * 128 + 128],
                        T4[:, w, h, ti * 128:ti * 128 + 128], start=True, stop=True)
                    if h < 3:
                        pe.quiet(f, *((*t4_ok, *bk.read[b]) if h == 0 else ()))
                    else:
                        tk = pe.op(f)
                r = dve.op(lambda e, b=b, dst=dst, ti=ti: e.tensor_tensor(
                    dst[:, 4 * ti:4 * ti + 4, :], PS[:, b, :].rearrange("p (h c) -> p h c", h=4),
                    DT[:, 4 * ti:4 * ti + 4, :], ALU.mult), tk, dt_ok)
                bk.read[b] = [r]
                ok.append(r)

        X, XT, T1, M0, M1 = (v.rearrange("p (r c) -> p r c", r=8) for v in
                             (*(R4[:, 1024 * q:1024 * q + 1024] for q in range(4)), BTf[:, 2048:3072]))
        r4_free = [t4_ok[-1], t4_ok[-2], t4_ok[-3], t4_ok[-4], t4_ok[2], t4_ok[3]]
        id8 = bc(ident, 1, 8)

        def level_mask(n, dst, *after):
            return pool.op(lambda e: e.tensor_tensor(dst, LT, bc(KT[:, K_LEV + 128 * n:K_LEV + 128 * n + 128], 1, 8), ALU.mult), *after)

        m_ok = level_mask(0, M0, *lt_ok, *r4_free)
        m_next = level_mask(1, M1)
        xt_ok = [dve.op(lambda e: e.tensor_tensor(XT, id8, M0, ALU.subtract), m_ok, *r4_free)]
        x_ok = []
        for q in range(2):
            b = bk.take()
            for r in range(4):
                f = lambda e, b=b, r=r, q=q: e.transpose(PS[:, b, r * 128:r * 128 + 128], M0[:, 4 * q + r, :], ident)
                if r < 3:
                    pe.quiet(f, *((m_ok, *bk.read[b]) if r == 0 else ()))
                else:
                    tk = pe.op(f)
            x = dve.op(lambda e, b=b, q=q: e.tensor_tensor(
                X[:, 4 * q:4 * q + 4, :], bc(ident, 1, 4), PS[:, b, :].rearrange("p (r c) -> p r c", r=4), ALU.subtract), tk, *r4_free)
            bk.read[b] = [x]
            x_ok.append(x)

        def eight(lhs, rhs, *after):
            out = []
            for q in range(2):
                b = bk.take()
                for r in range(4):
                    f = lambda e, b=b, r=r, q=q: e.matmul(PS[:, b, r * 128:r * 128 + 128], lhs(4 * q + r), rhs(4 * q + r), start=True, stop=True)
                    if r < 3:
                        pe.quiet(f, *((*after, *bk.read[b]) if r == 0 else ()))
                    else:
                        tk = pe.op(f)
                out.append((b, tk))
            return out

        mt = [tk]
        for n in range(1, 6):
            M = (M0, M1)[n % 2]
            fill(FILLS[3])
            out = eight(lambda r, M=M: M[:, r, :], lambda r: X[:, r, :], m_next, *x_ok)
            t1_ok = []
            for q, (b, tk) in enumerate(out):
                dst = T1[:, 4 * q:4 * q + 4, :]
                src = PS[:, b, :].rearrange("p (r c) -> p r c", r=4)
                if q == 0:
                    r = act.op(lambda e, dst=dst, src=src: e.copy(dst, src), tk, *mt, *r4_free)
                else:
                    r = dve.op(lambda e, dst=dst, src=src: e.tensor_copy(dst, src), tk, *mt)
                bk.read[b] = [r]
                t1_ok.append(r)
            if n < 5:
                m_next = level_mask(n + 1, (M1, M0)[n % 2], tk, *mt)
            fill(FILLS[4])
            outT = eight(lambda r: T1[:, r, :], lambda r: XT[:, r, :], *t1_ok, *xt_ok)
            new_x = []
            if n < 5:
                outX = eight(lambda r: XT[:, r, :], lambda r: T1[:, r, :])
                for q, (b, tk) in enumerate(outX):
                    v = X[:, 4 * q:4 * q + 4, :]
                    r = dve.op(lambda e, v=v, b=b: e.tensor_tensor(v, v, PS[:, b, :].rearrange("p (r c) -> p r c", r=4), ALU.subtract), tk)
                    bk.read[b] = [r]
                    new_x.append(r)
                mt = [tk]
            last = outX[1][1] if n < 5 else outT[1][1]
            new_t = []
            for q, (b, tk) in enumerate(outT):
                v = XT[:, 4 * q:4 * q + 4, :]
                r = dve.op(lambda e, v=v, b=b: e.tensor_tensor(v, v, PS[:, b, :].rearrange("p (r c) -> p r c", r=4), ALU.subtract), tk, last)
                bk.read[b] = [r]
                new_t.append(r)
            x_ok, xt_ok = new_x, new_t

        U = M0
        WT = M1
        inv_end = [new_t[0], new_t[1], last]
        out = eight(lambda r: XT[:, r, :], lambda r: N[:, r // 4, 8 + r % 4, :], *xt_ok, *vb_ok)
        u_ok, w_ok = [], []
        for q, (b, tk) in enumerate(out):
            r = act.op(lambda e, b=b, q=q: e.copy(U[:, 4 * q:4 * q + 4, :], PS[:, b, :].rearrange("p (r c) -> p r c", r=4)), tk, *inv_end)
            bk.read[b] = [r]
            u_ok.append(r)
        out = eight(lambda r: KG[:, r // 4, r % 4, :], lambda r: XT[:, r, :], *kg_ok)
        for q, (b, tk) in enumerate(out):
            r = dve.op(lambda e, b=b, q=q: e.tensor_copy(WT[:, 4 * q:4 * q + 4, :], PS[:, b, :].rearrange("p (r c) -> p r c", r=4)), tk, *inv_end)
            bk.read[b] = [r]
            w_ok.append(r)
        uw_end = tk

        ST = R4[:, 0:512].rearrange("p (h d) -> p h d", h=4)
        SD = R4[:, 512:1024].rearrange("p (h d) -> p h d", h=4)
        VN = R4[:, 2048:2560].rearrange("p (h d) -> p h d", h=4)
        ON = KG
        s_t = dve.op(lambda e: e.memset(ST, 0.0), *inv_end)
        on_ok = [[], []]
        vn_free = []
        oq_free = [uw_end]
        for c in range(4):
            ti, r0 = c // 2, 64 * (c % 2)
            rows = slice(r0, r0 + 64)
            b = bk.take()
            for h in range(4):
                f = lambda e, b=b, h=h, ti=ti, rows=rows, r0=r0: e.matmul(
                    PS[rows, b, h * 128:h * 128 + 128], WT[:, 4 * ti + h, r0:r0 + 64], ST[:, h, :], start=True, stop=True)
                if h < 3:
                    pe.quiet(f, *((s_t, *w_ok, *bk.read[b]) if h == 0 else ()))
                else:
                    tk = pe.op(f)
            vn = dve.op(lambda e, b=b, ti=ti, rows=rows: e.tensor_tensor(
                VN[rows], U[rows, 4 * ti:4 * ti + 4, :], PS[rows, b, :].rearrange("p (h d) -> p h d", h=4), ALU.subtract),
                tk, *u_ok, *vn_free, *inv_end)
            bk.read[b] = [vn]
            ob_ = bk.take()
            sb_ = bk.take()
            if c < 3:
                sd = dve.op(lambda e, c=c, ti=ti: e.tensor_tensor(
                    SD, ST, bc(egl[:, 8 * (c % 2) + 4 * ti:8 * (c % 2) + 4 * ti + 4], 2, 128), ALU.mult), s_t, e3, *inv_end)
                for h in range(4):
                    f = lambda e, h=h, ti=ti, rows=rows, sb_=sb_: e.matmul(
                        PS[:, sb_, h * 128:h * 128 + 128], KD[rows, ti, h, :], VN[rows, h, :], start=True, stop=True)
                    if h < 3:
                        pe.quiet(f, *((vn, *kd_ok, *bk.read[sb_]) if h == 0 else ()))
                    else:
                        tk = pe.op(f)
            for h in range(4):
                pe.quiet(lambda e, h=h, ti=ti, r0=r0, rows=rows, ob_=ob_: e.matmul(
                    PS[rows, ob_, h * 128:h * 128 + 128], T4[:, 3, h, ti * 128 + r0:ti * 128 + r0 + 64], ST[:, h, :],
                    start=True, stop=False), *((vn, s_t, *bk.read[ob_]) if h == 0 else ()))
                f = lambda e, h=h, ti=ti, r0=r0, rows=rows, ob_=ob_: e.matmul(
                    PS[rows, ob_, h * 128:h * 128 + 128], QK[rows, 4 * ti + h, r0:r0 + 64], VN[rows, h, :],
                    start=False, stop=True)
                if h < 3:
                    pe.quiet(f, *qk_ok)
                else:
                    tko = pe.op(f)
            vn_free = [tko]
            if c < 3:
                s_t = dve.op(lambda e, sb_=sb_: e.tensor_tensor(
                    ST, SD, PS[:, sb_, :].rearrange("p (h d) -> p h d", h=4), ALU.add), tk, sd, tko)
                bk.read[sb_] = [s_t]
            r = act.op(lambda e, ti=ti, rows=rows, ob_=ob_: e.copy(
                ON[rows, ti, :, :], PS[rows, ob_, :].rearrange("p (h d) -> p h d", h=4)), tko, *oq_free)
            bk.read[ob_] = [r]
            on_ok[ti].append(r)
            fill(FILLS[5])
        BT = BTf.rearrange("p (i h c) -> p i h c", i=4, h=4)
        bt_ok = {}
        dn_end = []
        for ti in range(2):
            c, a = sums(ON[:, ti], 4, 128, *on_ok[ti])
            r = power(c, 4, 1.0 / 128, a)
            a = scale(ON[:, ti], ON[:, ti], c, 128, r)
            a = dve.op(lambda e, ti=ti: e.tensor_tensor(ON[:, ti], ON[:, ti], Z[:, ti, :].rearrange("p (h d) -> p h d", h=4), ALU.mult), a, z_ok[ti])
            fill(1)
            bt_ok[(0, ti)] = turn4([ON[:, ti, h, :] for h in range(4)], BT[:, 0, :, ti * 128:ti * 128 + 128], [a], VW[:, W_OUTG:W_OUTG + 1])
            dn_end.append(bt_ok[(0, ti)])
        while bulk:
            fill(1)
        dn_end += [(pe.sem, pe.n), (dve.sem, dve.n), (act.sem, act.n), (pool.sem, pool.n)]

        GA_ = R4[:, 0:4096].rearrange("p (i m c) -> p i m c", i=2, m=8)
        GB_ = R1.rearrange("p (i m c) -> p i m c", i=2, m=8)
        gate_ok = {}
        gs = {}

        def gate_unit(n):
            def unit():
                b, tk = tile_hT()
                i, m = divmod(n, 8)
                g_ = (GA_ if i < 2 else GB_)[:, i % 2, m, :]
                gate_ok[n] = act.op(lambda e: e.activation(g_, PS[:, b, 0:256], ACT.Tanh, scale=0.5), tk, *dn_end)
                bk.read[b] = [gate_ok[n]]
            return unit

        for n in range(32):
            bulk.append(gate_unit(n))

        FT = KDT.rearrange("p (q h c) -> p q h c", q=2, h=4)
        ft_ok = []
        for ti in range(2):
            for q in range(2):
                v4 = F[:, q, ti, :].rearrange("p (h d) -> p h d", h=4)
                c, a = sums(v4, 4, 128, f_ok[(ti, q)])
                r = power(c, 4, 1.0 / 128, a)
                a = scale(v4, v4, c, 128, r)
                fill(1)
                ft_ok.append(turn4([F[:, q, ti, 128 * h:128 * h + 128] for h in range(4)],
                                   FT[:, q, :, ti * 128:ti * 128 + 128], [a, *dn_end], VW[:, W_FQ + q:W_FQ + q + 1]))

        c_sw = [sem("c_sw"), 0]
        Lsw = pool.dma(lambda e: e.dma_start(SW, t["sgw"]), c_sw, *moe_end)
        sw_ok = dve.op(lambda e: e.tensor_tensor(SW, SW, bc(tri, 1, 4), ALU.mult), Lsw)
        for ti in range(2):
            v4 = SV[:, ti, :].rearrange("p (g d) -> p g d", g=4)
            c, a = sums(v4, 4, 128, sv_ok[ti])
            r = power(c, 4, 1.0 / 128, a)
            a = scale(v4, v4, c, 128, r)
            a = dve.op(lambda e, ti=ti: e.tensor_tensor(SV[:, ti, :], SV[:, ti, :], VW[:, W_SGG:W_SGG + 512], ALU.mult), a)
            b = bk.take()
            for g in range(4):
                f = lambda e, b=b, g=g, ti=ti: e.matmul(
                    PS[:, b, g * 128:g * 128 + 128], SW[:, g, :], SV[:, ti, g * 128:g * 128 + 128], start=True, stop=True)
                if g < 3:
                    pe.quiet(f, *((a, sw_ok, *bk.read[b]) if g == 0 else ()))
                else:
                    tk = pe.op(f)
            for g in range(4):
                u = SU[:, ti, g * 128:g * 128 + 128]
                r = dve.op(lambda e, b=b, g=g, u=u: e.scalar_tensor_tensor(
                    u, PS[:, b, g * 128:g * 128 + 128], VW[:, W_SGB + g:W_SGB + g + 1], u, ALU.add, ALU.mult), tk, su_ok[ti])
            bk.read[b] = [r]
            bt_ok[(2, ti)] = turn4([SU[:, ti, g * 128:g * 128 + 128] for g in range(4)], BT[:, 2, :, ti * 128:ti * 128 + 128], [r])

        CT = BTf[:, 1024:1792].rearrange("p (c k) -> p c k", c=3)
        Nf = NN
        MQ = Nf[:, 0:1536].rearrange("p (t h d) -> p t h d", t=2, h=4)
        MK = Nf[:, 1536:2560].rearrange("p (t h d) -> p t h d", t=2, h=4)
        MR = Nf[:, 2560:3072].rearrange("p (t h d) -> p t h d", t=2, h=4)
        MV = KG
        Q1, Q2 = (Ff[:, 1024 * q:1024 * q + 1024].rearrange("p (h c) -> p h c", h=4) for q in range(2))
        K1, K2 = (SUV[:, 1024 * q:1024 * q + 1024].rearrange("p (h c) -> p h c", h=4) for q in range(2))
        heads_free = [(pe.sem, pe.n), (dve.sem, dve.n)]
        ct_ok = []
        for ti in range(2):
            cq, ckv = MS[:, ti, 0:256], MS[:, ti, 256:384]
            c1, a1 = sums(MS[:, ti, 0:256].unsqueeze(1), 1, 256, ms_ok[ti])
            c2, a2 = sums(MS[:, ti, 256:384].unsqueeze(1), 1, 128, ms_ok[ti])
            r1 = power(c1, 1, 1.0 / 256, a1)
            r2 = power(c2, 1, 1.0 / 128, a2)
            a1 = dve.op(lambda e, cq=cq, c1=c1: e.tensor_scalar(cq, cq, c1, None, ALU.mult), r1)
            a2 = dve.op(lambda e, ckv=ckv, c2=c2: e.tensor_scalar(ckv, ckv, c2, None, ALU.mult), r2)
            b = bk.take()
            for i in range(3):
                f = lambda e, b=b, i=i, ti=ti: e.transpose(PS[:, b, i * 128:i * 128 + 128], MS[:, ti, i * 128:i * 128 + 128], ident)
                if i < 2:
                    pe.quiet(f, *((a1, a2, *bk.read[b]) if i == 0 else ()))
                else:
                    tk = pe.op(f)
            for i in range(3):
                r = dve.op(lambda e, b=b, i=i, ti=ti: e.tensor_scalar(
                    CT[:, i, ti * 128:ti * 128 + 128], PS[:, b, i * 128:i * 128 + 128], VW[:, W_QN + i:W_QN + i + 1], None, ALU.mult), tk, *dn_end)
            bk.read[b] = [r]
            ct_ok.append(r)
        uq = [raw_piece(t["w2_uq"][k]) for k in range(2)]
        ukv = raw_piece(t["w2_ukv"])
        mq_ok, mk_ok, mv_ok = {}, {}, {}
        for ti in range(2):
            for nb in range(2):
                b, tk = tile_T(None, 0, 2, lambda k, ti=ti: CT[:, k, ti * 128:ti * 128 + 128],
                               lambda k, nb=nb: uq[k][1][:, 384 * nb:384 * nb + 384], 384, uq[0][2], uq[1][2], *ct_ok)
                r = act.op(lambda e, b=b, ti=ti, nb=nb: e.copy(
                    MQ[:, ti, 2 * nb:2 * nb + 2, :], PS[:, b, 0:384].rearrange("p (h d) -> p h d", h=2)), tk, *dn_end)
                bk.read[b] = [r]
                mq_ok[(ti, nb)] = r
        raw_used[uq[0][0]] = raw_used[uq[1][0]] = tk
        for ti in range(2):
            for nb in range(2):
                b, tk = tile_T(None, 0, 1, lambda k, ti=ti: CT[:, 2, ti * 128:ti * 128 + 128],
                               lambda k, nb=nb: ukv[1][:, 512 * nb:512 * nb + 512], 512, ukv[2])
                src = PS[:, b, :].rearrange("p (h d) -> p h d", h=2)
                r = act.op(lambda e, src=src, ti=ti, nb=nb: e.copy(MK[:, ti, 2 * nb:2 * nb + 2, :], src[:, :, 0:128]), tk, *dn_end)
                r2 = act.op(lambda e, src=src, ti=ti, nb=nb: e.copy(MV[:, ti, 2 * nb:2 * nb + 2, :], src[:, :, 128:256]), tk, *dn_end)
                bk.read[b] = [r2]
                mk_ok[(ti, nb)] = r
                mv_ok[(ti, nb)] = r2
        raw_used[ukv[0]] = tk
        gq, gk = VW[:, W_QG:W_QG + 192], VW[:, W_KG:W_KG + 192]
        rt_free = [[]]

        def rope_nat(x, ti, *after):
            w = [RT[:, 128 * i:128 * i + 128].rearrange("p (h d) -> p h d", h=4) for i in range(4)]
            cs, sn = bc(cosN[:, ti, :], 1, 4), bc(sinN[:, ti, :], 1, 4)
            x1, x2 = x[:, :, 0:32], x[:, :, 32:64]
            p = []
            for i, (a_, b_) in enumerate(((x1, cs), (x2, sn), (x2, cs), (x1, sn))):
                p.append(dve.op(lambda e, i=i, a_=a_, b_=b_: e.tensor_tensor(w[i], a_, b_, ALU.mult), k_tab, *after, *rt_free[0]))
            a = dve.op(lambda e: e.tensor_tensor(x1, w[0], w[1], ALU.subtract), *p)
            b = dve.op(lambda e: e.tensor_tensor(x2, w[2], w[3], ALU.add), *p)
            rt_free[0] = [b]
            return [a, b]

        qk2_ok = []
        for ti in range(2):
            c, a = sums(MQ[:, ti], 4, 192, mq_ok[(ti, 0)], mq_ok[(ti, 1)])
            r = power(c, 4, 1.0 / 192, a)
            a = scale(MQ[:, ti], MQ[:, ti], c, 192, r)
            a = dve.op(lambda e, ti=ti: e.tensor_tensor(MQ[:, ti], MQ[:, ti], bc(gq, 1, 4), ALU.mult), a)
            rp = rope_nat(MQ[:, ti, :, 128:192], ti, a)
            fill(1)
            tsl = slice(ti * 128, ti * 128 + 128)
            qk2_ok.append(turn4([MQ[:, ti, h, 0:128] for h in range(4)], Q1[:, :, tsl], [a, *heads_free]))
            qk2_ok.append(turn4([MQ[:, ti, h, 128:192] for h in range(4)], Q2[0:64, :, tsl], [*rp, *heads_free], rows=64))
            kr = MS[:, ti, 384:448]
            c, a = sums(MK[:, ti], 4, 128, mk_ok[(ti, 0)], mk_ok[(ti, 1)])
            c2, a2 = sums(kr.unsqueeze(1), 1, 64, ms_ok[ti])
            a = dve.op(lambda e, c=c, c2=c2: e.tensor_scalar(c, c, c2, None, ALU.add), a, a2)
            r = power(c, 4, 1.0 / 192, a)
            a = scale(MK[:, ti], MK[:, ti], c, 128, r)
            a = dve.op(lambda e, ti=ti: e.tensor_tensor(MK[:, ti], MK[:, ti], bc(gk[:, 0:128], 1, 4), ALU.mult), a)
            b = dve.op(lambda e, ti=ti, c=c, kr=kr: e.tensor_tensor(MR[:, ti], bc(kr, 1, 4), bc(c, 2, 64), ALU.mult), r, *dn_end)
            b = dve.op(lambda e, ti=ti: e.tensor_tensor(MR[:, ti], MR[:, ti], bc(gk[:, 128:192], 1, 4), ALU.mult), b)
            rp = rope_nat(MR[:, ti], ti, b)
            fill(1)
            qk2_ok.append(turn4([MK[:, ti, h, :] for h in range(4)], K1[:, :, tsl], [a, *heads_free]))
            qk2_ok.append(turn4([MR[:, ti, h, :] for h in range(4)], K2[0:64, :, tsl], [*rp, *heads_free], rows=64))

        DM = Z.rearrange("p t c -> p (t c)").rearrange("p (j t c) -> p j t c", j=2, t=2)
        sr = small(8)
        sc_free, pt_free = [[], []], [[], []]
        dm_ok, dm_free = {}, [[], []]
        MB = KT[:, K_MB:K_MB + 256]
        fr_free = [[]]

        def row_decay(h):
            j = h % 2
            R0 = RT[:, 0:256]
            R1_ = RT[:, 256:384]
            a = dve.op(lambda e: e.tensor_scalar(R0, KT[:, K_TRI:K_TRI + 256], lf[:, 0, h:h + 1], None, ALU.mult), l_ok, *fr_free[0], *rt_free[0])
            c = dve.op(lambda e: e.tensor_scalar(R1_, tri, lf[:, 1, h:h + 1], None, ALU.mult), l_ok, *fr_free[0], *rt_free[0])
            b = bk.take()
            pe.quiet(lambda e: e.matmul(PS[:, b, 0:256], one, R0, start=True, stop=False), a, c, *bk.read[b])
            tk = pe.op(lambda e: e.matmul(PS[:, b, 128:256], one, R1_, start=False, stop=True))
            fr_free[0] = [tk]
            r = []
            for ti in range(2):
                nk = 128 * ti + 128
                r.append(dve.op(lambda e, ti=ti, nk=nk: e.scalar_tensor_tensor(
                    DM[:, j, ti, 0:nk], PS[:, b, 0:nk], GC[:, 32 + 4 * ti + h:33 + 4 * ti + h], MB[:, 256 - nk:256],
                    ALU.subtract, ALU.subtract, reverse1=True), tk, gc_ok, *dm_free[j]))
            bk.read[b] = r
            dm_ok[h] = r

        def score(u):
            fox, h, ti = u
            nk = 128 * ti + 128
            j = cnt[0] % 2
            cnt[0] += 1
            q0 = slice(ti * 128, ti * 128 + 128)
            b = bk.take()
            if fox:
                if ti == 0:
                    row_decay(h)
                tk = pe.op(lambda e: e.matmul(PS[:, b, 0:nk], FT[:, 0, h, q0], FT[:, 1, h, 0:nk], start=True, stop=True), *ft_ok, *bk.read[b])
                bias, sc, w = DM[:, h % 2, ti, 0:nk], 128.0 ** -0.5, dm_ok[h]
            else:
                pe.quiet(lambda e: e.matmul(PS[:, b, 0:nk], Q1[:, h, q0], K1[:, h, 0:nk], start=True, stop=False), *qk2_ok, *bk.read[b])
                tk = pe.op(lambda e: e.matmul(PS[:, b, 0:nk], Q2[0:64, h, q0], K2[0:64, h, 0:nk], start=False, stop=True))
                bias, sc, w = MB[:, 256 - nk:256], 192.0 ** -0.5, []
            S_ = SC[:, j, 0:nk]
            m, l, rc = sr[:, 4 * j:4 * j + 1], sr[:, 4 * j + 1:4 * j + 2], sr[:, 4 * j + 2:4 * j + 3]
            a = dve.op(lambda e: e.scalar_tensor_tensor(S_, PS[:, b, 0:nk], sc, bias, ALU.mult, ALU.add), tk, *w, *sc_free[j])
            bk.read[b] = [a]
            if fox:
                dm_free[h % 2] = [a]
            a = dve.op(lambda e: e.tensor_reduce(m, S_, AX, ALU.max, negate=True), a)
            a = act.op(lambda e: e.activation(S_, S_, ACT.Exp, bias=m, scale=1.0, accum_out=l), a)
            a = dve.op(lambda e: e.reciprocal(rc, l), a)
            a = dve.op(lambda e: e.tensor_scalar(S_, S_, rc, None, ALU.mult), a)
            return (u, j, a)

        oacc = {}

        def value(state):
            (fox, h, ti), j, tok = state
            b = bk.take()
            for kt in range(ti + 1):
                f = lambda e, kt=kt: e.transpose(PS[:, b, kt * 128:kt * 128 + 128], SC[:, j, kt * 128:kt * 128 + 128], ident)
                w = (tok, *bk.read[b]) if kt == 0 else ()
                if kt < ti:
                    pe.quiet(f, *w)
                else:
                    tk = pe.op(f, *w)
            sc_free[j] = [tk]
            nk = 128 * ti + 128
            r = act.op(lambda e: e.copy(PT[:, j, 0:nk], PS[:, b, 0:nk]), tk, *pt_free[j])
            bk.read[b] = [r]
            b2 = bk.take()
            for kt in range(ti + 1):
                vv = F[:, 2, kt, 128 * h:128 * h + 128] if fox else MV[:, kt, h, :]
                f = lambda e, kt=kt, vv=vv: e.matmul(PS[:, b2, 0:128], vv, PT[:, j, kt * 128:kt * 128 + 128], start=(kt == 0), stop=(kt == ti))
                w = (r, *([f_ok[(0, 2)], f_ok[(1, 2)]] if fox else mv_ok.values()), *bk.read[b2]) if kt == 0 else ()
                if kt < ti:
                    pe.quiet(f, *w)
                else:
                    tk = pe.op(f, *w)
            pt_free[j] = [tk]
            br = 3 if fox else 1
            r = act.op(lambda e: e.copy(BT[:, br, h, ti * 128:ti * 128 + 128], PS[:, b2, 0:128]), tk)
            bk.read[b2] = [r]
            bt_ok[(br, h, ti)] = r

        cnt = [0]
        prev = None
        for u in [(True, h, ti) for h in range(4) for ti in range(2)] + [(False, h, ti) for h in range(4) for ti in range(2)]:
            st_ = score(u)
            fill(1)
            if prev is not None:
                value(prev)
            prev = st_
        fill(1)
        value(prev)
        while bulk:
            fill(1)

        gate_end = [(dve.sem, dve.n), (pe.sem, pe.n), (act.sem, act.n), (pool.sem, pool.n)]
        MT = NN[:, 0:2048].rearrange("p (m c) -> p m c", m=8)
        TM = SC
        tm_free = [list(gate_end), list(gate_end)]
        n = 0
        mt_ok = [None] * 8
        BH = hr.rearrange("p q (j c) -> p q j c", j=2)
        bh_free = [[], []]
        four = Banks(range(4))
        for b in range(6):
            if b < 4:
                four.read[b] = bk.read[b]
            else:
                open_read[b] = bk.read[b]
        bk = four

        def split_branch(i):
            src = BTf[:, 1024 * i:1024 * i + 1024]
            hi, lo = BH[:, 0, i % 2, :], BH[:, 1, i % 2, :]
            ok = [r for key, r in bt_ok.items() if key[0] == i]
            a = act.op(lambda e: e.copy(hi, src), *ok, *gate_end, *bh_free[i % 2])
            return [a, dve.op(lambda e: e.tensor_tensor(lo, src, hi.bitcast(F32), ALU.subtract), a)]

        ready = [split_branch(0), split_branch(1)]
        for i in range(4):
            B_ = [BH[:, p, i % 2, :].rearrange("p (k c) -> p k c", k=4) for p in range(2)]
            for m in range(8):
                if m % 2 == 0:
                    hi, lo, ok = piece()
                    v = [x.rearrange("p (m k c) -> p m k c", m=2, k=4) for x in (hi, lo)]
                b, tk = tile3(4, lambda p, k, v=v, m=m: v[p][:, m % 2, k, :], lambda p, k, B_=B_: B_[p][:, k, :], 256, *ok, *ready[i])
                if m % 2 == 1:
                    release(tk)
                g_ = (GA_ if i < 2 else GB_)[:, i % 2, m, :]
                if i == 0:
                    mt_ok[m] = dve.op(lambda e, b=b, g_=g_, m=m: e.scalar_tensor_tensor(
                        MT[:, m, :], g_, 1.0, PS[:, b, 0:256], ALU.add, ALU.mult), tk, *gate_end)
                    bk.read[b] = [mt_ok[m]]
                else:
                    j = n % 2
                    n += 1
                    c = dve.op(lambda e, b=b, g_=g_, j=j: e.scalar_tensor_tensor(
                        TM[:, j, :], g_, 1.0, PS[:, b, 0:256], ALU.add, ALU.mult), tk, *tm_free[j])
                    bk.read[b] = [c]
                    mt_ok[m] = pool.op(lambda e, m=m, j=j: e.tensor_tensor(MT[:, m, :], MT[:, m, :], TM[:, j, :], ALU.add), mt_ok[m], c)
                    tm_free[j] = [mt_ok[m]]
            bh_free[i % 2] = [tk]
            if i < 2:
                ready.append(split_branch(i + 2))
        MTh, MTl = (hr[:, p, :].rearrange("p (m c) -> p m c", m=8) for p in range(2))
        mts = []
        for m in range(8):
            a = act.op(lambda e, m=m: e.mul(MTh[:, m, :], MT[:, m, :], 0.5), mt_ok[m], tk)
            mts.append((a, dve.op(lambda e, m=m: e.scalar_tensor_tensor(
                MTl[:, m, :], MT[:, m, :], 0.5, MTh[:, m, :].bitcast(F32), ALU.mult, ALU.subtract), a)))

        quad = {(ti, db): 4 + 2 * ti + db for ti in range(2) for db in range(2)}
        two = [slice(0, 512), slice(512, 1024)]
        toks = {}
        for c in range(8):
            hi, lo, ok = piece()
            tk = rows3(quad, c == 0, c == 7, lambda p, ti, c=c: (MTh, MTl)[p][:, c, ti * 128:ti * 128 + 128],
                       lambda p, hi=hi, lo=lo: (hi, lo)[p], two, (*ok, *mts[c]), toks)
            release(tk)
        h_ok = {}
        for (ti, db), b in quad.items():
            hv = H[:, ti, db * 512:db * 512 + 512]
            h_ok[(ti, db)] = dve.op(lambda e, hv=hv, b=b: e.tensor_tensor(hv, hv, PS[:, b, :], ALU.add), toks[(ti, db)])
            open_read[b] = [h_ok[(ti, db)]]
        merge_end = [(dve.sem, dve.n), (pe.sem, pe.n), (act.sem, act.n), (pool.sem, pool.n)]

        mid.close()
        fh = sb1("fh", 16384, F32R, second)[:, :].rearrange("p (q m c) -> p q m c", q=2, m=32)
        late = sb1("late", 2048 + 1024 + 4096, F32, second)
        XB2 = late[:, 0:2048].rearrange("p (t c) -> p t c", t=2)
        tmp2 = late[:, 2048:3072]
        RL = late[:, 3072:7168].rearrange("p (j q c) -> p j q c", j=8, q=2)
        h2_ok = []
        for ti in range(2):
            r, x = rms2(XB2, ti, 4 + ti, h_ok[(ti, 0)], h_ok[(ti, 1)], *merge_end)
            a = dve.op(lambda e, ti=ti, x=x: e.tensor_scalar(XB2[:, ti, :], H[:, ti, :], x, None, ALU.mult), r)
            h2_ok += turn_two(XB2, ti, vec[:, V_N2:V_N2 + 8], tmp2, [a, *merge_end, *h2_ok])
        ff_ok = []
        rl_free = [[] for _ in range(8)]
        for m in range(32):
            b, tk = tile_hT(*h2_ok)
            j = m % 8
            r_, s_ = RL[:, j, 0, :], RL[:, j, 1, :]
            hi, lo = fh[:, 0, m, :], fh[:, 1, m, :]
            a = act.op(lambda e, b=b, r_=r_: e.activation(r_, PS[:, b, 0:256], ACT.Relu), tk, *merge_end, *rl_free[j])
            bk.read[b] = [a]
            a = dve.op(lambda e, r_=r_, s_=s_: e.tensor_tensor(s_, r_, r_, ALU.mult), a)
            c = act.op(lambda e, s_=s_, hi=hi: e.copy(hi, s_), a, *merge_end)
            a = dve.op(lambda e, s_=s_, hi=hi, lo=lo: e.tensor_tensor(lo, s_, hi.bitcast(F32), ALU.subtract), c)
            rl_free[j] = [a]
            ff_ok.append((c, a))
        toks = {}
        for m in range(32):
            hi, lo, ok = piece()
            tk = rows3(quad, m == 0, m == 31, lambda p, ti, m=m: fh[:, p, m, ti * 128:ti * 128 + 128],
                       lambda p, hi=hi, lo=lo: (hi, lo)[p], two, (*ok, *ff_ok[m]), toks)
            release(tk)
        for (ti, db), b in quad.items():
            hv = H[:, ti, db * 512:db * 512 + 512]
            r = dve.op(lambda e, hv=hv, b=b: e.tensor_tensor(hv, hv, PS[:, b, :], ALU.add), toks[(ti, db)])
            c_o = [sem(f"c_o{ti}{db}"), 0]
            outs.append(act.dma(lambda e, hv=hv, ti=ti, db=db: e.dma_start(t["out"][:, ti, db * 512:db * 512 + 512], hv), c_o, r))
        act.quiet(None, *outs)

        for n, (src, after) in enumerate(stream2):
            dst = raw[:, (n % RAW) * 1024:(n % RAW) * 1024 + src.shape[1]]
            sp.dma(lambda e, dst=dst, src=src: e.dma_start(dst, src), raw_sem[n % RAW], *after())

        block = ctx.enter_context(nc.Block())

        @block.sync
        def _(e):
            sp.emit(e)

        @block.scalar
        def _(e):
            act.emit(e)

        @block.vector
        def _(e):
            dve.emit(e)

        @block.gpsimd
        def _(e):
            pool.emit(e)

        @block.tensor
        def _(e):
            pe.emit(e)


def pack_T(w):
    K, N = w.shape
    return np.ascontiguousarray(w.reshape(K // 128, 128, N // 256, 256).transpose(2, 1, 0, 3)).reshape(N // 256, 128, -1)


def pack_N(w):
    K, N = w.shape
    a = w.reshape(K // 512, 4, 128, N // 512, 512).transpose(3, 0, 2, 1, 4)
    return np.ascontiguousarray(a).reshape(-1, 128, 2048)


def tiles(w):
    return np.ascontiguousarray(w.reshape(8, 128, -1, 128).transpose(2, 1, 0, 3)).reshape(-1, 128, 1024)


def blocks(w):
    return np.ascontiguousarray(w.reshape(4, 2, 128, -1, 512).transpose(3, 0, 2, 1, 4)).reshape(-1, 128, 1024)


def pack_R(w):
    K, N = w.shape
    return np.ascontiguousarray(w.reshape(K // 256, 2, 128, N).transpose(0, 2, 1, 3)).reshape(-1, 128, 2 * N)


def col(v):
    return np.ascontiguousarray(v.reshape(-1, 128).T)


def layout(i):
    a = {}
    a["x"] = np.ascontiguousarray(i["x"][0].reshape(2, 128, D).transpose(1, 0, 2))
    a["meta"] = np.ascontiguousarray(i["meta_tokens"])
    a["cst"] = constants()
    w = i["w_in"][0]
    order = [w[:, 512:1024], w[:, 0:512]]
    tri = [w[:, o + 128 * m:o + 128 * m + 128] for m in range(4) for o in (1536, 2560, 2048)]
    a["w_in"] = np.concatenate([pack_T(order[0]), pack_T(order[1]), pack_N(w[:, 1024:1536]), pack_T(np.concatenate(tri, 1))])
    a["w_out"] = pack_R(i["w_out"][0])
    for n in ("w_gate", "w_up", "w_down"):
        a[n] = np.ascontiguousarray(i[n][0])
    v = np.zeros((P, NVEC), np.float32)
    v[:, V_MIXG:V_MIXG + 8] = col(i["mix_norm_g"][0])
    cw = i["conv_w"][0]
    for m in range(4):
        for k in range(3):
            v[:, V_CONV + 3 * m + k] = cw[k, 128 * m:128 * m + 128]
    v[:, V_SUB] = i["attn_subln_g"][0]
    for j, n in enumerate(("lambda_q1", "lambda_k1", "lambda_q2", "lambda_k2")):
        v[:, V_LAM + 64 * j:V_LAM + 64 * j + 64] = i[n][0][None, :]
    v[:, V_WR:V_WR + 128] = i["w_router"][0].reshape(8, 128, 16).transpose(1, 0, 2).reshape(128, 128)
    v[:, V_N2:V_N2 + 8] = col(i["norm2_g_2"][0])
    a["vec"] = v
    g = np.zeros((2, P, D), np.float32)
    g[0] = i["ffn_norm_g"][0][None, :]
    g[1] = i["final_norm_g"][None, :]
    a["gbc"] = g
    a["pos"] = np.ascontiguousarray(i["positions_2"][0].reshape(2, 128).T)
    w = i["w_in_2"][0]
    q_, z_, a_, b_, cq, ckv, kr, su, sv, fq, ff, gt = np.split(
        w, np.cumsum([1536, 512, 4, 4, 256, 128, 64, 512, 512, 1536, 4])[:11], axis=1)
    misc = np.concatenate([cq, ckv, kr, a_, b_, ff, np.zeros((D, 52), np.float32)], 1)
    rows = lambda w: w.reshape(-1, 128, 1024)
    a["w2"] = np.concatenate([
        tiles(q_), blocks(np.concatenate([misc, z_, su, sv, fq], 1)), tiles(gt),
        *(x.reshape(4, 128, 4, 2, 128).transpose(2, 1, 3, 0, 4).reshape(4, 128, 1024) for x in i["w_branch_2"][0]),
        rows(i["w_out_2"][0]), tiles(i["w_ff1_2"][0]), rows(i["w_ff2_2"][0])])
    a["w2_uq"] = np.ascontiguousarray(i["mla_w_uq_2"][0].reshape(2, 128, 768))
    a["w2_ukv"] = np.ascontiguousarray(i["mla_w_ukv_2"][0])
    a["sgw"] = np.ascontiguousarray(i["sg_w_s_2"][0].transpose(2, 0, 1))
    v = np.zeros((P, NW2), np.float32)
    v[:, W_N1:W_N1 + 8] = col(i["norm1_g_2"][0])
    v[:, W_CONV:W_CONV + 48] = i["dn_conv_w_2"][0].reshape(4, 12, 128).transpose(2, 1, 0).reshape(128, 48)
    v[:, W_DT:W_DT + 4] = i["dn_dt_bias_2"][0][None, :]
    v[:, W_ALOG:W_ALOG + 4] = i["dn_a_log_2"][0][None, :]
    v[:, W_OUTG] = i["dn_out_norm_g_2"][0]
    v[:, W_QN:W_QN + 2] = col(i["mla_q_norm_g_2"][0])
    v[:, W_KVN] = i["mla_kv_norm_g_2"][0]
    v[:, W_QG:W_QG + 192] = i["mla_qk_q_g_2"][0][None, :]
    v[:, W_KG:W_KG + 192] = i["mla_qk_k_g_2"][0][None, :]
    v[:, W_SGB:W_SGB + 4] = i["sg_b_s_2"][0].T
    v[:, W_FQ] = i["fox_q_norm_g_2"][0]
    v[:, W_FK] = i["fox_k_norm_g_2"][0]
    v[:, W_FB:W_FB + 4] = i["fox_f_bias_2"][0][None, :]
    v[:, W_SGG:W_SGG + 512] = i["sg_v_norm_g_2"][0].reshape(1, 512)
    a["kw2"] = np.concatenate([constants_2(), v], 1)
    return a


def kernel(**inputs):
    import concourse.bacc as bacc
    from concourse.bass_utils import run_bass_kernel_spmd

    arrays = layout({n: np.asarray(a) for n, a in inputs.items()})
    nc = bacc.Bacc("TRN2", target_bir_lowering=False, num_devices=1)
    t = {n: nc.dram_tensor(f"in_{n}", a.shape, mybir.dt.from_np(a.dtype), kind="ExternalInput").ap()
         for n, a in arrays.items()}
    t["out"] = nc.dram_tensor("out_y", (P, 2, D), F32, kind="ExternalOutput").ap()
    program(nc, t)
    r = run_bass_kernel_spmd(nc, [{f"in_{n}": a for n, a in arrays.items()}], core_ids=[0])
    y = r.results[0]["out_y"]
    return np.ascontiguousarray(y.transpose(1, 0, 2)).reshape(1, 256, D)
```

```python
from contextlib import ExitStack

import numpy as np
import concourse.bass as bass
from concourse import mybir

F32 = mybir.dt.float32
F32R = mybir.dt.float32r
I32 = mybir.dt.int32
ALU = mybir.AluOpType
ACT = mybir.ActivationFunctionType
AX = mybir.AxisListType.X

P = 128
D = 1024
L = 272
NM = 16
NE = 16
CAP = 34
EPS = 1e-6
RING = 12
AR = 22000
TT = [(16, 128), (144, 128), (0, 16)]

C_ID, C_ONE, C_ROT, C_COS, C_SIN, C_IOTA = 0, 128, 256, 384, 656, 928
NCST = 992
K_TRIC, K_TRI, K_ONE, K_BLK, K_SEL, K_LEV, K_MB, K_INV = 0, 128, 256, 384, 512, 768, 1536, 1792
NK2 = 1824
W_N1, W_CONV, W_DT, W_ALOG, W_OUTG, W_QN, W_KVN, W_QG, W_KG = 0, 8, 56, 60, 64, 65, 67, 68, 260
W_SGB, W_FQ, W_FK, W_FB, W_N2, W_SGG = 452, 456, 457, 458, 462, 470
NW2 = 982
RAW = 3
WR = 4
FIRST_ROOM = RING * 2048 + 14848
TWO_PI = 6.283185307179586
C1 = 6.28125
C2 = float(np.float32(0.0019350051879882812))
C3 = TWO_PI - C1 - C2
V_MIXG, V_CONV, V_SUB, V_LAM, V_WR = 0, 8, 20, 21, 277
V_N2 = 405
NVEC = 413
FILLS = (1, 2, 2, 2, 1, 1, 1)
JOBS = 1
LAG = 1
O_LATE = 1


def constants():
    c = np.zeros((P, NCST), np.float32)
    c[:, C_ID:C_ID + 128] = np.eye(P)
    c[:, C_ONE:C_ONE + 128] = 1.0
    for m in range(P):
        if m % 64 < 32:
            c[m + 32, C_ROT + m] = -1.0
        else:
            c[m - 32, C_ROT + m] = 1.0
    inv = (np.float32(10000.0) ** (-np.arange(0, 64, 2, dtype=np.float32) / np.float32(64))).astype(np.float32)
    ang = np.arange(L, dtype=np.float32)[:, None] * inv[None, :]
    c[:, C_COS:C_COS + L] = np.tile(np.cos(ang).T, (4, 1))
    c[:, C_SIN:C_SIN + L] = np.tile(np.sin(ang).T, (4, 1))
    c[:, C_IOTA:C_IOTA + 64] = np.arange(64)[None, :]
    return c


def constants_2():
    k = np.zeros((P, NK2), np.float32)
    j, i = np.arange(P)[:, None], np.arange(P)[None, :]
    k[:, K_TRIC:K_TRIC + 128] = (j <= i) & (j // 64 == i // 64)
    k[:, K_TRI:K_TRI + 128] = j <= i
    k[:, K_ONE:K_ONE + 128] = 1.0
    k[:, K_BLK:K_BLK + 128] = j // 64 == i // 64
    k[:64, K_SEL:K_SEL + 128] = 1.0
    k[64:, K_SEL + 128:K_SEL + 256] = 1.0
    for n in range(6):
        s = 1 << n
        k[:, K_LEV + 128 * n:K_LEV + 128 * n + 128] = (i // s % 2 == 1) & (j // s == i // s - 1)
    k[:, K_MB + 128:K_MB + 256] = np.where(i <= j, 0.0, -1e30)
    k[:, K_INV:K_INV + 32] = (np.float32(10000.0) ** (-np.arange(0, 64, 2, dtype=np.float32) / np.float32(64)))[None, :]
    return k


class Queue:

    def __init__(self, sem, chained=False):
        self.sem, self.n, self.items, self.chained = sem, 0, [], chained

    def op(self, fn, *after):
        if self.chained and self.n:
            after += ((self.sem, self.n),)
        self.n += 1
        self.items.append((after, fn, self.sem, 1))
        return (self.sem, self.n)

    def quiet(self, fn, *after):
        self.items.append((after, fn, None, 0))

    def dma(self, fn, counter, *after):
        counter[1] += 16
        self.items.append((after, fn, counter[0], 16))
        return (counter[0], counter[1])

    def emit(self, eng):
        reached = {}
        for after, fn, sem, by in self.items:
            for s, v in after:
                if reached.get(s.name, 0) < v:
                    eng.wait_ge(s, v)
                    reached[s.name] = v
            ins = fn(eng) if fn is not None else None
            if sem is not None:
                ins.then_inc(sem, by)


class Banks:

    def __init__(self, ids):
        self.ids, self.at = list(ids), 0
        self.read = {b: [] for b in self.ids}

    def take(self):
        b = self.ids[self.at % len(self.ids)]
        self.at += 1
        return b


def bc(ap, axis, n):
    a = ap.unsqueeze(axis)
    shape = list(a.shape)
    shape[axis] = n
    return a.broadcast_to(shape)


def program(nc, t):
    ctx = ExitStack()
    with ctx:
        def sb(name, cols, dt=F32):
            return ctx.enter_context(nc.sbuf_tensor(f"sb_{name}", [P, cols], dt))

        def sem(name):
            return ctx.enter_context(nc.semaphore(name))

        pe, dve, act, sp = (Queue(sem(f"s_{n}")) for n in ("pe", "dve", "act", "sp"))
        pool = Queue(sem("s_pool"), chained=True)
        PS = ctx.enter_context(nc.psum_tensor("PS", [P, 8, 512], F32))

        cst = sb("cst", NCST)
        vec = sb("vec", NVEC)
        gbc = sb("gbc", 1024)
        Hx = sb("Hx", 3 * 1024)
        sm = sb("sm", 768)
        posi = ctx.enter_context(nc.sbuf_tensor("sb_posi", [P, 2], I32))
        tab = sb("tab", 128)
        invf = sb("invf", 32)
        first = ExitStack()

        def sb1(name, cols, dt=F32, of=first):
            return of.enter_context(nc.sbuf_tensor(f"sb_{name}", [P, cols], dt))

        ring = sb1("ring", RING * 2048)
        ar = sb1("ar", AR)

        H = Hx[:, :].rearrange("p (t d) -> p t d", t=3)
        ident = cst[:, C_ID:C_ID + 128]
        ones = cst[:, C_ONE:C_ONE + 128]
        nsm = [0]

        def small(n):
            nsm[0] += n
            assert nsm[0] <= 768
            return sm[:, nsm[0] - n:nsm[0]]

        at = [0]

        def take(n, *dims):
            at[0] += n
            assert at[0] <= AR, at[0]
            v = ar[:, at[0] - n:at[0]]
            if len(dims) == 1:
                v = v.rearrange("p (a b) -> p a b", a=dims[0])
            elif len(dims) == 2:
                v = v.rearrange("p (a b c) -> p a b c", a=dims[0], b=dims[1])
            return v

        slot_sem = [[sem(f"w{i}"), 0] for i in range(RING)]
        stream = []
        used = []

        place = []
        holder = [None] * RING
        turns = [0] * RING
        before = []

        def assign():
            i = len(place)
            s = i % RING
            place.append(s)
            before.append(holder[s])
            holder[s] = i
            turns[s] += 1
            return s, turns[s]

        def weights(fn):
            stream.append(fn)
            used.append(None)
            return len(stream) - 1

        class Slot:

            def __init__(self, src, shape=None):
                self.i = weights(src)
                s, turn_ = assign()
                self.v = ring[:, s * 2048:s * 2048 + 2048]
                self.tok = (slot_sem[s][0], 16 * turn_)

            def done(self, tok):
                used[self.i] = tok

        def packed(src, n):
            return [Slot(src[i]) for i in range(n)]

        c_cst = [sem("c_cst"), 0]
        c_vec = [sem("c_vec"), 0]
        c_g = [sem("c_g"), 0]
        Li = act.dma(lambda e: e.dma_start(cst[:, 0:256], t["cst"][:, 0:256]), [sem("c_id"), 0])
        Lv = act.dma(lambda e: e.dma_start(vec[:, :], t["vec"]), c_vec)
        Lx = [act.dma(lambda e: e.dma_start(H[:, 0, :], t["x"][:, 0, :]), [sem("c_x0"), 0]),
              act.dma(lambda e: e.dma_start(H[:, 1, :], t["x"][:, 1, :]), [sem("c_x1"), 0]),
              act.dma(lambda e: e.dma_start(H[0:NM, 2, :], t["meta"]), [sem("c_x2"), 0])]
        Lc = act.dma(lambda e: e.dma_start(cst[:, 256:], t["cst"][:, 256:]), c_cst)
        Lg = act.dma(lambda e: e.dma_start(gbc[:, :], t["gbc"][0]), c_g)

        XN = take(3072, 3)
        hnT = take(8 * L, 8)
        junk = take(1024)
        ss = small(4)
        rs = small(4)
        mhalf = small(16)
        k_mh = dve.op(lambda e: e.memset(mhalf, -0.5))
        bk = Banks(range(8))

        def rms(src, n, sscol, rscol, inv_n, width_junk, *after):
            a = act.op(lambda e: e.activation(width_junk, src, ACT.Square, accum_out=sscol), *after)
            b = dve.op(lambda e: e.tensor_scalar(rscol, sscol, inv_n, EPS, ALU.mult, ALU.add), a)
            c = pool.op(lambda e: e.tensor_tensor(rscol, rscol, mhalf[0:n, 0:1], ALU.pow), b, k_mh)
            return a, c

        def turn(src, n, dst_fn, evac_fn, *after):
            pass

        def turn_tile(XN, ti, n, col0, dstT, after, gcol=None, eng=None):
            out = []
            for half in range(2):
                b = bk.take()
                rd = bk.read[b]
                for k in range(4):
                    c = half * 4 + k
                    f = lambda e, b=b, k=k, c=c: e.transpose(
                        PS[:, b, k * 128:k * 128 + n], XN[0:n, ti, c * 128:c * 128 + 128], ident[0:n, 0:n])
                    if k < 3:
                        pe.quiet(f, *(rd + after + [Li] if k == 0 else []))
                    else:
                        tk = pe.op(f)
                src = PS[:, b, :].rearrange("p (k c) -> p k c", k=4)[:, :, 0:n]
                dst = dstT[:, half * 4:half * 4 + 4, col0:col0 + n]
                if gcol is not None:
                    r = dve.op(lambda e, s=src, d=dst, h=half: e.tensor_tensor(
                        d, s, bc(gcol[:, h * 4:h * 4 + 4], 2, n), ALU.mult), tk, Lv)
                elif half == 0:
                    r = act.op(lambda e, s=src, d=dst: e.copy(d, s), tk)
                else:
                    r = dve.op(lambda e, s=src, d=dst: e.tensor_copy(d, s), tk)
                bk.read[b] = [r]
                out.append(r)
            return out

        hn_ok, scaled = [], []
        xn_free = []
        jprev = ()
        for ti, (c0, n) in enumerate(TT):
            a, r = rms(H[0:n, ti, :], n, ss[0:n, ti:ti + 1], rs[0:n, ti:ti + 1], 1.0 / D, junk[0:n, :], Lx[ti], *jprev)
            jprev = (a,)
            x = dve.op(lambda e, ti=ti, n=n: e.tensor_scalar(
                XN[0:n, ti, :], H[0:n, ti, :], rs[0:n, ti:ti + 1], None, ALU.mult), r)
            scaled.append(x)
        for ti, (c0, n) in enumerate(TT):
            hn_ok += turn_tile(XN, ti, n, c0, hnT, [scaled[ti]], vec[:, V_MIXG:V_MIXG + 8])
        last_turn = (pe.sem, pe.n)

        c_k2 = [sem("c_k2"), 0]
        cosN = tab[:, 0:64].rearrange("p (t c) -> p t c", t=2)
        sinN = tab[:, 64:128].rearrange("p (t c) -> p t c", t=2)
        Lp = sp.dma(lambda e: e.dma_start(posi[:, :], t["pos"]), c_k2)
        Lp = sp.dma(lambda e: e.dma_start(invf[:, :], t["kw2"][:, K_INV:K_INV + 32]), c_k2)
        posf = small(2)
        tr_ = small(64 * 3)
        ang, kk, rr = (tr_[:, 64 * q:64 * q + 64] for q in range(3))
        a = dve.op(lambda e: e.tensor_copy(posf, posi[:, :]), Lp)
        a = dve.op(lambda e: e.tensor_tensor(ang.rearrange("p (t c) -> p t c", t=2), bc(posf, 2, 32), bc(invf[:, :], 1, 2), ALU.mult), a)
        a = dve.op(lambda e: e.tensor_scalar(kk, ang, 1.0 / TWO_PI, 12582912.0, ALU.mult, ALU.add), a)
        a = dve.op(lambda e: e.tensor_scalar(kk, kk, -12582912.0, None, ALU.add), a)
        a = dve.op(lambda e: e.scalar_tensor_tensor(rr, kk, -C1, ang, ALU.mult, ALU.add), a)
        a = dve.op(lambda e: e.scalar_tensor_tensor(rr, kk, -C2, rr, ALU.mult, ALU.add), a)
        a = dve.op(lambda e: e.scalar_tensor_tensor(rr, kk, -C3, rr, ALU.mult, ALU.add), a)
        a = dve.op(lambda e: e.tensor_scalar(rr, rr, 3.1415925, -3.1415925, ALU.min, ALU.max), a)
        x = act.op(lambda e: e.activation(sinN.rearrange("p t c -> p (t c)"), rr, ACT.Sin), a)
        a = dve.op(lambda e: e.tensor_scalar(kk, rr, TWO_PI / 4, TWO_PI / 2, ALU.add, ALU.is_gt), a)
        a = dve.op(lambda e: e.scalar_tensor_tensor(kk, kk, -TWO_PI, rr, ALU.mult, ALU.add), a)
        a = dve.op(lambda e: e.tensor_scalar(kk, kk, TWO_PI / 4, 3.1415925, ALU.add, ALU.min), a)
        a = dve.op(lambda e: e.tensor_scalar(kk, kk, -3.1415925, None, ALU.max), a)
        k_tab = act.op(lambda e: e.activation(cosN.rearrange("p t c -> p (t c)"), kk, ACT.Sin), a)

        def proj_T(sl, half, N, actT, *after):
            b = bk.take()
            for k in range(8):
                f = lambda e, k=k: e.matmul(PS[:, b, 0:N], sl.v.rearrange("p (k c) -> p k c", k=8)[
                    :, k, half * 128:half * 128 + 128], actT[:, k, 0:N], start=(k == 0), stop=(k == 7))
                w = (sl.tok, *bk.read[b], *after) if k == 0 else ()
                if k < 7:
                    pe.quiet(f, *w)
                else:
                    tk = pe.op(f, *w)
            if half == 1:
                sl.done(tk)
            return b, tk

        qraw = take(2 * L, 2)
        t1 = take(2 * L, 2)
        t2 = take(2 * L, 2)
        kT = take(4 * L, 4)
        qz = take(8 * L, 4, 2)
        z0 = pool.op(lambda e: e.memset(qz[64:128, :, 0, :], 0.0))
        z1 = pool.op(lambda e: e.memset(qz[0:64, :, 1, :], 0.0))
        cosT = cst[:, C_COS:C_COS + L]
        sinT = cst[:, C_SIN:C_SIN + L]
        rotm = cst[:, C_ROT:C_ROT + 128]
        kq_ok = []
        pend = []
        free_raw = [[], []]
        free_t = [[], []]

        def rope(j, which, h, raw_tok):
            b = bk.take()
            tk = pe.op(lambda e: e.matmul(PS[:, b, 0:L], rotm, qraw[:, j, :], start=True, stop=True),
                       raw_tok, Lc, *bk.read[b])
            a = pool.op(lambda e: e.tensor_tensor(t1[:, j, :], qraw[:, j, :], cosT, ALU.mult), raw_tok, Lc, *free_t[j])
            c = dve.op(lambda e: e.tensor_tensor(t2[:, j, :], PS[:, b, 0:L], sinT, ALU.mult), tk, *free_t[j])
            bk.read[b] = [c]
            free_raw[j] = [tk, a]
            if which == 0:
                r = [dve.op(lambda e: e.tensor_tensor(kT[:, h, :], t1[:, j, :], t2[:, j, :], ALU.add), a, c)]
            else:
                r = [dve.op(lambda e, i=i: e.tensor_tensor(
                    qz[64 * i:64 * i + 64, h, i, :], t1[64 * i:64 * i + 64, j, :],
                    t2[64 * i:64 * i + 64, j, :], ALU.add), a, c) for i in range(2)]
            free_t[j] = r
            kq_ok.extend(r)

        n = 0
        for which in range(2):
            for s2 in range(2):
                sl = Slot(t["w_in"][which * 2 + s2])
                for half in range(2):
                    j = n % 2
                    b, tk = proj_T(sl, half, L, hnT, *hn_ok)
                    r = act.op(lambda e, b=b, j=j: e.copy(qraw[:, j, :], PS[:, b, 0:L]), tk, *free_raw[j])
                    bk.read[b] = [r]
                    if pend:
                        rope(*pend.pop())
                    pend.append((j, which, s2 * 2 + half, r))
                    n += 1
        V = take(3 * 512, 3)
        sv = [Slot(t["w_in"][4]), Slot(t["w_in"][5])]
        v_ok = []
        for ti, (c0, n) in enumerate(TT):
            b = bk.take()
            if ti == 2:
                for k in range(4):
                    for g in range(2):
                        f = lambda e, k=k, g=g, b=b, c0=c0, n=n: e.matmul(
                            PS[64 * g:64 * g + n, b, :], hnT[:, 4 * g + k, c0:c0 + n],
                            sv[g].v[:, k * 512:k * 512 + 512], start=(k == 0), stop=(k == 3))
                        if k == 3 and g == 1:
                            tk = pe.op(f)
                        else:
                            pe.quiet(f, *(bk.read[b] if k == 0 else ()))
                r = act.op(lambda e, b=b, n=n: e.copy(V[0:n, 2, :], PS[64:64 + n, b, :]), tk)
                r = dve.op(lambda e, b=b, n=n: e.tensor_tensor(V[0:n, 2, :], V[0:n, 2, :], PS[0:n, b, :], ALU.add), r)
                bk.read[b] = [r]
                v_ok.append(r)
                if pend:
                    rope(*pend.pop())
                continue
            for k in range(8):
                f = lambda e, k=k, b=b, c0=c0, n=n: e.matmul(
                    PS[0:n, b, :], hnT[:, k, c0:c0 + n], sv[k // 4].v[:, (k % 4) * 512:(k % 4) * 512 + 512],
                    start=(k == 0), stop=(k == 7))
                w = (sv[0].tok, *bk.read[b]) if k == 0 else (sv[1].tok,) if k == 4 else ()
                if k == 7:
                    tk = pe.op(f, *w)
                else:
                    pe.quiet(f, *w)
            r = act.op(lambda e, b=b, ti=ti, n=n: e.copy(V[0:n, ti, :], PS[0:n, b, :]), tk)
            bk.read[b] = [r]
            v_ok.append(r)
            if pend:
                rope(*pend.pop())
        sv[0].done(tk)
        sv[1].done(tk)

        lt = small(128)
        l2 = small(2)
        l3 = small(2)
        lam = small(2)
        vl = vec[:, V_LAM:V_LAM + 256].rearrange("p (i a d) -> p i a d", i=2, a=2)
        a = dve.op(lambda e: e.tensor_tensor(lt.rearrange("p (i d) -> p i d", i=2), vl[:, :, 0, :], vl[:, :, 1, :], ALU.mult), Lv)
        a = dve.op(lambda e: e.tensor_reduce(l2, lt.rearrange("p (i d) -> p i d", i=2), AX, ALU.add), a)
        a = act.op(lambda e: e.activation(l3, l2, ACT.Exp), a)
        a = dve.op(lambda e: e.tensor_tensor(lam[:, 0:1], l3[:, 1:2], l3[:, 0:1], ALU.subtract), a)
        k_lam = dve.op(lambda e: e.tensor_scalar(lam[:, 1:2], lam[:, 0:1], -(0.8 - 0.6 * 1.0), None, ALU.add), a)

        Pm = take(2 * 2 * L, 2, 2)
        Am = take(2 * L, 2)
        AT = take(2 * 3 * 128, 2, 3)
        O = take(3 * 512, 3)
        O2 = take(512)
        mixT = take(8 * L, 8)
        cxs = take(L)
        up = take(2 * (L + 2), 2)
        cv = take(2 * L, 2)
        st = small(16)
        z2 = pool.op(lambda e: e.memset(up[:, :, 0:1], 0.0))
        z3 = pool.op(lambda e: e.memset(up[:, :, L + 1:L + 2], 0.0))
        p_free = [[], []]
        a_free = [[], []]
        at_free = [[], []]

        def scores(u):
            ti, h = divmod(u, 4)
            c0, n = TT[ti]
            j = u % 2
            bs = [bk.take(), bk.take()]
            rowm = st[0:n, 8 * j:8 * j + 2]
            rowb = st[0:n, 8 * j + 2:8 * j + 4]
            rows = st[0:n, 8 * j + 4:8 * j + 6]
            rowr = st[0:n, 8 * j + 6:8 * j + 8]
            ex = []
            for i in range(2):
                b = bs[i]
                tk = pe.op(lambda e, b=b, i=i: e.matmul(
                    PS[0:n, b, 0:L], qz[:, h, i, c0:c0 + n], kT[:, h, :], start=True, stop=True),
                    *kq_ok, z0, z1, *bk.read[b])
                m = dve.op(lambda e, b=b, i=i: e.tensor_reduce(rowm[:, i:i + 1], PS[0:n, b, 0:L], AX, ALU.max), tk, *a_free[j])
                m = dve.op(lambda e, i=i: e.tensor_scalar(rowb[:, i:i + 1], rowm[:, i:i + 1], -0.125, None, ALU.mult), m)
                x = act.op(lambda e, b=b, i=i: e.activation(
                    Pm[0:n, j, i, :], PS[0:n, b, 0:L], ACT.Exp, bias=rowb[:, i:i + 1], scale=0.125,
                    accum_out=rows[:, i:i + 1]), m, *p_free[j])
                bk.read[b] = [x]
                ex.append(x)
            r = dve.op(lambda e: e.reciprocal(rowr, rows), *ex)
            c = dve.op(lambda e: e.tensor_scalar(rowm[:, 1:2], rowr[:, 1:2], lam[0:n, 1:2], None, ALU.mult), r, k_lam)
            c = dve.op(lambda e: e.tensor_scalar(Am[0:n, j, :], Pm[0:n, j, 1, :], rowm[:, 1:2], None, ALU.mult), c, *a_free[j])
            c = dve.op(lambda e: e.scalar_tensor_tensor(
                Am[0:n, j, :], Pm[0:n, j, 0, :], rowr[:, 0:1], Am[0:n, j, :], ALU.mult, ALU.add), c)
            p_free[j] = [c]
            return c

        ob = {}

        def pv_turn(u, tok):
            ti, h = divmod(u, 4)
            c0, n = TT[ti]
            j = u % 2
            b = bk.take()
            for kt, (k0, kn) in enumerate(TT):
                f = lambda e, kt=kt, k0=k0, kn=kn: e.transpose(
                    PS[0:kn, b, kt * 128:kt * 128 + n], Am[0:n, j, k0:k0 + kn], ident[0:n, 0:n])
                if kt < 2:
                    pe.quiet(f, *((tok, *bk.read[b]) if kt == 0 else ()))
                else:
                    tk = pe.op(f)
            a_free[j] = [tk]
            src = PS[:, b, 0:256].rearrange("p (k c) -> p k c", k=2)[:, :, 0:n]
            r1 = act.op(lambda e: e.copy(AT[:, j, 0:2, 0:n], src), tk, *at_free[j])
            r2 = act.op(lambda e: e.copy(AT[0:NM, j, 2, 0:n], PS[0:NM, b, 256:256 + n]), tk)
            bk.read[b] = [r2]
            return r2

        def pv(u, r2):
            ti, h = divmod(u, 4)
            c0, n = TT[ti]
            j = u % 2
            if h == 0:
                ob[ti] = obk.take()
            o = ob[ti]
            for kt, (k0, kn) in enumerate(TT):
                f = lambda e, kt=kt, kn=kn: e.matmul(
                    PS[0:n, o, h * 128:h * 128 + 128], AT[0:kn, j, kt, 0:n], V[0:kn, kt, h * 128:h * 128 + 128],
                    start=(kt == 0), stop=(kt == 2))
                if kt < 2:
                    pe.quiet(f, *((r2, *v_ok, *(obk.read[o] if h == 0 else [])) if kt == 0 else ()))
                else:
                    tk = pe.op(f)
            at_free[j] = [tk]
            if h == 3:
                r = act.op(lambda e: e.copy(O[0:n, ti, :], PS[0:n, o, :]), tk)
                obk.read[o] = [r]
                return r

        oss = small(12)
        osr = small(12)
        o2_free = []

        def o_norm(ti, tok):
            n = TT[ti][1]
            o3 = O[0:n, ti, :].rearrange("p (h d) -> p h d", h=4)
            a = pool.op(lambda e: e.tensor_tensor(O2[0:n, :], O[0:n, ti, :], O[0:n, ti, :], ALU.mult), tok, *o2_free)
            a = dve.op(lambda e: e.tensor_reduce(oss[0:n, 4 * ti:4 * ti + 4], O2[0:n, :].rearrange("p (h d) -> p h d", h=4), AX, ALU.add), a)
            o2_free[:] = [a]
            a = dve.op(lambda e: e.tensor_scalar(osr[0:n, 4 * ti:4 * ti + 4], oss[0:n, 4 * ti:4 * ti + 4], 1.0 / 128, EPS, ALU.mult, ALU.add), a)
            a = pool.op(lambda e: e.tensor_tensor(osr[0:n, 4 * ti:4 * ti + 4], osr[0:n, 4 * ti:4 * ti + 4], mhalf[0:n, 0:4], ALU.pow), a)
            a = dve.op(lambda e: e.tensor_tensor(o3, o3, bc(osr[0:n, 4 * ti:4 * ti + 4], 2, 128), ALU.mult), a)
            return a

        def o_turn(ti, a):
            c0, n = TT[ti]
            b = bk.take()
            for h in range(4):
                f = lambda e, h=h: e.transpose(PS[:, b, h * 128:h * 128 + n], O[0:n, ti, h * 128:h * 128 + 128], ident[0:n, 0:n])
                if h < 3:
                    pe.quiet(f, *((a, *bk.read[b]) if h == 0 else ()))
                else:
                    tk = pe.op(f)
            r = dve.op(lambda e: e.tensor_scalar(
                mixT[:, 0:4, c0:c0 + n], PS[:, b, :].rearrange("p (h c) -> p h c", h=4)[:, :, 0:n],
                vec[:, V_SUB:V_SUB + 1], 0.8, ALU.mult, ALU.mult), tk)
            bk.read[b] = [r]
            return r

        cx_state = {}
        cxs_free = [[]]
        up_free = [[z2, z3], [z2, z3]]
        mix_ok, mix_t = [], {}

        def conv(i):
            m, part = divmod(i, 3)
            if i % 2 == 0:
                cx_state["sl"] = Slot(t["w_in"][6 + i // 2])
            b, tk = proj_T(cx_state["sl"], i % 2, L, hnT)
            j = m % 2
            cw = lambda k: vec[:, V_CONV + 3 * m + k:V_CONV + 3 * m + k + 1]
            if part == 0:
                r = act.op(lambda e: e.copy(cxs, PS[:, b, 0:L]), tk, *cxs_free[0])
                cx_state["cx"] = r
            elif part == 1:
                r = dve.op(lambda e: e.tensor_tensor(up[:, j, 1:L + 1], PS[:, b, 0:L], cxs, ALU.mult), tk, cx_state["cx"], *up_free[j])
                cxs_free[0] = [r]
                a = dve.op(lambda e: e.tensor_scalar(cv[:, j, :], up[:, j, 0:L], cw(0), None, ALU.mult), r, *up_free[j])
                a = dve.op(lambda e: e.scalar_tensor_tensor(cv[:, j, :], up[:, j, 1:L + 1], cw(1), cv[:, j, :], ALU.mult, ALU.add), a)
                a = dve.op(lambda e: e.scalar_tensor_tensor(cv[:, j, :], up[:, j, 2:L + 2], cw(2), cv[:, j, :], ALU.mult, ALU.add), a)
                cx_state["cv"] = a
            else:
                r = dve.op(lambda e: e.tensor_tensor(mixT[:, 4 + m, :], PS[:, b, 0:L], cv[:, j, :], ALU.mult), tk, cx_state["cv"])
                up_free[j] = [r]
                mix_ok.append(r)
            bk.read[b] = [r]

        obk = Banks([6, 7])
        att = Banks(range(6))
        for b in range(8):
            (obk if b > 5 else att).read[b] = bk.read[b]
        bk = att
        prev = None
        normed = {}
        for u in range(12):
            r2 = pv_turn(u - 1, prev) if prev is not None else None
            prev = scores(u)
            conv(u)
            if r2 is not None:
                r = pv(u - 1, r2)
                if r is not None:
                    normed[(u - 1) // 4] = o_norm((u - 1) // 4, r)
                elif (u - 1) % 4 == O_LATE and u > 4:
                    mix_t[u // 4 - 1] = o_turn(u // 4 - 1, normed[u // 4 - 1])
        last_norm = o_norm(2, pv(11, pv_turn(11, prev)))

        whole = Banks(range(8))
        for b in range(8):
            whole.read[b] = (obk if b > 5 else att).read[b]
        bk = whole
        so1 = [Slot(t["w_out"][i]) for i in range(4)]
        H_ok, xn_ok, trs = {}, [], []
        for ti, (c0, n) in enumerate(TT):
            if ti == 1:
                mix_t[2] = o_turn(2, last_norm)
            if ti == 2:
                b = bk.take()
                for c in range(8):
                    for db in range(2):
                        f = lambda e, c=c, b=b, c0=c0, n=n, db=db: e.matmul(
                            PS[64 * db:64 * db + n, b, :], mixT[:, c, c0:c0 + n],
                            so1[c // 2].v[:, (c % 2) * 1024 + db * 512:(c % 2) * 1024 + db * 512 + 512],
                            start=(c == 0), stop=(c == 7))
                        if c == 7 and db == 1:
                            tk = pe.op(f)
                        else:
                            pe.quiet(f, *((*mix_ok, mix_t[ti], *bk.read[b]) if c == 0 else ()))
                r1 = act.op(lambda e, b=b, n=n: e.copy(O2[0:n, :], PS[64:64 + n, b, :]), tk, *o2_free)
                r = dve.op(lambda e, b=b, n=n: e.tensor_tensor(H[0:n, 2, 0:512], H[0:n, 2, 0:512], PS[0:n, b, :], ALU.add), tk)
                r2 = dve.op(lambda e, n=n: e.tensor_tensor(H[0:n, 2, 512:1024], H[0:n, 2, 512:1024], O2[0:n, :], ALU.add), r1)
                bk.read[b] = [r, r1]
                H_ok[2] = [r, r2]
            for db in range(2 if ti < 2 else 0):
                b = bk.take()
                for c in range(8):
                    f = lambda e, c=c, b=b, c0=c0, n=n, db=db: e.matmul(
                        PS[0:n, b, :], mixT[:, c, c0:c0 + n],
                        so1[c // 2].v[:, (c % 2) * 1024 + db * 512:(c % 2) * 1024 + db * 512 + 512],
                        start=(c == 0), stop=(c == 7))
                    w = ((*mix_ok, mix_t[ti], *bk.read[b]) if c == 0 else ()) + (so1[c // 2].tok,)
                    if c < 7:
                        pe.quiet(f, *w)
                    else:
                        tk = pe.op(f, *w)
                hv = H[0:n, ti, db * 512:db * 512 + 512]
                r = dve.op(lambda e, hv=hv, b=b, n=n: e.tensor_tensor(hv, hv, PS[0:n, b, :], ALU.add), tk)
                bk.read[b] = [r]
                H_ok[ti] = [r] if db == 0 else H_ok[ti] + [r]
            a, r = rms(H[0:n, ti, :], n, ss[0:n, ti:ti + 1], rs[0:n, ti:ti + 1], 1.0 / D, junk[0:n, :], *H_ok[ti], *jprev)
            jprev = (a,)
            x = dve.op(lambda e, ti=ti, n=n: e.scalar_tensor_tensor(
                XN[0:n, ti, :], H[0:n, ti, :], rs[0:n, ti:ti + 1], gbc[0:n, :], ALU.mult, ALU.mult), r, Lg, last_turn)
            xn_ok.append(x)
            if ti > 0:
                trs.append(turn_tile(XN, ti - 1, TT[ti - 1][1], TT[ti - 1][0], hnT, [xn_ok[ti - 1], tk]))
        for s in so1:
            s.done((pe.sem, pe.n))

        lg = take(3 * 16, 3)
        af = take(3 * 16, 3)
        rt = small(12)
        wr = vec[:, V_WR:V_WR + 128].rearrange("p (k c) -> p k c", k=8)
        af_ok = []
        aT = take(L + 6)
        wk = take(2 * (L + 6), 2)
        bt = bk.take()
        bt_read = bk.read[bt]
        bk_ids = [b for b in range(8) if b != bt]
        rest = Banks(bk_ids)
        for b in bk_ids:
            rest.read[b] = bk.read[b]
        bk = rest
        lgs = []
        for ti, (c0, n) in enumerate(TT):
            if ti == 2:
                trs.append(turn_tile(XN, 2, TT[2][1], TT[2][0], hnT, [xn_ok[2], tk]))
            tr = trs[ti]
            b = bk.take()
            for k in range(8):
                f = lambda e, k=k, b=b, c0=c0, n=n: e.matmul(
                    PS[0:n, b, 0:16], hnT[:, k, c0:c0 + n], wr[:, k, :], start=(k == 0), stop=(k == 7))
                if k < 7:
                    pe.quiet(f, *((*tr, Lv, *bk.read[b]) if k == 0 else ()))
                else:
                    t3 = pe.op(f)
            lgs.append((b, t3))
        for ti, (c0, n) in enumerate(TT):
            b, t3 = lgs[ti]
            m = rt[0:n, 4 * ti:4 * ti + 1]
            s_ = rt[0:n, 4 * ti + 1:4 * ti + 2]
            r_ = rt[0:n, 4 * ti + 2:4 * ti + 3]
            a = dve.op(lambda e, m=m, b=b, n=n: e.tensor_reduce(m, PS[0:n, b, 0:16], AX, ALU.max, negate=True), t3)
            a = act.op(lambda e, ti=ti, n=n, b=b, m=m, s_=s_: e.activation(
                lg[0:n, ti, :], PS[0:n, b, 0:16], ACT.Exp, bias=m, scale=1.0, accum_out=s_), a)
            bk.read[b] = [a]
            a = dve.op(lambda e, s_=s_, r_=r_: e.reciprocal(r_, s_), a)
            a = dve.op(lambda e, ti=ti, n=n, r_=r_: e.tensor_scalar(af[0:n, ti, :], lg[0:n, ti, :], r_, None, ALU.mult), a)
            af_ok.append(a)
        for ti, (c0, n) in enumerate(TT):
            a = af_ok[ti]
            t4 = pe.op(lambda e, ti=ti, n=n, c0=c0: e.transpose(PS[0:16, bt, c0:c0 + n], af[0:n, ti, :], ident[0:n, 0:n]), a, *bt_read)
        a0 = dve.op(lambda e: e.tensor_copy(aT[0:16, 0:L], PS[0:16, bt, 0:L]), t4)
        a1 = dve.op(lambda e: e.memset(aT[0:16, L:L + 6], 2.0))
        bk_bt = [a0]
        m8 = small(8)
        cur = aT
        a = a1
        for r in range(5):
            a = dve.op(lambda e, cur=cur: e.max(m8[0:16, :], cur[0:16, :]), a, a0)
            nxt = wk[:, r % 2, :]
            a = dve.op(lambda e, cur=cur, nxt=nxt: e.match_replace(nxt[0:16, :], m8[0:16, :], cur[0:16, :], -1.0), a)
            cur = nxt
        mk = wk[0:16, 1, 0:L]
        cs = aT[0:16, 0:L]
        fin = wk[0:16, 0, 0:L]
        a = dve.op(lambda e: e.tensor_scalar(mk, fin, -1.0, None, ALU.is_equal), a)
        a = dve.op(lambda e: e.tensor_tensor_scan(cs, ones[0:16, 0:1].broadcast_to([16, L]), mk, 0.0, ALU.mult, ALU.add), a)
        a = dve.op(lambda e: e.tensor_tensor(cs, cs, mk, ALU.mult), a)
        a = dve.op(lambda e: e.tensor_scalar(cs, cs, -1.0, None, ALU.add), a)
        ps_ = take(3 * 16, 3)
        for ti, (c0, n) in enumerate(TT):
            t4 = pe.op(lambda e, ti=ti, n=n, c0=c0: e.transpose(PS[0:n, bt, ti * 16:ti * 16 + 16], cs[:, c0:c0 + n], ident[0:16, 0:16]), a)
        a = dve.op(lambda e: e.tensor_copy(ps_[:, 0:2, :], PS[:, bt, 0:32].rearrange("p (t c) -> p t c", t=2)), t4)
        b_ = dve.op(lambda e: e.tensor_copy(ps_[0:NM, 2, :], PS[0:NM, bt, 32:48]), t4)
        bt_free = b_
        base = at[0]
        at[0] = 3072
        S = take(3 * 1024, 3, 16)
        XG = take(2 * 1024, 2, 8)
        SL = take(1024, 2)
        Hh = take(1024, 2)
        HT = take(2 * 1024, 2, 8)
        Y = take(2 * 1024, 2)
        GA = take(256, 2)
        GT = take(256, 2)
        assert at[0] <= AR - 3 * 16 * 3 - 3 * (L + 6)
        at[0] = base
        iota = cst[:, C_IOTA:C_IOTA + 64]
        s_ok = []
        for e0, e1 in ((0, 2), (2, 16)):
            for ti, (c0, n) in enumerate(TT):
                s_ok.append(dve.op(lambda e, ti=ti, n=n, e0=e0, e1=e1: e.tensor_tensor(
                    S[0:n, ti, e0:e1, :], bc(iota[0:n, :], 1, e1 - e0), bc(ps_[0:n, ti, e0:e1], 2, 64), ALU.is_equal), a, b_))

        kw_free = [*s_ok, (act.sem, act.n), (pe.sem, pe.n), (pool.sem, pool.n)]
        Lg2 = act.dma(lambda e: e.dma_start(gbc[:, :], t["gbc"][1]), c_g, *xn_ok)

        misc = Banks([5, 6, 7])
        for b in misc.ids:
            misc.read[b] = [bt_free, (act.sem, act.n), (dve.sem, dve.n), (pe.sem, pe.n)]
        start_all = [(act.sem, act.n), (dve.sem, dve.n)]
        gu_free = [list(start_all), list(start_all)]
        y_free = list(start_all)
        xg_free = [[], []]
        xg_ok = [None, None]
        ht_free = [[], []]
        yb_free = [[], []]
        gt_ok = {}
        y_tok = {}

        def gather(p):
            j = p % 2
            ok = []
            for half in range(2):
                b = misc.take()
                for c4 in range(4):
                    c = half * 4 + c4
                    for ti, (c0, n) in enumerate(TT):
                        f = lambda e, b=b, c4=c4, c=c, ti=ti, n=n: e.matmul(
                            PS[:, b, c4 * 128:c4 * 128 + 128], XN[0:n, ti, c * 128:c * 128 + 128],
                            S[0:n, ti, 2 * p:2 * p + 2, :], start=(ti == 0), stop=(ti == 2))
                        w = (*(s_ok[:3] if p == 0 else s_ok), *xn_ok, *misc.read[b]) if c4 == 0 and ti == 0 else ()
                        if c4 == 3 and ti == 2:
                            tk = pe.op(f, *w)
                        else:
                            pe.quiet(f, *w)
                dst = XG[:, j, half * 4:half * 4 + 4, :]
                src = PS[:, b, :].rearrange("p (k c) -> p k c", k=4)
                if half == 0:
                    r = act.op(lambda e, dst=dst, src=src: e.copy(dst, src), tk, *xg_free[j])
                else:
                    r = dve.op(lambda e, dst=dst, src=src: e.tensor_copy(dst, src), tk, *xg_free[j])
                misc.read[b] = [r]
                ok.append(r)
            xg_ok[j] = ok

        ga_free = [[]]
        gt_free = [[]]

        def gates(p):
            a = [dve.op(lambda e, ti=ti: e.tensor_tensor(
                GA[:, ti, :].rearrange("p (e s) -> p e s", e=2), S[:, ti, 2 * p:2 * p + 2, :],
                bc(af[:, ti, 2 * p:2 * p + 2], 2, 64), ALU.mult), *ga_free[0]) for ti in range(2)]
            b = misc.take()
            pe.quiet(lambda e: e.transpose(PS[:, b, 0:128], GA[:, 0, :], ident), *a, *misc.read[b])
            tk = pe.op(lambda e: e.transpose(PS[:, b, 128:256], GA[:, 1, :], ident))
            ga_free[0] = [tk]
            r = dve.op(lambda e: e.tensor_copy(GT[:, :, :], PS[:, b, 0:256].rearrange("p (t c) -> p t c", t=2)), tk, *gt_free[0])
            misc.read[b] = [r]
            gt_ok[p] = r

        def scatter(p):
            j = p % 2
            out = []
            for ti in range(2):
                for db in range(2):
                    b = misc.take()
                    tk = pe.op(lambda e, ti=ti, db=db, b=b: e.matmul(
                        PS[:, b, :], GT[:, ti, :], Y[:, j, db * 512:db * 512 + 512], start=True, stop=True),
                        gt_ok[p], *y_tok[p], *misc.read[b])
                    hv = H[:, ti, db * 512:db * 512 + 512]
                    r = dve.op(lambda e, hv=hv, b=b: e.tensor_tensor(hv, hv, PS[:, b, :], ALU.add), tk)
                    misc.read[b] = [r]
                    out.append(r)
            gt_free[0] = [tk]
            yb_free[j] = [tk]
            return out

        def gate_up(ex):
            p, par = divmod(ex, 2)
            j = p % 2
            for k in range(8):
                for mat, name in enumerate(("w_gate", "w_up")):
                    sl = Slot(t[name][ex, k * 128:k * 128 + 128, :])
                    for q in range(2):
                        for g in range(2):
                            f = lambda e, k=k, mat=mat, q=q, g=g, sl=sl: e.matmul(
                                PS[64 * g:64 * g + 64, 2 * mat + q, :], XG[:, j, k, 64 * par:64 * par + 64],
                                sl.v[:, (2 * g + q) * 512:(2 * g + q) * 512 + 512], start=(k == 0), stop=(k == 7))
                            w = [sl.tok, *xg_ok[j]]
                            if k == 0:
                                w += gu_free[q]
                            if q == 1 and g == 1:
                                tk = pe.op(f, *w)
                            else:
                                pe.quiet(f, *w)
                    sl.done(tk)
            if par == 1:
                xg_free[j] = [tk]
            return tk

        hh_free = [[], []]

        def hidden(ex, tk):
            ok = []
            for q in range(2):
                a = act.op(lambda e, q=q: e.activation(SL[:, q, :], PS[:, q, :], ACT.Silu), tk, *hh_free[q])
                r = dve.op(lambda e, q=q: e.tensor_tensor(Hh[:, q, :], SL[:, q, :], PS[:, 2 + q, :], ALU.mult), a, *hh_free[q])
                gu_free[q] = [r]
                ok.append(r)
            return ok

        def down(ex, hok):
            p, par = divmod(ex, 2)
            j = ex % 2
            ht_ok = []
            for q in range(2):
                b = misc.take()
                for i in range(4):
                    f = lambda e, q=q, i=i, b=b: e.transpose(PS[:, b, i * 128:i * 128 + 128], Hh[:, q, i * 128:i * 128 + 128], ident)
                    if i < 3:
                        pe.quiet(f, *((hok[q], *misc.read[b]) if i == 0 else ()))
                    else:
                        tk = pe.op(f)
                hh_free[q] = [tk]
                dst = HT[:, j, 4 * q:4 * q + 4, :]
                src = PS[:, b, :].rearrange("p (k c) -> p k c", k=4)
                if q == 0:
                    r = act.op(lambda e, dst=dst, src=src: e.copy(dst, src), tk, *ht_free[j])
                else:
                    r = dve.op(lambda e, dst=dst, src=src: e.tensor_copy(dst, src), tk, *ht_free[j])
                misc.read[b] = [r]
                ht_ok.append(r)
            for s in range(8):
                sl = Slot(t["w_down"][ex, 256 * s:256 * s + 256, :].rearrange("(a p) d -> p a d", p=128))
                for a in range(2):
                    c = 2 * s + a
                    for g in range(2):
                        f = lambda e, a=a, g=g, c=c, sl=sl: e.matmul(
                            PS[64 * g:64 * g + 64, 4, :], HT[:, j, c % 8, (c // 8) * 64:(c // 8) * 64 + 64],
                            sl.v[:, a * 1024 + g * 512:a * 1024 + g * 512 + 512], start=(c == 0), stop=(c == 15))
                        w = [sl.tok, ht_ok[0], ht_ok[1]] + (list(y_free) if c == 0 else [])
                        if a == 1 and g == 1:
                            tk = pe.op(f, *w)
                        else:
                            pe.quiet(f, *w)
                sl.done(tk)
            ht_free[j] = [tk]
            rs_ = [act.op(lambda e, g=g: e.copy(
                Y[64 * par:64 * par + 64, p % 2, 512 * g:512 * g + 512], PS[64 * g:64 * g + 64, 4, :]),
                tk, *yb_free[p % 2]) for g in range(2)]
            y_free[:] = rs_
            y_tok.setdefault(p, []).extend(rs_)

        NX = t.get("n_experts", NE)
        if NX:
            gather(0)
        for ex in range(NX):
            tk = gate_up(ex)
            hok = hidden(ex, tk)
            if ex % 2 == 0:
                if ex >= 2:
                    scatter(ex // 2 - 1)
                gates(ex // 2)
            elif ex + 1 < NX:
                gather(ex // 2 + 1)
            down(ex, hok)
        moe_ok = scatter(NX // 2 - 1) if NX else H_ok[0] + H_ok[1]

        for i, src in enumerate(stream):
            after = (used[before[i]],) if before[i] is not None else (Lv, *Lx, Lc) if i == 1 else ()
            s = place[i]
            dst = ring[:, s * 2048:s * 2048 + 2048]
            if len(src.shape) == 3:
                dst = dst.rearrange("p (a d) -> p a d", a=src.shape[1])
            sp.dma(lambda e, dst=dst, src=src: e.dma_start(dst, src), slot_sem[s], *after)

        moe_end = [(act.sem, act.n), (dve.sem, dve.n), (pe.sem, pe.n)]
        first.close()
        second = ExitStack()
        ctx.enter_context(second)
        wp = sb1("wp", WR * 2048, F32R, second)[:, :].rearrange("p (w q c) -> p w q c", w=WR, q=2)
        hr = sb1("hr", 4096, F32R, second)[:, :].rearrange("p (q c) -> p q c", q=2)
        raw = sb1("raw", RAW * 1024, F32, second)
        raw_over = WR + 2
        mid = ExitStack()
        ctx.enter_context(mid)
        big = sb1("big", FIRST_ROOM - WR * 2048 - 4096 - RAW * 1024, F32, mid)
        KW = sb1("kw", NK2 + NW2, F32, mid)
        little = sb1("little", RING * 2048 + AR - FIRST_ROOM - NK2 - NW2, F32, mid)
        c_kw = [sem("c_kw"), 0]
        Lk2 = pool.dma(lambda e: e.dma_start(KW[:, :], t["kw2"]), c_kw, *kw_free)
        KT = KW[:, 0:NK2]
        VW = KW[:, NK2:NK2 + NW2]
        segs = {"big": [big, 0, FIRST_ROOM - WR * 2048 - 4096 - RAW * 1024],
                "little": [little, 0, RING * 2048 + AR - FIRST_ROOM - NK2 - NW2], "Hx": [Hx, 2048, 3072]}

        def shaped(v, dims):
            if len(dims) == 1:
                v = v.rearrange("p (a b) -> p a b", a=dims[0])
            elif len(dims) == 2:
                v = v.rearrange("p (a b c) -> p a b c", a=dims[0], b=dims[1])
            return v

        def room(where, n, *dims):
            s_ = segs[where]
            assert s_[2] - s_[1] >= n, (where, n, s_[2] - s_[1])
            s_[1] += n
            return shaped(s_[0][:, s_[1] - n:s_[1]], dims)

        R1 = room("big", 4096)
        R4 = room("big", 4096)
        NN = room("big", 3072)
        BTf = room("big", 4096)
        Ff = room("big", 3072)
        KDT = room("big", 2048)
        KG = room("big", 1024, 2, 4)
        SUV = room("big", 2048)
        RT = room("big", 512)
        MS = room("little", 1024, 2)
        Z = room("little", 1024, 2)
        SQ = room("little", 1024)
        SW = room("little", 512, 4)
        SC = room("little", 512, 2)
        RD = room("little", 128)
        PT = room("Hx", 512, 2)
        XB = NN[:, 0:2048].rearrange("p (t c) -> p t c", t=2)
        hTh = hr[:, 0, :].rearrange("p (k c) -> p k c", k=8)
        hTl = hr[:, 1, :].rearrange("p (k c) -> p k c", k=8)

        raw_sem = [[sem(f"r{n}"), 0] for n in range(RAW)]
        stream2, raw_used = [], []
        last_of_slot = {place[n]: used[n] for n in range(len(place))}

        def raw_piece(src):
            n = len(stream2)
            stream2.append((src, lambda: [raw_used[n - RAW]] if n >= RAW else [last_of_slot[raw_over + n // 2]]))
            raw_used.append(None)
            return n, raw[:, (n % RAW) * 1024:(n % RAW) * 1024 + src.shape[1]], (raw_sem[n % RAW][0], 16 * (n // RAW + 1))

        parts, parts_used, took = [], [], [0]

        def prepare(n):
            if n >= t["w2"].shape[0]:
                return
            r, v, tok = raw_piece(t["w2"][n])
            hi, lo = wp[:, n % WR, 0, :], wp[:, n % WR, 1, :]
            a = act.op(lambda e: e.copy(hi, v), tok, *moe_end, *([parts_used[n - WR]] if n >= WR else []))
            b = dve.op(lambda e: e.tensor_tensor(lo, v, hi.bitcast(F32), ALU.subtract), a)
            raw_used[r] = b
            parts.append((hi, lo, (a, b)))

        def piece():
            n = took[0]
            took[0] += 1
            assert len(parts_used) == n
            prepare(n + WR - 1)
            return parts[n]

        def release(tok):
            parts_used.append(tok)

        c_sw = [sem("c_sw"), 0]
        Lsw = pool.dma(lambda e: e.dma_start(SW, t["sgw"]), c_sw, *moe_end)
        bk = Banks(range(6))
        open_read = {b: list(moe_end) for b in range(8)}
        for b in bk.ids:
            bk.read[b] = list(moe_end)
        fr = small(16)

        def power1(x, *after):
            return pool.op(lambda e: e.tensor_tensor(x, x, mhalf[:, 0:1], ALU.pow), *after, k_mh)

        def turn_two(XB, gcol, tmps, ready, *after):
            out, split = [], []
            for ti in range(2):
                for half in range(2):
                    b = bk.take()
                    for k in range(4):
                        c = half * 4 + k
                        f = lambda e, b=b, k=k, c=c, ti=ti: e.transpose(PS[:, b, k * 128:k * 128 + 128], XB[:, ti, c * 128:c * 128 + 128], ident)
                        if k < 3:
                            pe.quiet(f, *((ready[ti], *after, *bk.read[b]) if k == 0 else ()))
                        else:
                            tk = pe.op(f)
                    tm = tmps[ti][:, half * 512:half * 512 + 512].rearrange("p (k c) -> p k c", k=4)
                    hi = hTh[:, half * 4:half * 4 + 4, ti * 128:ti * 128 + 128]
                    lo = hTl[:, half * 4:half * 4 + 4, ti * 128:ti * 128 + 128]
                    r = dve.op(lambda e, tm=tm, b=b, half=half: e.tensor_tensor(
                        tm, PS[:, b, :].rearrange("p (k c) -> p k c", k=4), bc(gcol[:, half * 4:half * 4 + 4], 2, 128), ALU.mult), tk, Lk2, Lv, *after)
                    bk.read[b] = [r]
                    a = act.op(lambda e, tm=tm, hi=hi: e.copy(hi, tm), r)
                    out.append(a)
                    split.append((lambda e, tm=tm, hi=hi, lo=lo: e.tensor_tensor(lo, tm, hi.bitcast(F32), ALU.subtract), a))
                    if half == 0:
                        out.append(pool.op(*split.pop(), r))
                    elif ti == 1:
                        out += [dve.op(*x) for x in split]
            return out

        hT_ok = []
        sq_ = [BTf[:, 1024 * q:1024 * q + 1024] for q in range(4)]
        s1, s2, s12 = ([fr[:, 2 * q + ti:2 * q + ti + 1] for ti in range(2)] for q in range(3))
        ys, sy, sx, done = [], [], [], []
        for ti in range(2):
            ys.append(dve.op(lambda e, ti=ti: e.tensor_tensor(XB[:, ti, :], H[:, ti, :], gbc[:, :], ALU.mult), *moe_end, Lg2))
            sx.append(act.op(lambda e, ti=ti: e.activation(sq_[ti], H[:, ti, :], ACT.Square, accum_out=s1[ti]), *moe_end))
            sy.append(act.op(lambda e, ti=ti: e.activation(sq_[2 + ti], XB[:, ti, :], ACT.Square, accum_out=s2[ti]), ys[ti]))
        for ti in range(2):
            x, y, z = s1[ti], s2[ti], s12[ti]
            a = dve.op(lambda e, x=x: e.tensor_scalar(x, x, 1.0 / D, EPS, ALU.mult, ALU.add), sx[ti])
            r1 = power1(x, a)
            a = dve.op(lambda e, x=x, y=y, z=z: e.scalar_tensor_tensor(z, y, 1.0 / D, x, ALU.mult, ALU.mult), r1, sy[ti])
            a = dve.op(lambda e, x=x, z=z: e.tensor_scalar(z, z, x, EPS, ALU.mult, ALU.add), a)
            a = power1(z, a)
            a = dve.op(lambda e, x=x, z=z: e.tensor_scalar(z, z, x, None, ALU.mult), a)
            if ti == 0:
                done.append(dve.op(lambda e, z=z: e.tensor_scalar(XB[:, 0, :], XB[:, 0, :], z, None, ALU.mult), a))
            else:
                done.append(act.op(lambda e, z=z: e.activation(XB[:, 1, :], XB[:, 1, :], ACT.Copy, scale=z), a))
        prepare(0)
        hT_ok += turn_two(XB, VW[:, W_N1:W_N1 + 8], sq_[:2], done, *sy)
        for n in range(1, WR - 1):
            prepare(n)
        hn_end = [dve.op(lambda e, ti=ti: e.scalar_tensor_tensor(
            H[:, ti, :], H[:, ti, :], s1[ti], gbc[:, :], ALU.mult, ALU.mult), sx[ti]) for ti in range(2)]

        def tile_T(sl, off, K, lhs, rhs, N, *after):
            b = bk.take()
            for k in range(K):
                f = lambda e, k=k: e.matmul(PS[:, b, 0:N], lhs(k), rhs(k), start=(k == 0), stop=(k == K - 1))
                w = (*after, *bk.read[b]) if k == 0 else ()
                if k < K - 1:
                    pe.quiet(f, *w)
                else:
                    tk = pe.op(f, *w)
            return b, tk

        PASSES = ((0, 0), (0, 1), (1, 0))

        def tile3(K, lhs, rhs, N, *after):
            b = bk.take()
            for k in range(K):
                for q, (p1, p2) in enumerate(PASSES):
                    f = lambda e, k=k, p1=p1, p2=p2, q=q: e.matmul(
                        PS[:, b, 0:N], lhs(p1, k), rhs(p2, k), start=(k == 0 and q == 0), stop=(k == K - 1 and q == 2))
                    w = (*after, *bk.read[b]) if k == 0 and q == 0 else ()
                    if k < K - 1 or q < 2:
                        pe.quiet(f, *w)
                    else:
                        tk = pe.op(f, *w)
            return b, tk

        def rows3(banks, first, last, acts, wts, cols, after, toks):
            n = 0
            for (ti, c), b in banks.items():
                for q, (p1, p2) in enumerate(PASSES):
                    f = lambda e, ti=ti, c=c, b=b, p1=p1, p2=p2, q=q: e.matmul(
                        PS[:, b, :], acts(p1, ti), wts(p2)[:, cols[c]], start=(first and q == 0), stop=(last and q == 2))
                    w = tuple(after if n == 0 else ()) + tuple(open_read[b] if first and q == 0 else ())
                    n += 1
                    if q == 2 and (last or n == 3 * len(banks)):
                        tk = pe.op(f, *w)
                        toks[(ti, c)] = tk
                    else:
                        pe.quiet(f, *w)
            return tk

        bulk, side = [], []
        at = {"done": 0, "stage": 0}
        outs = []

        def fill(n=1):
            for _ in range(n):
                if bulk:
                    bulk.pop(0)()
                    at["done"] += 1
                elif at["stage"] < 3:
                    return
                for _ in range(JOBS):
                    if side and at["done"] >= side[0][0] and at["stage"] >= side[0][1]:
                        side.pop(0)[2]()

        QT = R1[:, 0:3072].rearrange("p (m c) -> p m c", m=12)
        cb_ = R4[:, 0:4 * 259].rearrange("p (a c) -> p a c", a=4)
        cc_ = R4[:, 1100:1100 + 4 * 256].rearrange("p (a c) -> p a c", a=4)
        zz = pool.op(lambda e: e.memset(cb_[:, :, 0:3], 0.0), *moe_end)
        qt_ok = []
        cf = [[zz] for _ in range(4)]

        def tile_hT(*after):
            hi, lo, ok = piece()
            v = [x.rearrange("p (k c) -> p k c", k=8) for x in (hi, lo)]
            b, tk = tile3(8, lambda p, k: v[p][:, k, :], lambda p, k: (hTh, hTl)[p][:, k, :], 256, *ok, *after)
            release(tk)
            return b, tk

        convs = []

        def conv_silu(m, j, tok):
            a = act.op(lambda e: e.activation(QT[:, m, :], cc_[:, j, :], ACT.Silu), tok)
            cf[j] = [a]
            qt_ok.append(a)

        for m in range(12):
            b, tk = tile_hT(*hT_ok)
            j = m % 4
            a = act.op(lambda e, b=b, j=j: e.copy(cb_[:, j, 3:259], PS[:, b, 0:256]), tk, *cf[j])
            bk.read[b] = [a]
            cw = lambda k, m=m: VW[:, W_CONV + 4 * m + k:W_CONV + 4 * m + k + 1]
            a = dve.op(lambda e, j=j, cw=cw: e.tensor_scalar(cc_[:, j, :], cb_[:, j, 0:256], cw(0), None, ALU.mult), a, Lk2, *cf[j])
            for k in range(1, 4):
                a = dve.op(lambda e, j=j, k=k, cw=cw: e.scalar_tensor_tensor(
                    cc_[:, j, :], cb_[:, j, k:k + 256], cw(k), cc_[:, j, :], ALU.mult, ALU.add), a)
            convs.append((m, j, a))
            if m > 0:
                conv_silu(*convs[m - 1])
        conv_silu(*convs[11])

        def nat_steps(evac):
            toks = {}

            def step(s_):
                hi, lo, ok = piece()
                for k2 in range(2):
                    k = 2 * s_ + k2
                    tk = rows3({(0, 0): 6, (1, 0): 7}, k == 0, k == 7,
                               lambda p, ti, k=k: (hTh, hTl)[p][:, k, ti * 128:ti * 128 + 128],
                               lambda p, k2=k2: (hi, lo)[p][:, k2 * 512:k2 * 512 + 512], [slice(0, 512)],
                               (*ok, *hT_ok), toks)
                release(tk)
                if s_ == 3:
                    for ti in range(2):
                        open_read[6 + ti] = [evac(ti, 6 + ti, toks[(ti, 0)])]
            return [lambda s_=s_: step(s_) for s_ in range(4)]

        ms_ok, z_ok = [None, None], [None, None]
        SU = SUV[:, 0:1024].rearrange("p (t c) -> p t c", t=2)
        SV = SUV[:, 1024:2048].rearrange("p (t c) -> p t c", t=2)
        F = Ff.rearrange("p (q t c) -> p q t c", q=3, t=2)
        su_ok, sv_ok, f_ok = [None, None], [None, None], {}

        def to(dst, ok, key, func=None):
            def evac(ti, b, tk):
                r = act.op((lambda e: e.copy(dst[:, ti, :], PS[:, b, :])) if func is None else
                           (lambda e: e.activation(dst[:, ti, :], PS[:, b, :], func)), tk, *moe_end)
                ok[key(ti)] = r
                return r
            return evac

        for f in nat_steps(to(MS, ms_ok, lambda ti: ti)) + nat_steps(to(Z, z_ok, lambda ti: ti, ACT.Silu)):
            f()
        bulk += nat_steps(to(SU, su_ok, lambda ti: ti, ACT.Gelu_apprx_tanh))
        bulk += nat_steps(to(SV, sv_ok, lambda ti: ti, ACT.Gelu_apprx_tanh))
        for q in range(3):
            bulk += nat_steps(to(F[:, q], f_ok, lambda ti, q=q: (ti, q)))
        fill(FILLS[0])

        sq_free = [[]]

        def sums(src, G, W, *after):
            return sums_of(squares_of(src, G, W, *after))

        def squares_of(src, G, W, *after):
            s3 = SQ[:, 0:G * W].rearrange("p (g w) -> p g w", g=G)
            return s3, G, pool.op(lambda e: e.tensor_tensor(s3, src, src, ALU.mult), *after, *sq_free[0])

        def sums_of(squares):
            s3, G, a = squares
            c = small(G)
            b = dve.op(lambda e: e.tensor_reduce(c, s3, AX, ALU.add), a)
            sq_free[0] = [b]
            return c, b

        def power(c, G, mean, *after):
            a = dve.op(lambda e: e.tensor_scalar(c, c, mean, EPS, ALU.mult, ALU.add), *after)
            return pool.op(lambda e: e.tensor_tensor(c, c, mhalf[:, 0:G], ALU.pow), a)

        def scale(dst, src, c, W, *after):
            return dve.op(lambda e: e.tensor_tensor(dst, src, bc(c, 2, W), ALU.mult), *after)

        def turn4(srcs, dsts, after, gcol=None, rows=128, eng=None):
            b = bk.take()
            G = len(srcs)
            for i, s_ in enumerate(srcs):
                f = lambda e, i=i, s_=s_: e.transpose(PS[0:rows, b, i * 128:i * 128 + 128], s_, ident)
                if i < G - 1:
                    pe.quiet(f, *((*after, *bk.read[b]) if i == 0 else ()))
                else:
                    tk = pe.op(f, *((*after, *bk.read[b]) if i == 0 else ()))
            src = PS[0:rows, b, 0:G * 128].rearrange("p (g c) -> p g c", g=G)
            if gcol is not None:
                r = dve.op(lambda e: e.tensor_scalar(dsts, src, gcol, None, ALU.mult), tk)
            elif eng is dve:
                r = dve.op(lambda e: e.tensor_copy(dsts, src), tk)
            else:
                r = act.op(lambda e: e.copy(dsts, src), tk)
            bk.read[b] = [r]
            return r

        spx = small(16).rearrange("p (t c) -> p t c", t=2)
        spa = small(16).rearrange("p (t c) -> p t c", t=2)
        g8 = small(8).rearrange("p (t c) -> p t c", t=2)
        lf = small(8).rearrange("p (t c) -> p t c", t=2)
        beta = small(8).rearrange("p (t c) -> p t c", t=2)
        ea = small(4)
        GC = small(40)
        eg = small(8)
        ed = small(8)
        egl = small(16)
        bg = small(8)
        a1 = dve.op(lambda e: e.tensor_tensor(spx[:, :, 0:4], MS[:, :, 448:452], bc(VW[:, W_DT:W_DT + 4], 1, 2), ALU.add), *ms_ok, Lk2)
        a = dve.op(lambda e: e.tensor_tensor(spx[:, :, 4:8], MS[:, :, 456:460], bc(VW[:, W_FB:W_FB + 4], 1, 2), ALU.add), *ms_ok)
        a2 = dve.op(lambda e: e.tensor_scalar(spx[:, :, 4:8], spx[:, :, 4:8], -1.0, None, ALU.mult), a)
        a = dve.op(lambda e: e.scalar_tensor_tensor(spa, spx, -1.0, spx, ALU.mult, ALU.max), a1, a2)
        a = act.op(lambda e: e.activation(spa, spa, ACT.Exp, scale=-1.0), a)
        b1 = act.op(lambda e: e.activation(beta, MS[:, :, 452:456], ACT.Exp, scale=-1.0), *ms_ok)
        b2 = act.op(lambda e: e.activation(ea, VW[:, W_ALOG:W_ALOG + 4], ACT.Exp), Lk2)
        a = dve.op(lambda e: e.tensor_scalar(spa, spa, 1.0, None, ALU.add), a)
        a = act.op(lambda e: e.activation(spa, spa, ACT.Ln), a)
        a = dve.op(lambda e: e.scalar_tensor_tensor(spa, spx, 0.0, spa, ALU.max, ALU.add), a)
        g_ok = dve.op(lambda e: e.scalar_tensor_tensor(g8, spa[:, :, 0:4], -1.0, bc(ea, 1, 2), ALU.mult, ALU.mult), a, b2)
        l_ok = dve.op(lambda e: e.tensor_scalar(lf, spa[:, :, 4:8], -1.0, None, ALU.mult), a)
        b1 = dve.op(lambda e: e.tensor_scalar(beta, beta, 1.0, None, ALU.add), b1)
        b_ok = dve.op(lambda e: e.reciprocal(beta, beta), b1)
        N = NN.rearrange("p (t m c) -> p t m c", t=2, m=12)
        n_ok = {}
        for ti in range(2):
            for q in range(3):
                n_ok[(ti, q)] = turn4([QT[:, 4 * q + h, ti * 128:ti * 128 + 128] for h in range(4)],
                                      N[:, ti, 4 * q:4 * q + 4, :], qt_ok + list(moe_end), eng=dve if q == 1 else None)
        g8f, lff = g8.rearrange("p t c -> p (t c)"), lf.rearrange("p t c -> p (t c)")
        tri = KT[:, K_TRI:K_TRI + 128]
        tric = KT[:, K_TRIC:K_TRIC + 128]
        one = KT[:, K_ONE:K_ONE + 128]
        b = bk.take()
        for n_, (c0, lhs, rhs, first, last) in enumerate([
                (0, tric, g8f, True, True), (8, KT[:, K_BLK:K_BLK + 128], g8f, True, True),
                (16, KT[:, K_SEL:K_SEL + 128], g8f, True, True), (24, KT[:, K_SEL + 128:K_SEL + 256], g8f, True, True),
                (32, tri, lf[:, 0, :], True, True), (36, one, lf[:, 0, :], True, False), (36, tri, lf[:, 1, :], False, True)]):
            w = rhs.free_size()
            f = lambda e, b=b, c0=c0, lhs=lhs, rhs=rhs, first=first, last=last, w=w: e.matmul(
                PS[:, b, c0:c0 + w], lhs, rhs, start=first, stop=last)
            if n_ < 6:
                pe.quiet(f, *((g_ok, l_ok, *bk.read[b]) if n_ == 0 else ()))
            else:
                tk = pe.op(f)
        gc_ok = dve.op(lambda e, b=b: e.tensor_copy(GC, PS[:, b, 0:40]), tk)
        bk.read[b] = [gc_ok]
        e1 = act.op(lambda e: e.activation(eg, GC[:, 0:8], ACT.Exp), gc_ok)
        a = dve.op(lambda e: e.tensor_tensor(ed, GC[:, 8:16], GC[:, 0:8], ALU.subtract), gc_ok)
        e2 = act.op(lambda e: e.activation(ed, ed, ACT.Exp), a)
        e3 = act.op(lambda e: e.activation(egl, GC[:, 16:32], ACT.Exp), gc_ok)
        bg_ok = dve.op(lambda e: e.tensor_tensor(bg, beta.rearrange("p t c -> p (t c)"), eg, ALU.mult), e1, b_ok)
        KD = KDT[:, 0:1024].rearrange("p (t h d) -> p t h d", t=2, h=4)
        DT = KDT[:, 1024:2048].rearrange("p (r i) -> p r i", r=8)
        RB = R4[:, 2200:3224].rearrange("p (r i) -> p r i", r=8)
        a = dve.op(lambda e: e.tensor_tensor(RB, bc(tric, 1, 8), bc(g8f, 2, 128), ALU.mult), g_ok, *moe_end)
        d_ok = []
        for q in range(2):
            b = bk.take()
            tk = pe.op(lambda e, b=b, q=q: e.matmul(PS[:, b, :], one, R4[:, 2200 + 512 * q:2712 + 512 * q], start=True, stop=True), a, *bk.read[b])
            for r in range(4):
                x = dve.op(lambda e, b=b, q=q, r=r: e.tensor_scalar(
                    DT[:, 4 * q + r, :], PS[:, b, r * 128:r * 128 + 128], GC[:, 4 * q + r:4 * q + r + 1], 0.0, ALU.subtract, ALU.min), tk, gc_ok)
            bk.read[b] = [x]
            d_ok.append(act.op(lambda e, q=q: e.activation(DT[:, 4 * q:4 * q + 4, :], DT[:, 4 * q:4 * q + 4, :], ACT.Exp), x))
        dt_ok = dve.op(lambda e: e.tensor_tensor(DT, DT, bc(tric, 1, 8), ALU.mult), *d_ok)
        fill(FILLS[1])

        qk_ok = []
        gate_ok = {}

        def gate_room(i, m):
            at_ = (0, 2048, 2048, 0)[i] + m * 256
            return (R1 if i < 2 else R4)[:, at_:at_ + 256]

        def gate_unit(n):
            def unit():
                assert n < 24 or 3 in dm_ok
                assert n < 28 or len(qk2_ok) == 8
                b, tk = tile_hT()
                g_ = gate_room(n // 8, n % 8)
                gate_ok[n] = act.op(lambda e: e.activation(g_, PS[:, b, 0:256], ACT.Tanh, scale=0.5), tk, *(qk_ok if n < 8 else dn_end), *(fr_free[0] if n >= 24 else ()), *(qk2_ok if n >= 28 else ()))
                bk.read[b] = [gate_ok[n]]
            return unit

        BPOS = (0, 1, 3, 2)
        BT = lambda i: BTf[:, 1024 * BPOS[i]:1024 * BPOS[i] + 1024].rearrange("p (h c) -> p h c", h=4)
        bt_ok = {}
        FTq = [v.rearrange("p (h c) -> p h c", h=4) for v in (NN[:, 0:1024], KDT[:, 1024:2048])]
        ft_ok, fox_n = [], {}

        def fox_norm(ti, q):
            v4 = F[:, q, ti, :].rearrange("p (h d) -> p h d", h=4)
            c, a = sums(v4, 4, 128, f_ok[(ti, q)])
            r = power(c, 4, 1.0 / 128, a)
            fox_n[(ti, q)] = scale(v4, v4, c, 128, r)

        def fox_turn(ti, q):
            ft_ok.append(turn4([F[:, q, ti, 128 * h:128 * h + 128] for h in range(4)],
                               FTq[q][:, :, ti * 128:ti * 128 + 128], [fox_n[(ti, q)], *qk_ok, *kd_ok, *kg_ok], VW[:, W_FQ + q:W_FQ + q + 1]))

        sg = {}

        def sg_norm(ti):
            v4 = SV[:, ti, :].rearrange("p (g d) -> p g d", g=4)
            c, a = sums(v4, 4, 128, sv_ok[ti])
            r = power(c, 4, 1.0 / 128, a)
            a = scale(v4, v4, c, 128, r)
            sg[ti] = dve.op(lambda e: e.tensor_tensor(SV[:, ti, :], SV[:, ti, :], VW[:, W_SGG:W_SGG + 512], ALU.mult), a)

        def sg_mix(ti):
            b = bk.take()
            for g in range(4):
                f = lambda e, g=g: e.matmul(
                    PS[:, b, g * 128:g * 128 + 128], SW[:, g, :], SV[:, ti, g * 128:g * 128 + 128], start=True, stop=True)
                if g < 3:
                    pe.quiet(f, *((sg[ti], sw_ok, *bk.read[b]) if g == 0 else ()))
                else:
                    tk = pe.op(f)
            for g in range(4):
                u = SU[:, ti, g * 128:g * 128 + 128]
                r = dve.op(lambda e, g=g, u=u: e.scalar_tensor_tensor(
                    u, PS[:, b, g * 128:g * 128 + 128], VW[:, W_SGB + g:W_SGB + g + 1], u, ALU.add, ALU.mult), tk, su_ok[ti])
            bk.read[b] = [r]
            sg[ti] = r

        def sg_turn(ti):
            bt_ok[(2, ti)] = turn4([SU[:, ti, g * 128:g * 128 + 128] for g in range(4)], BT(2)[:, :, ti * 128:ti * 128 + 128],
                                   [sg[ti], *moe_end])

        CT1 = room("Hx", 512, 2)
        CT2 = RT[:, 256:512]
        ct_ok, ct_n, lat = [], {}, {}

        def latent_norm(ti):
            cq, ckv = MS[:, ti, 0:256], MS[:, ti, 256:384]
            c1, a1 = sums(MS[:, ti, 0:256].unsqueeze(1), 1, 256, ms_ok[ti])
            c2, a2 = sums(MS[:, ti, 256:384].unsqueeze(1), 1, 128, ms_ok[ti])
            r1 = power(c1, 1, 1.0 / 256, a1)
            r2 = power(c2, 1, 1.0 / 128, a2)
            lat[("kr", ti)] = sums(MS[:, ti, 384:448].unsqueeze(1), 1, 64, ms_ok[ti])
            ct_n[ti] = [dve.op(lambda e: e.tensor_scalar(cq, cq, c1, None, ALU.mult), r1),
                        dve.op(lambda e: e.tensor_scalar(ckv, ckv, c2, None, ALU.mult), r2)]

        def latent_turn(ti):
            b = bk.take()
            for i in range(3):
                f = lambda e, i=i: e.transpose(PS[:, b, i * 128:i * 128 + 128], MS[:, ti, i * 128:i * 128 + 128], ident)
                if i < 2:
                    pe.quiet(f, *((*ct_n[ti], *bk.read[b]) if i == 0 else ()))
                else:
                    tk = pe.op(f)
            for i in range(3):
                dst = CT1[:, i, ti * 128:ti * 128 + 128] if i < 2 else CT2[:, ti * 128:ti * 128 + 128]
                r = dve.op(lambda e, i=i, dst=dst: e.tensor_scalar(
                    dst, PS[:, b, i * 128:i * 128 + 128], VW[:, W_QN + i:W_QN + i + 1], None, ALU.mult), tk, *moe_end)
            bk.read[b] = [r]
            ct_ok.append(r)

        for n in range(8):
            bulk.append(gate_unit(n))
        job = lambda done, stage, f, *args: side.append((done, stage, lambda: f(*args)))
        for f, done, args in ((latent_norm, 0, ()), (latent_turn, 0, ()), (sg_norm, 8, ()), (sg_mix, 8, ()), (sg_turn, 8, ()),
                              (fox_norm, 12, (0,)), (fox_turn, 12, (0,)), (fox_norm, 16, (1,)), (fox_turn, 16, (1,))):
            for ti in range(2):
                job(done, 1, f, ti, *args)

        QD = R4[:, 0:1024].rearrange("p (t h d) -> p t h d", t=2, h=4)
        KB = R4[:, 1024:2048].rearrange("p (t h d) -> p t h d", t=2, h=4)
        T4 = R1.rearrange("p (w h c) -> p w h c", w=4, h=4)
        t4_ok = []
        kd_ok, kg_ok, vb_ok = [], [], []
        conv_end = [qt_ok[-1], qt_ok[-2], qt_ok[-3], qt_ok[-4]]
        for ti in range(2):
            c, a = sums(N[:, ti, 0:8, :], 8, 128, n_ok[(ti, 0)], n_ok[(ti, 1)])
            r = power(c, 8, 1.0, a)
            qr = dve.op(lambda e, c=c: e.tensor_scalar(c[:, 0:4], c[:, 0:4], 128.0 ** -0.5, None, ALU.mult), r)
            s_ = slice(4 * ti, 4 * ti + 4)
            qn = scale(N[:, ti, 0:4, :], N[:, ti, 0:4, :], c[:, 0:4], 128, qr)
            kn = scale(N[:, ti, 4:8, :], N[:, ti, 4:8, :], c[:, 4:8], 128, r)
            kb = scale(KB[:, ti], N[:, ti, 4:8, :], beta[:, ti, :], 128, kn, b_ok, *conv_end, dt_ok)
            qd = scale(QD[:, ti], N[:, ti, 0:4, :], eg[:, s_], 128, qn, e1)
            vb_ok.append(scale(N[:, ti, 8:12, :], N[:, ti, 8:12, :], beta[:, ti, :], 128, n_ok[(ti, 2)], b_ok))
            kg_ok.append(scale(KG[:, ti], N[:, ti, 4:8, :], bg[:, s_], 128, kn, bg_ok))
            kd_ok.append(scale(KD[:, ti], N[:, ti, 4:8, :], ed[:, s_], 128, kn, e2))
            fill(FILLS[2])
            turned = list(n_ok.values())
            for w, (src, a) in enumerate(((N[:, ti, 0:4], qn), (N[:, ti, 4:8], kn), (KB[:, ti], kb), (QD[:, ti], qd))):
                t4_ok.append(turn4([src[:, h, :] for h in range(4)], T4[:, w, :, ti * 128:ti * 128 + 128], [a] + turned,
                                   eng=dve if w % 2 else None))
        LT = BTf[:, 0:1024].rearrange("p (r c) -> p r c", r=8)
        QK = BTf[:, 1024:2048].rearrange("p (r c) -> p r c", r=8)
        lt_ok = []
        for w, dst, ok in ((2, LT, lt_ok), (0, QK, qk_ok)):
            for ti in range(2):
                b = bk.take()
                for h in range(4):
                    f = lambda e, b=b, h=h, ti=ti, w=w: e.matmul(
                        PS[:, b, h * 128:h * 128 + 128], T4[:, 1, h, ti * 128:ti * 128 + 128],
                        T4[:, w, h, ti * 128:ti * 128 + 128], start=True, stop=True)
                    if h < 3:
                        pe.quiet(f, *((*t4_ok, *bk.read[b]) if h == 0 else ()))
                    else:
                        tk = pe.op(f)
                r = dve.op(lambda e, b=b, dst=dst, ti=ti: e.tensor_tensor(
                    dst[:, 4 * ti:4 * ti + 4, :], PS[:, b, :].rearrange("p (h c) -> p h c", h=4),
                    DT[:, 4 * ti:4 * ti + 4, :], ALU.mult), tk, dt_ok)
                bk.read[b] = [r]
                ok.append(r)

        at["stage"] = 1
        sw_ok = dve.op(lambda e: e.tensor_tensor(SW, SW, bc(tri, 1, 4), ALU.mult), Lsw)

        X, XT, T1, M0, M1 = (v.rearrange("p (r c) -> p r c", r=8) for v in
                             (*(R4[:, 1024 * q:1024 * q + 1024] for q in range(4)), BTf[:, 2048:3072]))
        r4_free = [t4_ok[-1], t4_ok[-2], t4_ok[-3], t4_ok[-4], t4_ok[2], t4_ok[3]]
        id8 = bc(ident, 1, 8)

        def level_mask(n, dst, *after):
            return pool.op(lambda e: e.tensor_tensor(dst, LT, bc(KT[:, K_LEV + 128 * n:K_LEV + 128 * n + 128], 1, 8), ALU.mult), *after)

        m_ok = level_mask(0, M0, *lt_ok, *r4_free)
        m_next = level_mask(1, M1)
        xt_ok = [dve.op(lambda e: e.tensor_tensor(XT, id8, M0, ALU.subtract), m_ok, *r4_free)]
        x_ok = []
        for q in range(2):
            b = bk.take()
            for r in range(4):
                f = lambda e, b=b, r=r, q=q: e.transpose(PS[:, b, r * 128:r * 128 + 128], M0[:, 4 * q + r, :], ident)
                if r < 3:
                    pe.quiet(f, *((m_ok, *bk.read[b]) if r == 0 else ()))
                else:
                    tk = pe.op(f)
            x = dve.op(lambda e, b=b, q=q: e.tensor_tensor(
                X[:, 4 * q:4 * q + 4, :], bc(ident, 1, 4), PS[:, b, :].rearrange("p (r c) -> p r c", r=4), ALU.subtract), tk, *r4_free)
            bk.read[b] = [x]
            x_ok.append(x)

        def eight(lhs, rhs, *after):
            out = []
            for q in range(2):
                b = bk.take()
                for r in range(4):
                    f = lambda e, b=b, r=r, q=q: e.matmul(PS[:, b, r * 128:r * 128 + 128], lhs(4 * q + r), rhs(4 * q + r), start=True, stop=True)
                    if r < 3:
                        pe.quiet(f, *((*after, *bk.read[b]) if r == 0 else ()))
                    else:
                        tk = pe.op(f)
                out.append((b, tk))
            return out

        mt = [tk]
        for n in range(1, 6):
            M = (M0, M1)[n % 2]
            fill(FILLS[3])
            out = eight(lambda r, M=M: M[:, r, :], lambda r: X[:, r, :], m_next, *x_ok)
            t1_ok = []
            for q, (b, tk) in enumerate(out):
                dst = T1[:, 4 * q:4 * q + 4, :]
                src = PS[:, b, :].rearrange("p (r c) -> p r c", r=4)
                if q == 0:
                    r = act.op(lambda e, dst=dst, src=src: e.copy(dst, src), tk, *mt, *r4_free)
                else:
                    r = dve.op(lambda e, dst=dst, src=src: e.tensor_copy(dst, src), tk, *mt)
                bk.read[b] = [r]
                t1_ok.append(r)
            if n < 5:
                m_next = level_mask(n + 1, (M1, M0)[n % 2], tk, *mt)
            fill(FILLS[4])
            outT = eight(lambda r: T1[:, r, :], lambda r: XT[:, r, :], *t1_ok, *xt_ok)
            new_x = []
            if n < 5:
                outX = eight(lambda r: XT[:, r, :], lambda r: T1[:, r, :])
                for q, (b, tk) in enumerate(outX):
                    v = X[:, 4 * q:4 * q + 4, :]
                    r = dve.op(lambda e, v=v, b=b: e.tensor_tensor(v, v, PS[:, b, :].rearrange("p (r c) -> p r c", r=4), ALU.subtract), tk)
                    bk.read[b] = [r]
                    new_x.append(r)
                mt = [tk]
            last = outX[1][1] if n < 5 else outT[1][1]
            new_t = []
            for q, (b, tk) in enumerate(outT):
                v = XT[:, 4 * q:4 * q + 4, :]
                r = dve.op(lambda e, v=v, b=b: e.tensor_tensor(v, v, PS[:, b, :].rearrange("p (r c) -> p r c", r=4), ALU.subtract), tk, last)
                bk.read[b] = [r]
                new_t.append(r)
            x_ok, xt_ok = new_x, new_t

        U = M0
        WT = M1
        inv_end = [new_t[0], new_t[1], last]
        out = eight(lambda r: XT[:, r, :], lambda r: N[:, r // 4, 8 + r % 4, :], *xt_ok, *vb_ok)
        u_ok, w_ok = [], []
        for q, (b, tk) in enumerate(out):
            r = act.op(lambda e, b=b, q=q: e.copy(U[:, 4 * q:4 * q + 4, :], PS[:, b, :].rearrange("p (r c) -> p r c", r=4)), tk, *inv_end)
            bk.read[b] = [r]
            u_ok.append(r)
        out = eight(lambda r: KG[:, r // 4, r % 4, :], lambda r: XT[:, r, :], *kg_ok)
        for q, (b, tk) in enumerate(out):
            r = dve.op(lambda e, b=b, q=q: e.tensor_copy(WT[:, 4 * q:4 * q + 4, :], PS[:, b, :].rearrange("p (r c) -> p r c", r=4)), tk, *inv_end)
            bk.read[b] = [r]
            w_ok.append(r)
        uw_end = tk

        Nf = NN
        MQ = Nf[:, 1024:2560].rearrange("p (t h d) -> p t h d", t=2, h=4)
        MK = R4[:, 1024:2048].rearrange("p (t h d) -> p t h d", t=2, h=4)
        MR = Nf[:, 2560:3072].rearrange("p (t h d) -> p t h d", t=2, h=4)
        MV = KG
        Q1, Q2 = (Ff[:, 1024 * q:1024 * q + 1024].rearrange("p (h c) -> p h c", h=4) for q in range(2))
        K1, K2 = (SUV[:, 1024 * q:1024 * q + 1024].rearrange("p (h c) -> p h c", h=4) for q in range(2))
        mq_ok, mk_ok, mv_ok = {}, {}, {}
        nn_free = [uw_end, *w_ok, *kg_ok, *kd_ok, *vb_ok]
        upw = {}

        def latent_q(ti, nb):
            uq = upw["q"]
            b, tk = tile_T(None, 0, 2, lambda k: CT1[:, k, ti * 128:ti * 128 + 128],
                           lambda k: uq[k][1][:, 384 * nb:384 * nb + 384], 384, uq[0][2], uq[1][2], *ct_ok)
            r = act.op(lambda e: e.copy(MQ[:, ti, 2 * nb:2 * nb + 2, :], PS[:, b, 0:384].rearrange("p (h d) -> p h d", h=2)), tk, *nn_free)
            bk.read[b] = [r]
            mq_ok[(ti, nb)] = r
            if ti == 1 and nb == 1:
                raw_used[uq[0][0]] = raw_used[uq[1][0]] = tk

        def latent_kv(ti, nb):
            ukv = upw["kv"]
            b, tk = tile_T(None, 0, 1, lambda k: CT2[:, ti * 128:ti * 128 + 128],
                           lambda k: ukv[1][:, 512 * nb:512 * nb + 512], 512, ukv[2], *ct_ok)
            src = PS[:, b, :].rearrange("p (h d) -> p h d", h=2)
            r = act.op(lambda e: e.copy(MK[:, ti, 2 * nb:2 * nb + 2, :], src[:, :, 0:128]), tk, *nn_free)
            r2 = act.op(lambda e: e.copy(MV[:, ti, 2 * nb:2 * nb + 2, :], src[:, :, 128:256]), tk, *nn_free)
            bk.read[b] = [r2]
            mk_ok[(ti, nb)] = r
            mv_ok[(ti, nb)] = r2
            if ti == 1 and nb == 1:
                raw_used[ukv[0]] = tk
                rt_free[0] = [tk]

        gq, gk = VW[:, W_QG:W_QG + 192], VW[:, W_KG:W_KG + 192]
        rt_free, fr_free = [[]], [[]]

        def rope_nat(x, ti, *after):
            w = [RT[:, 128 * i:128 * i + 128].rearrange("p (h d) -> p h d", h=4) for i in range(4)]
            cs, sn = bc(cosN[:, ti, :], 1, 4), bc(sinN[:, ti, :], 1, 4)
            x1, x2 = x[:, :, 0:32], x[:, :, 32:64]
            p = []
            for i, (a_, b_) in enumerate(((x1, cs), (x2, sn), (x2, cs), (x1, sn))):
                p.append(pool.op(lambda e, i=i, a_=a_, b_=b_: e.tensor_tensor(w[i], a_, b_, ALU.mult), k_tab, *after, *rt_free[0]))
            a = pool.op(lambda e: e.tensor_tensor(x1, w[0], w[1], ALU.subtract), *p)
            b = pool.op(lambda e: e.tensor_tensor(x2, w[2], w[3], ALU.add), *p)
            rt_free[0] = [b]
            return [a, b]

        qk2_ok = []

        def query_square(ti):
            lat[("q2", ti)] = squares_of(MQ[:, ti], 4, 192, mq_ok[(ti, 0)], mq_ok[(ti, 1)])

        def query_power(ti):
            c, a = sums_of(lat[("q2", ti)])
            lat[("qr", ti)] = c, power(c, 4, 1.0 / 192, a)

        def query_norm(ti):
            c, r = lat[("qr", ti)]
            a = scale(MQ[:, ti], MQ[:, ti], c, 192, r)
            a = pool.op(lambda e: e.tensor_tensor(MQ[:, ti], MQ[:, ti], bc(gq, 1, 4), ALU.mult), a)
            lat[("q", ti)] = (a, rope_nat(MQ[:, ti, :, 128:192], ti, a))

        def query_turn(ti):
            a, rp = lat[("q", ti)]
            tsl = slice(ti * 128, ti * 128 + 128)
            qk2_ok.append(turn4([MQ[:, ti, h, 0:128] for h in range(4)], Q1[:, :, tsl], [a, *ft_ok]))
            qk2_ok.append(turn4([MQ[:, ti, h, 128:192] for h in range(4)], Q2[0:64, :, tsl], [*rp, *ft_ok], rows=64))

        def key_square(ti):
            lat[("k2", ti)] = squares_of(MK[:, ti], 4, 128, mk_ok[(ti, 0)], mk_ok[(ti, 1)])

        def key_power(ti):
            c, a = sums_of(lat[("k2", ti)])
            c2, a2 = lat[("kr", ti)]
            a = dve.op(lambda e: e.tensor_scalar(c, c, c2, None, ALU.add), a, a2)
            lat[("kc", ti)] = c, power(c, 4, 1.0 / 192, a)

        def key_norm(ti):
            kr = MS[:, ti, 384:448]
            c, r = lat[("kc", ti)]
            a = scale(MK[:, ti], MK[:, ti], c, 128, r)
            b = dve.op(lambda e: e.tensor_tensor(MR[:, ti], bc(kr, 1, 4), bc(c, 2, 64), ALU.mult), r, *nn_free)
            a = pool.op(lambda e: e.tensor_tensor(MK[:, ti], MK[:, ti], bc(gk[:, 0:128], 1, 4), ALU.mult), a)
            b = pool.op(lambda e: e.tensor_tensor(MR[:, ti], MR[:, ti], bc(gk[:, 128:192], 1, 4), ALU.mult), b)
            lat[("k", ti)] = (a, rope_nat(MR[:, ti], ti, b))

        def key_turn(ti):
            a, rp = lat[("k", ti)]
            tsl = slice(ti * 128, ti * 128 + 128)
            free = [bt_ok[(2, 0)], bt_ok[(2, 1)], sg[0], sg[1]]
            qk2_ok.append(turn4([MK[:, ti, h, :] for h in range(4)], K1[:, :, tsl], [a, *free]))
            qk2_ok.append(turn4([MR[:, ti, h, :] for h in range(4)], K2[0:64, :, tsl], [*rp, *free], rows=64))

        def request_q():
            upw["q"] = [raw_piece(t["w2_uq"][k]) for k in range(2)]

        def all_q():
            for ti in range(2):
                for nb in range(2):
                    latent_q(ti, nb)
            upw["kv"] = raw_piece(t["w2_ukv"])

        def all_kv():
            for ti in range(2):
                for nb in range(2):
                    latent_kv(ti, nb)

        for f in (request_q, all_q, all_kv):
            job(20, 2, f)
        def steps(*fs):
            for f, ti in fs:
                f(ti)

        for fs in (((query_square, 0),), ((query_power, 0), (key_square, 0)),
                   ((query_norm, 0), (key_power, 0), (query_square, 1)), ((key_norm, 0), (query_power, 1), (key_square, 1)),
                   ((query_turn, 0), (query_norm, 1), (key_power, 1)), ((key_turn, 0), (key_norm, 1)),
                   ((query_turn, 1),), ((key_turn, 1),)):
            job(20, 2, steps, *fs)

        at["stage"] = 2

        ST = R4[:, 0:512].rearrange("p (h d) -> p h d", h=4)
        SD = R4[:, 512:1024].rearrange("p (h d) -> p h d", h=4)
        VN = R4[:, 2048:2560].rearrange("p (h d) -> p h d", h=4)
        ON = R1[:, 2048:3072].rearrange("p (t h d) -> p t h d", t=2, h=4)
        s_t = dve.op(lambda e: e.memset(ST, 0.0), *inv_end)
        on_ok = [[], []]
        vn_free = []
        oq_free = [uw_end]
        for c in range(4):
            ti, r0 = c // 2, 64 * (c % 2)
            rows = slice(r0, r0 + 64)
            b = bk.take()
            for h in range(4):
                f = lambda e, b=b, h=h, ti=ti, rows=rows, r0=r0: e.matmul(
                    PS[rows, b, h * 128:h * 128 + 128], WT[:, 4 * ti + h, r0:r0 + 64], ST[:, h, :], start=True, stop=True)
                if h < 3:
                    pe.quiet(f, *((s_t, *w_ok, *bk.read[b]) if h == 0 else ()))
                else:
                    tk = pe.op(f)
            vn = dve.op(lambda e, b=b, ti=ti, rows=rows: e.tensor_tensor(
                VN[rows], U[rows, 4 * ti:4 * ti + 4, :], PS[rows, b, :].rearrange("p (h d) -> p h d", h=4), ALU.subtract),
                tk, *u_ok, *vn_free, *inv_end)
            bk.read[b] = [vn]
            ob_ = bk.take()
            sb_ = bk.take()
            if c < 3:
                sd = dve.op(lambda e, c=c, ti=ti: e.tensor_tensor(
                    SD, ST, bc(egl[:, 8 * (c % 2) + 4 * ti:8 * (c % 2) + 4 * ti + 4], 2, 128), ALU.mult), s_t, e3, *inv_end)
                for h in range(4):
                    f = lambda e, h=h, ti=ti, rows=rows, sb_=sb_: e.matmul(
                        PS[:, sb_, h * 128:h * 128 + 128], KD[rows, ti, h, :], VN[rows, h, :], start=True, stop=True)
                    if h < 3:
                        pe.quiet(f, *((vn, *kd_ok, *bk.read[sb_]) if h == 0 else ()))
                    else:
                        tk = pe.op(f)
            for h in range(4):
                pe.quiet(lambda e, h=h, ti=ti, r0=r0, rows=rows, ob_=ob_: e.matmul(
                    PS[rows, ob_, h * 128:h * 128 + 128], T4[:, 3, h, ti * 128 + r0:ti * 128 + r0 + 64], ST[:, h, :],
                    start=True, stop=False), *((vn, s_t, *bk.read[ob_]) if h == 0 else ()))
                f = lambda e, h=h, ti=ti, r0=r0, rows=rows, ob_=ob_: e.matmul(
                    PS[rows, ob_, h * 128:h * 128 + 128], QK[rows, 4 * ti + h, r0:r0 + 64], VN[rows, h, :],
                    start=False, stop=True)
                if h < 3:
                    pe.quiet(f, *qk_ok)
                else:
                    tko = pe.op(f)
            vn_free = [tko]
            if c < 3:
                s_t = dve.op(lambda e, sb_=sb_: e.tensor_tensor(
                    ST, SD, PS[:, sb_, :].rearrange("p (h d) -> p h d", h=4), ALU.add), tk, sd, tko)
                bk.read[sb_] = [s_t]
            r = act.op(lambda e, ti=ti, rows=rows, ob_=ob_: e.copy(
                ON[rows, ti, :, :], PS[rows, ob_, :].rearrange("p (h d) -> p h d", h=4)), tko, *oq_free)
            bk.read[ob_] = [r]
            on_ok[ti].append(r)
            fill(FILLS[5])
        DM = Z.rearrange("p t c -> p (t c)").rearrange("p (j t c) -> p j t c", j=2, t=2)
        dm_ok, dm_free = {}, [[], []]
        MB = KT[:, K_MB:K_MB + 256]

        R0, R1_ = R4[:, 0:256], RD
        rows_ok = {}

        def row_start(h):
            rows_ok[h] = [
                dve.op(lambda e: e.tensor_scalar(R0, KT[:, K_TRI:K_TRI + 256], lf[:, 0, h:h + 1], None, ALU.mult), l_ok, *fr_free[0], *on_ok[0], *on_ok[1]),
                dve.op(lambda e: e.tensor_scalar(R1_, tri, lf[:, 1, h:h + 1], None, ALU.mult), l_ok, *fr_free[0], *on_ok[0], *on_ok[1])]

        def row_decay(h):
            j = h % 2
            a, c = rows_ok[h]
            b = bk.take()
            pe.quiet(lambda e: e.matmul(PS[:, b, 0:256], one, R0, start=True, stop=False), a, c, *bk.read[b])
            tk = pe.op(lambda e: e.matmul(PS[:, b, 128:256], one, R1_, start=False, stop=True))
            fr_free[0] = [tk]
            r = []
            for ti in range(2):
                nk = 128 * ti + 128
                r.append(dve.op(lambda e, ti=ti, nk=nk: e.scalar_tensor_tensor(
                    DM[:, j, ti, 0:nk], PS[:, b, 0:nk], GC[:, 32 + 4 * ti + h:33 + 4 * ti + h], MB[:, 256 - nk:256],
                    ALU.subtract, ALU.subtract, reverse1=True), tk, gc_ok, *dm_free[j]))
            bk.read[b] = r
            dm_ok[h] = r

        dn_end = []
        for ti in range(2):
            c, a = sums(ON[:, ti], 4, 128, *on_ok[ti])
            r = power(c, 4, 1.0 / 128, a)
            a = scale(ON[:, ti], ON[:, ti], c, 128, r)
            a = dve.op(lambda e, ti=ti: e.tensor_tensor(ON[:, ti], ON[:, ti], Z[:, ti, :].rearrange("p (h d) -> p h d", h=4), ALU.mult), a, z_ok[ti])
            if ti == 0:
                row_start(0)
            else:
                row_decay(0)
            fill(FILLS[6])
            bt_ok[(0, ti)] = turn4([ON[:, ti, h, :] for h in range(4)], BT(0)[:, :, ti * 128:ti * 128 + 128], [a], VW[:, W_OUTG:W_OUTG + 1])
            dn_end.append(bt_ok[(0, ti)])
        dn_end += [(pe.sem, pe.n), (dve.sem, dve.n), (act.sem, act.n), (pool.sem, pool.n)]

        at["stage"] = 3
        for n in range(8, 32):
            bulk.append(gate_unit(n))

        sr = small(12)
        sc_free, pt_free = [list(dn_end) for _ in range(4)], [list(dn_end) for _ in range(4)]
        SCs = [KDT[:, 256 * j:256 * j + 256] for j in range(4)]
        PTs = [SC[:, 0, :], SC[:, 1, :], PT[:, 0, :], PT[:, 1, :]]
        def score(u):
            fox, h, ti = u
            nk = 128 * ti + 128
            j = cnt[0] % 4
            cnt[0] += 1
            q0 = slice(ti * 128, ti * 128 + 128)
            b = bk.take()
            if fox:
                if h < 3:
                    (row_decay if ti else row_start)(h + 1)
                tk = pe.op(lambda e: e.matmul(PS[:, b, 0:nk], FTq[0][:, h, q0], FTq[1][:, h, 0:nk], start=True, stop=True), *ft_ok, *bk.read[b])
                bias, sc, w = DM[:, h % 2, ti, 0:nk], 128.0 ** -0.5, dm_ok[h]
            else:
                pe.quiet(lambda e: e.matmul(PS[:, b, 0:nk], Q1[:, h, q0], K1[:, h, 0:nk], start=True, stop=False), *qk2_ok, *bk.read[b])
                tk = pe.op(lambda e: e.matmul(PS[:, b, 0:nk], Q2[0:64, h, q0], K2[0:64, h, 0:nk], start=False, stop=True))
                bias, sc, w = MB[:, 256 - nk:256], 192.0 ** -0.5, []
            S_ = SCs[j][:, 0:nk]
            m, l, rc = sr[:, 3 * j:3 * j + 1], sr[:, 3 * j + 1:3 * j + 2], sr[:, 3 * j + 2:3 * j + 3]
            a = dve.op(lambda e: e.scalar_tensor_tensor(S_, PS[:, b, 0:nk], sc, bias, ALU.mult, ALU.add), tk, *w, *sc_free[j])
            bk.read[b] = [a]
            if fox:
                dm_free[h % 2] = [a]
            a = dve.op(lambda e: e.tensor_reduce(m, S_, AX, ALU.max, negate=True), a)
            a = act.op(lambda e: e.activation(S_, S_, ACT.Exp, bias=m, scale=1.0, accum_out=l), a)
            a = dve.op(lambda e: e.reciprocal(rc, l), a)
            a = dve.op(lambda e: e.tensor_scalar(S_, S_, rc, None, ALU.mult), a)
            return (u, j, a)

        oacc = {}

        def turn_scores(state):
            (fox, h, ti), j, tok = state
            b = bk.take()
            for kt in range(ti + 1):
                f = lambda e, kt=kt: e.transpose(PS[:, b, kt * 128:kt * 128 + 128], SCs[j][:, kt * 128:kt * 128 + 128], ident)
                w = (tok, *bk.read[b]) if kt == 0 else ()
                if kt < ti:
                    pe.quiet(f, *w)
                else:
                    tk = pe.op(f, *w)
            sc_free[j] = [tk]
            nk = 128 * ti + 128
            r = act.op(lambda e: e.copy(PTs[j][:, 0:nk], PS[:, b, 0:nk]), tk, *pt_free[j])
            bk.read[b] = [r]
            return (fox, h, ti), j, r

        def value(state):
            (fox, h, ti), j, r = state
            b2 = bk.take()
            for kt in range(ti + 1):
                vv = F[:, 2, kt, 128 * h:128 * h + 128] if fox else MV[:, kt, h, :]
                f = lambda e, kt=kt, vv=vv: e.matmul(PS[:, b2, 0:128], vv, PTs[j][:, kt * 128:kt * 128 + 128], start=(kt == 0), stop=(kt == ti))
                w = (r, *([f_ok[(0, 2)], f_ok[(1, 2)]] if fox else mv_ok.values()), *bk.read[b2]) if kt == 0 else ()
                if kt < ti:
                    pe.quiet(f, *w)
                else:
                    tk = pe.op(f, *w)
            pt_free[j] = [tk]
            br = 3 if fox else 1
            r = act.op(lambda e: e.copy(BT(br)[:, h, ti * 128:ti * 128 + 128], PS[:, b2, 0:128]), tk)
            bk.read[b2] = [r]
            bt_ok[(br, h, ti)] = r

        cnt = [0]
        waiting = []
        while side and side[0][1] < 2:
            fill(1)
        for u in [(fox, h, ti) for fox in (True, False) for h in range(4) for ti in range(2)]:
            while side and not u[0]:
                fill(1)
            turned = turn_scores(waiting.pop(0)) if len(waiting) >= LAG else None
            waiting.append(score(u))
            fill(1)
            if turned is not None:
                value(turned)
        for state in waiting:
            turned = turn_scores(state)
            fill(1)
            value(turned)
        while bulk:
            fill(1)

        gate_end = [(dve.sem, dve.n), (pe.sem, pe.n), (act.sem, act.n), (pool.sem, pool.n)]
        MT = NN[:, 0:2048].rearrange("p (m c) -> p m c", m=8)
        TM = SC
        tm_free = [list(gate_end), list(gate_end)]
        n = 0
        mt_ok = [None] * 8
        BH = hr.rearrange("p q (j c) -> p q j c", j=2)
        bh_free = [[], []]
        four = Banks(range(4))
        for b in range(6):
            if b < 4:
                four.read[b] = bk.read[b]
            else:
                open_read[b] = bk.read[b]
        bk = four

        def split_branch(i):
            src = BTf[:, 1024 * BPOS[i]:1024 * BPOS[i] + 1024]
            hi, lo = BH[:, 0, i % 2, :], BH[:, 1, i % 2, :]
            ok = [r for key, r in bt_ok.items() if key[0] == i]
            a = act.op(lambda e: e.copy(hi, src), *ok, *gate_end, *bh_free[i % 2])
            return [a, dve.op(lambda e: e.tensor_tensor(lo, src, hi.bitcast(F32), ALU.subtract), a)]

        ready = [split_branch(0), split_branch(1)]
        for i in range(4):
            B_ = [BH[:, p, i % 2, :].rearrange("p (k c) -> p k c", k=4) for p in range(2)]
            for m in range(8):
                if m % 2 == 0:
                    hi, lo, ok = piece()
                    v = [x.rearrange("p (m k c) -> p m k c", m=2, k=4) for x in (hi, lo)]
                b, tk = tile3(4, lambda p, k, v=v, m=m: v[p][:, m % 2, k, :], lambda p, k, B_=B_: B_[p][:, k, :], 256, *ok, *ready[i])
                if m % 2 == 1:
                    release(tk)
                g_ = gate_room(i, m)
                if i == 0:
                    mt_ok[m] = dve.op(lambda e, b=b, g_=g_, m=m: e.scalar_tensor_tensor(
                        MT[:, m, :], g_, 1.0, PS[:, b, 0:256], ALU.add, ALU.mult), tk, *gate_end)
                    bk.read[b] = [mt_ok[m]]
                else:
                    j = n % 2
                    n += 1
                    c = dve.op(lambda e, b=b, g_=g_, j=j: e.scalar_tensor_tensor(
                        TM[:, j, :], g_, 1.0, PS[:, b, 0:256], ALU.add, ALU.mult), tk, *tm_free[j])
                    bk.read[b] = [c]
                    mt_ok[m] = pool.op(lambda e, m=m, j=j: e.tensor_tensor(MT[:, m, :], MT[:, m, :], TM[:, j, :], ALU.add), mt_ok[m], c)
                    tm_free[j] = [mt_ok[m]]
            bh_free[i % 2] = [tk]
            if i < 2:
                ready.append(split_branch(i + 2))
        MTh, MTl = (hr[:, p, :].rearrange("p (m c) -> p m c", m=8) for p in range(2))
        mts = []
        for m in range(8):
            a = act.op(lambda e, m=m: e.mul(MTh[:, m, :], MT[:, m, :], 0.5), mt_ok[m], tk)
            mts.append((a, dve.op(lambda e, m=m: e.scalar_tensor_tensor(
                MTl[:, m, :], MT[:, m, :], 0.5, MTh[:, m, :].bitcast(F32), ALU.mult, ALU.subtract), a)))

        quad = {(ti, db): 4 + 2 * ti + db for ti in range(2) for db in range(2)}
        two = [slice(0, 512), slice(512, 1024)]
        toks = {}
        for c in range(8):
            hi, lo, ok = piece()
            tk = rows3(quad, c == 0, c == 7, lambda p, ti, c=c: (MTh, MTl)[p][:, c, ti * 128:ti * 128 + 128],
                       lambda p, hi=hi, lo=lo: (hi, lo)[p], two, (*ok, *mts[c]), toks)
            release(tk)
        h_ok = {}
        for (ti, db), b in quad.items():
            hv = H[:, ti, db * 512:db * 512 + 512]
            h_ok[(ti, db)] = dve.op(lambda e, hv=hv, b=b: e.tensor_tensor(hv, hv, PS[:, b, :], ALU.add), toks[(ti, db)])
            open_read[b] = [h_ok[(ti, db)]]
        merge_end = [(dve.sem, dve.n), (pe.sem, pe.n), (act.sem, act.n), (pool.sem, pool.n)]

        mid.close()
        fh = sb1("fh", 16384, F32R, second)[:, :].rearrange("p (q m c) -> p q m c", q=2, m=32)
        late = sb1("late", 2048 + 1024 + 4096, F32, second)
        XB2 = late[:, 0:2048].rearrange("p (t c) -> p t c", t=2)
        tmp2 = late[:, 2048:3072]
        tmp3 = late[:, 6144:7168]
        RL = late[:, 3072:7168].rearrange("p (j q c) -> p j q c", j=8, q=2)
        h2_ok, sqs, done = [], {}, []
        for (ti, db) in quad:
            x = fr[:, 8 + 2 * ti + db:9 + 2 * ti + db]
            sqs[(ti, db)] = act.op(lambda e, ti=ti, db=db, x=x: e.activation(
                RL[:, 2 * ti + db, :, :].rearrange("p q c -> p (q c)"), H[:, ti, db * 512:db * 512 + 512], ACT.Square, accum_out=x),
                h_ok[(ti, db)], *merge_end)
        for ti in range(2):
            x, y = fr[:, 8 + 2 * ti:9 + 2 * ti], fr[:, 9 + 2 * ti:10 + 2 * ti]
            a = dve.op(lambda e, x=x, y=y: e.tensor_scalar(x, x, y, None, ALU.add), sqs[(ti, 0)], sqs[(ti, 1)])
            a = dve.op(lambda e, x=x: e.tensor_scalar(x, x, 1.0 / D, EPS, ALU.mult, ALU.add), a)
            a = power1(x, a)
            if ti == 0:
                done.append(dve.op(lambda e, x=x: e.tensor_scalar(XB2[:, 0, :], H[:, 0, :], x, None, ALU.mult), a))
            else:
                done.append(act.op(lambda e, x=x: e.activation(XB2[:, 1, :], H[:, 1, :], ACT.Copy, scale=x), a))
        h2_ok += turn_two(XB2, vec[:, V_N2:V_N2 + 8], [tmp2, tmp3], done, *merge_end)
        ff_ok = []
        rl_free = [[] for _ in range(8)]
        squares = []

        def split_hidden(m):
            j, tok = squares[m]
            s_, hi, lo = RL[:, j, 1, :], fh[:, 0, m, :], fh[:, 1, m, :]
            c = act.op(lambda e: e.copy(hi, s_), tok, *merge_end)
            a = dve.op(lambda e: e.tensor_tensor(lo, s_, hi.bitcast(F32), ALU.subtract), c)
            rl_free[j] = [a]
            ff_ok.append((c, a))

        for m in range(32):
            b, tk = tile_hT(*h2_ok)
            j = m % 8
            r_, s_ = RL[:, j, 0, :], RL[:, j, 1, :]
            a = act.op(lambda e, b=b, r_=r_: e.activation(r_, PS[:, b, 0:256], ACT.Relu), tk, *merge_end, *rl_free[j])
            bk.read[b] = [a]
            squares.append((j, dve.op(lambda e, r_=r_, s_=s_: e.tensor_tensor(s_, r_, r_, ALU.mult), a)))
            if m > 0:
                split_hidden(m - 1)
        split_hidden(31)
        toks = {}
        for m in range(32):
            hi, lo, ok = piece()
            tk = rows3(quad, m == 0, m == 31, lambda p, ti, m=m: fh[:, p, m, ti * 128:ti * 128 + 128],
                       lambda p, hi=hi, lo=lo: (hi, lo)[p], two, (*ok, *ff_ok[m]), toks)
            release(tk)
        for (ti, db), b in quad.items():
            hv = H[:, ti, db * 512:db * 512 + 512]
            r = dve.op(lambda e, hv=hv, b=b: e.tensor_tensor(hv, hv, PS[:, b, :], ALU.add), toks[(ti, db)])
            c_o = [sem(f"c_o{ti}{db}"), 0]
            outs.append(act.dma(lambda e, hv=hv, ti=ti, db=db: e.dma_start(t["out"][:, ti, db * 512:db * 512 + 512], hv), c_o, r))
        act.quiet(None, *outs)

        for n, (src, after) in enumerate(stream2):
            dst = raw[:, (n % RAW) * 1024:(n % RAW) * 1024 + src.shape[1]]
            sp.dma(lambda e, dst=dst, src=src: e.dma_start(dst, src), raw_sem[n % RAW], *after())

        block = ctx.enter_context(nc.Block())

        @block.sync
        def _(e):
            sp.emit(e)

        @block.scalar
        def _(e):
            act.emit(e)

        @block.vector
        def _(e):
            dve.emit(e)

        @block.gpsimd
        def _(e):
            pool.emit(e)

        @block.tensor
        def _(e):
            pe.emit(e)


def pack_T(w):
    K, N = w.shape
    return np.ascontiguousarray(w.reshape(K // 128, 128, N // 256, 256).transpose(2, 1, 0, 3)).reshape(N // 256, 128, -1)


def pack_N(w):
    K, N = w.shape
    a = w.reshape(K // 512, 4, 128, N // 512, 512).transpose(3, 0, 2, 1, 4)
    return np.ascontiguousarray(a).reshape(-1, 128, 2048)


def tiles(w):
    return np.ascontiguousarray(w.reshape(8, 128, -1, 128).transpose(2, 1, 0, 3)).reshape(-1, 128, 1024)


def blocks(w):
    return np.ascontiguousarray(w.reshape(4, 2, 128, -1, 512).transpose(3, 0, 2, 1, 4)).reshape(-1, 128, 1024)


def pack_R(w):
    K, N = w.shape
    return np.ascontiguousarray(w.reshape(K // 256, 2, 128, N).transpose(0, 2, 1, 3)).reshape(-1, 128, 2 * N)


def col(v):
    return np.ascontiguousarray(v.reshape(-1, 128).T)


def layout(i):
    a = {}
    a["x"] = np.ascontiguousarray(i["x"][0].reshape(2, 128, D).transpose(1, 0, 2))
    a["meta"] = np.ascontiguousarray(i["meta_tokens"])
    a["cst"] = constants()
    w = i["w_in"][0]
    order = [w[:, 512:1024], w[:, 0:512]]
    tri = [w[:, o + 128 * m:o + 128 * m + 128] for m in range(4) for o in (1536, 2560, 2048)]
    a["w_in"] = np.concatenate([pack_T(order[0]), pack_T(order[1]), pack_N(w[:, 1024:1536]), pack_T(np.concatenate(tri, 1))])
    a["w_out"] = pack_R(i["w_out"][0])
    for n in ("w_gate", "w_up", "w_down"):
        a[n] = np.ascontiguousarray(i[n][0])
    v = np.zeros((P, NVEC), np.float32)
    v[:, V_MIXG:V_MIXG + 8] = col(i["mix_norm_g"][0])
    cw = i["conv_w"][0]
    for m in range(4):
        for k in range(3):
            v[:, V_CONV + 3 * m + k] = cw[k, 128 * m:128 * m + 128]
    v[:, V_SUB] = i["attn_subln_g"][0]
    for j, n in enumerate(("lambda_q1", "lambda_k1", "lambda_q2", "lambda_k2")):
        v[:, V_LAM + 64 * j:V_LAM + 64 * j + 64] = i[n][0][None, :]
    v[:, V_WR:V_WR + 128] = i["w_router"][0].reshape(8, 128, 16).transpose(1, 0, 2).reshape(128, 128)
    v[:, V_N2:V_N2 + 8] = col(i["norm2_g_2"][0])
    a["vec"] = v
    g = np.zeros((2, P, D), np.float32)
    g[0] = i["ffn_norm_g"][0][None, :]
    g[1] = i["final_norm_g"][None, :]
    a["gbc"] = g
    a["pos"] = np.ascontiguousarray(i["positions_2"][0].reshape(2, 128).T)
    w = i["w_in_2"][0]
    q_, z_, a_, b_, cq, ckv, kr, su, sv, fq, ff, gt = np.split(
        w, np.cumsum([1536, 512, 4, 4, 256, 128, 64, 512, 512, 1536, 4])[:11], axis=1)
    misc = np.concatenate([cq, ckv, kr, a_, b_, ff, np.zeros((D, 52), np.float32)], 1)
    rows = lambda w: w.reshape(-1, 128, 1024)
    a["w2"] = np.concatenate([
        tiles(q_), blocks(np.concatenate([misc, z_, su, sv, fq], 1)), tiles(gt),
        *(x.reshape(4, 128, 4, 2, 128).transpose(2, 1, 3, 0, 4).reshape(4, 128, 1024) for x in i["w_branch_2"][0]),
        rows(i["w_out_2"][0]), tiles(i["w_ff1_2"][0]), rows(i["w_ff2_2"][0])])
    a["w2_uq"] = np.ascontiguousarray(i["mla_w_uq_2"][0].reshape(2, 128, 768))
    a["w2_ukv"] = np.ascontiguousarray(i["mla_w_ukv_2"][0])
    a["sgw"] = np.ascontiguousarray(i["sg_w_s_2"][0].transpose(2, 0, 1))
    v = np.zeros((P, NW2), np.float32)
    v[:, W_N1:W_N1 + 8] = col(i["norm1_g_2"][0])
    v[:, W_CONV:W_CONV + 48] = i["dn_conv_w_2"][0].reshape(4, 12, 128).transpose(2, 1, 0).reshape(128, 48)
    v[:, W_DT:W_DT + 4] = i["dn_dt_bias_2"][0][None, :]
    v[:, W_ALOG:W_ALOG + 4] = i["dn_a_log_2"][0][None, :]
    v[:, W_OUTG] = i["dn_out_norm_g_2"][0]
    v[:, W_QN:W_QN + 2] = col(i["mla_q_norm_g_2"][0])
    v[:, W_KVN] = i["mla_kv_norm_g_2"][0]
    v[:, W_QG:W_QG + 192] = i["mla_qk_q_g_2"][0][None, :]
    v[:, W_KG:W_KG + 192] = i["mla_qk_k_g_2"][0][None, :]
    v[:, W_SGB:W_SGB + 4] = i["sg_b_s_2"][0].T
    v[:, W_FQ] = i["fox_q_norm_g_2"][0]
    v[:, W_FK] = i["fox_k_norm_g_2"][0]
    v[:, W_FB:W_FB + 4] = i["fox_f_bias_2"][0][None, :]
    v[:, W_SGG:W_SGG + 512] = i["sg_v_norm_g_2"][0].reshape(1, 512)
    a["kw2"] = np.concatenate([constants_2(), v], 1)
    return a


def kernel(**inputs):
    import concourse.bacc as bacc
    from concourse.bass_utils import run_bass_kernel_spmd

    arrays = layout({n: np.asarray(a) for n, a in inputs.items()})
    nc = bacc.Bacc("TRN2", target_bir_lowering=False, num_devices=1)
    t = {n: nc.dram_tensor(f"in_{n}", a.shape, mybir.dt.from_np(a.dtype), kind="ExternalInput").ap()
         for n, a in arrays.items()}
    t["out"] = nc.dram_tensor("out_y", (P, 2, D), F32, kind="ExternalOutput").ap()
    program(nc, t)
    r = run_bass_kernel_spmd(nc, [{f"in_{n}": a for n, a in arrays.items()}], core_ids=[0])
    y = r.results[0]["out_y"]
    return np.ascontiguousarray(y.transpose(1, 0, 2)).reshape(1, 256, D)
```
